# Optimizing a Trainium2 kernel written in Bass

```python
import jax, jax.numpy as jnp
from jax import lax
import numpy as np

D_MODEL = 1024
BATCH = 1
SEQ = 512
DEPTH = 1

SSD_EXPAND = 2
SSD_D_INNER = SSD_EXPAND * D_MODEL
SSD_HEAD_DIM = 64
SSD_N_HEADS = SSD_D_INNER // SSD_HEAD_DIM
SSD_N_GROUPS = 4
SSD_HEADS_PER_GROUP = SSD_N_HEADS // SSD_N_GROUPS
SSD_D_STATE = 128
SSD_CONV_WIDTH = 4
SSD_CHUNK = 128
SSD_CONV_DIM = SSD_D_INNER + 2 * SSD_N_GROUPS * SSD_D_STATE
DT_MIN = 1e-3
DT_MAX = 1e-1

SC_WIDTH = D_MODEL
SC_CONV_WIDTH = 3

N_BRANCHES = 2

D_FF = 2816
FFN_CONV_WIDTH = 3

EPS = 1e-6

IN_SPLIT_SIZES = (SSD_D_INNER, SSD_CONV_DIM, SSD_N_HEADS,
                  SC_WIDTH, SC_WIDTH, SC_WIDTH, N_BRANCHES * D_MODEL)
D_IN_PROJ = sum(IN_SPLIT_SIZES)


def rmsnorm(x, g):
    xf = x.astype(jnp.float32)
    xf = xf * lax.rsqrt(jnp.mean(xf * xf, axis=-1, keepdims=True) + EPS)
    return xf.astype(x.dtype) * g

def grouped_rmsnorm(y, g, n_groups):
    shp = y.shape
    yf = y.astype(jnp.float32).reshape(*shp[:-1], n_groups, shp[-1] // n_groups)
    yf = yf * lax.rsqrt(jnp.mean(yf * yf, axis=-1, keepdims=True) + EPS)
    return yf.reshape(shp) * g

def causal_dwconv(u, w, b=None):
    k_width = w.shape[0]
    seqlen = u.shape[1]
    up = jnp.pad(u, ((0, 0), (k_width - 1, 0), (0, 0)))
    y = up[:, 0:seqlen] * w[0]
    for k in range(1, k_width):
        y = y + up[:, k:k + seqlen] * w[k]
    if b is not None:
        y = y + b
    return y

def ssd_chunked(xh, dt, a, bmat, cmat):
    bsz, seqlen = xh.shape[0], xh.shape[1]
    nc = seqlen // SSD_CHUNK
    L, G, R, P, N = SSD_CHUNK, SSD_N_GROUPS, SSD_HEADS_PER_GROUP, SSD_HEAD_DIM, SSD_D_STATE
    x = (xh * dt[..., None]).reshape(bsz, nc, L, G, R, P)
    adt = jnp.moveaxis((dt * a).reshape(bsz, nc, L, G, R), 2, -1)
    a_cs = jnp.cumsum(adt, axis=-1)
    bc = bmat.reshape(bsz, nc, L, G, N)
    cc = cmat.reshape(bsz, nc, L, G, N)

    causal = jnp.tril(jnp.ones((L, L), dtype=bool))
    decay = jnp.exp(jnp.where(causal, a_cs[..., :, None] - a_cs[..., None, :], -jnp.inf))
    scores = jnp.einsum("bclgn,bcsgn->bcgls", cc, bc)
    m = scores[:, :, :, None] * decay
    y_diag = jnp.einsum("bcgrls,bcsgrp->bclgrp", m, x)

    decay_states = jnp.exp(a_cs[..., -1:] - a_cs)
    states = jnp.einsum("bclgn,bcgrl,bclgrp->bcgrpn", bc, decay_states, x)
    chunk_decay = jnp.exp(a_cs[..., -1])

    def step(h, inp):
        s_c, d_c = inp
        h_new = h * d_c[..., None, None] + s_c
        return h_new, h

    h0 = jnp.zeros((bsz, G, R, P, N), dtype=states.dtype)
    _, prev = lax.scan(step, h0, (jnp.moveaxis(states, 1, 0), jnp.moveaxis(chunk_decay, 1, 0)))
    prev = jnp.moveaxis(prev, 0, 1)

    y_off = jnp.einsum("bclgn,bcgrpn,bcgrl->bclgrp", cc, prev, jnp.exp(a_cs))
    return (y_diag + y_off).reshape(bsz, seqlen, SSD_N_HEADS, P)

def ssd_branch(z, xbc, dt_raw, conv_w, conv_b, dt_bias, a_log, d_skip, norm_g):
    bsz, seqlen = z.shape[0], z.shape[1]
    xbc = jax.nn.silu(causal_dwconv(xbc, conv_w, conv_b))
    gn = SSD_N_GROUPS * SSD_D_STATE
    xs, bm, cm = jnp.split(xbc, [SSD_D_INNER, SSD_D_INNER + gn], axis=-1)
    xh = xs.reshape(bsz, seqlen, SSD_N_HEADS, SSD_HEAD_DIM)
    dt = jax.nn.softplus(dt_raw.astype(jnp.float32) + dt_bias.astype(jnp.float32))
    a = -jnp.exp(a_log.astype(jnp.float32))
    y = ssd_chunked(xh.astype(jnp.float32), dt, a,
                    bm.reshape(bsz, seqlen, SSD_N_GROUPS, SSD_D_STATE).astype(jnp.float32),
                    cm.reshape(bsz, seqlen, SSD_N_GROUPS, SSD_D_STATE).astype(jnp.float32))
    y = y + d_skip.astype(jnp.float32)[:, None] * xh.astype(jnp.float32)
    y = y.reshape(bsz, seqlen, SSD_D_INNER) * jax.nn.silu(z.astype(jnp.float32))
    return grouped_rmsnorm(y, norm_g, SSD_N_GROUPS).astype(z.dtype)

def short_conv_branch(b_gate, c_gate, h, conv_w):
    return b_gate * causal_dwconv(c_gate * h, conv_w)

def hybrid_layer(x, c_act, ada_w, ada_b, mix_pre_g, mix_post_g, w_in,
                 ssd_conv_w, ssd_conv_b, ssd_dt_bias, ssd_a_log, ssd_d, ssd_norm_g,
                 w_ssd_out, sc_conv_w, w_sc_out, w_o,
                 ffn_pre_g, ffn_post_g, w_up, ffn_conv_w, ffn_conv_b, w_down):
    mod = c_act @ ada_w + ada_b
    sh1, sc1, gt1, sh2, sc2, gt2 = [m[:, None, :] for m in jnp.split(mod, 6, axis=-1)]

    h = rmsnorm(x, mix_pre_g) * (1.0 + sc1) + sh1
    proj = h @ w_in
    points, acc = [], 0
    for s in IN_SPLIT_SIZES[:-1]:
        acc += s
        points.append(acc)
    z, xbc, dt_raw, sc_b, sc_c, sc_h, gates = jnp.split(proj, points, axis=-1)
    y_ssd = ssd_branch(z, xbc, dt_raw, ssd_conv_w, ssd_conv_b, ssd_dt_bias,
                       ssd_a_log, ssd_d, ssd_norm_g) @ w_ssd_out
    y_sc = short_conv_branch(sc_b, sc_c, sc_h, sc_conv_w) @ w_sc_out
    g_ssd, g_sc = jnp.split(jax.nn.sigmoid(gates), 2, axis=-1)
    mix = (g_ssd * y_ssd + g_sc * y_sc) @ w_o
    x = x + gt1 * rmsnorm(mix, mix_post_g)

    h = rmsnorm(x, ffn_pre_g) * (1.0 + sc2) + sh2
    u = causal_dwconv(h @ w_up, ffn_conv_w, ffn_conv_b)
    u_gate, u_val = jnp.split(u, 2, axis=-1)
    f = (jax.nn.silu(u_gate) * u_val) @ w_down
    x = x + gt2 * rmsnorm(f, ffn_post_g)
    return x

def first_inputs(seed: int = 0) -> dict:
    key = jax.random.key(seed)
    ks = jax.random.split(key, 32)
    f32 = jnp.float32

    def dense(k, fan_in, fan_out, scale=1.0):
        return jax.random.normal(k, (DEPTH, fan_in, fan_out), f32) * (scale * fan_in ** -0.5)

    def gain(k, n):
        return 1.0 + 0.05 * jax.random.normal(k, (DEPTH, n), f32)

    def small(k, shape, s=0.02):
        return s * jax.random.normal(k, shape, f32)

    u = jax.random.uniform(ks[8], (DEPTH, SSD_N_HEADS), f32)
    dt0 = jnp.exp(u * (np.log(DT_MAX) - np.log(DT_MIN)) + np.log(DT_MIN))
    dt_bias = dt0 + jnp.log(-jnp.expm1(-dt0))
    a_log = jnp.log(jax.random.uniform(ks[9], (DEPTH, SSD_N_HEADS), f32, 1.0, 16.0))

    return {
        "x": jax.random.normal(ks[0], (BATCH, SEQ, D_MODEL), f32),
        "c": jax.random.normal(ks[1], (BATCH, D_MODEL), f32),
        "ada_w": dense(ks[2], D_MODEL, 6 * D_MODEL, 0.5),
        "ada_b": small(ks[3], (DEPTH, 6 * D_MODEL)),
        "mix_pre_g": gain(ks[4], D_MODEL),
        "mix_post_g": gain(ks[5], D_MODEL),
        "w_in": dense(ks[6], D_MODEL, D_IN_PROJ),
        "ssd_conv_w": jax.random.normal(ks[7], (DEPTH, SSD_CONV_WIDTH, SSD_CONV_DIM), f32) * SSD_CONV_WIDTH ** -0.5,
        "ssd_conv_b": small(ks[10], (DEPTH, SSD_CONV_DIM)),
        "ssd_dt_bias": dt_bias,
        "ssd_a_log": a_log,
        "ssd_d": 1.0 + 0.1 * jax.random.normal(ks[11], (DEPTH, SSD_N_HEADS), f32),
        "ssd_norm_g": gain(ks[12], SSD_D_INNER),
        "w_ssd_out": dense(ks[13], SSD_D_INNER, D_MODEL),
        "sc_conv_w": jax.random.normal(ks[14], (DEPTH, SC_CONV_WIDTH, SC_WIDTH), f32) * SC_CONV_WIDTH ** -0.5,
        "w_sc_out": dense(ks[15], SC_WIDTH, D_MODEL),
        "w_o": dense(ks[16], D_MODEL, D_MODEL),
        "ffn_pre_g": gain(ks[17], D_MODEL),
        "ffn_post_g": gain(ks[18], D_MODEL),
        "w_up": dense(ks[19], D_MODEL, 2 * D_FF),
        "ffn_conv_w": jax.random.normal(ks[20], (DEPTH, FFN_CONV_WIDTH, 2 * D_FF), f32) * FFN_CONV_WIDTH ** -0.5,
        "ffn_conv_b": small(ks[21], (DEPTH, 2 * D_FF)),
        "w_down": dense(ks[22], D_FF, D_MODEL),
    }

def first_block(x, c, ada_w, ada_b, mix_pre_g, mix_post_g, w_in,
              ssd_conv_w, ssd_conv_b, ssd_dt_bias, ssd_a_log, ssd_d, ssd_norm_g,
              w_ssd_out, sc_conv_w, w_sc_out, w_o,
              ffn_pre_g, ffn_post_g, w_up, ffn_conv_w, ffn_conv_b, w_down):
    c_act = jax.nn.silu(c)
    for i in range(DEPTH):
        x = hybrid_layer(x, c_act, ada_w[i], ada_b[i], mix_pre_g[i], mix_post_g[i], w_in[i],
                         ssd_conv_w[i], ssd_conv_b[i], ssd_dt_bias[i], ssd_a_log[i], ssd_d[i],
                         ssd_norm_g[i], w_ssd_out[i], sc_conv_w[i], w_sc_out[i], w_o[i],
                         ffn_pre_g[i], ffn_post_g[i], w_up[i], ffn_conv_w[i], ffn_conv_b[i],
                         w_down[i])
    return x


HEAD_DIM = 64
MIX_WIDTH = D_MODEL
FOURIER_WIDTH = MIX_WIDTH // 2
ATTN_WIDTH = MIX_WIDTH - FOURIER_WIDTH
N_FOURIER_GROUPS = FOURIER_WIDTH // HEAD_DIM
N_SLOTS = ATTN_WIDTH // HEAD_DIM
DILATED_CONFIGS = ((128, 1), (512, 4), (2048, 16))
N_CFG = len(DILATED_CONFIGS)
N_ATTN_HEADS = N_SLOTS * N_CFG
QKV_WIDTH = N_ATTN_HEADS * HEAD_DIM
IN_WIDTH = 2 * FOURIER_WIDTH + 3 * QKV_WIDTH + ATTN_WIDTH
SPLIT_POINTS = tuple(int(p) for p in np.cumsum([FOURIER_WIDTH, FOURIER_WIDTH, QKV_WIDTH, QKV_WIDTH, QKV_WIDTH]))
NORM_EPS = 1e-6
MASK_VALUE = -1e30


def alibi_slopes(n):
    return 2.0 ** (-8.0 * jnp.arange(1, n + 1, dtype=jnp.float32) / n)

def rms_norm(t, w):
    t32 = t.astype(jnp.float32)
    return t32 * lax.rsqrt(jnp.mean(t32 * t32, axis=-1, keepdims=True) + NORM_EPS) * w.astype(jnp.float32)

def dilated_window_attention(q, k, v, window, dilation, slopes):
    B, S, H, DH = q.shape
    radius = window // (2 * dilation)
    blk = radius
    L = S // dilation
    N = B * dilation
    nb = -(-L // blk)
    Lp = nb * blk

    def to_sub(t):
        return t.reshape(B, L, dilation, H, DH).transpose(0, 2, 1, 3, 4).reshape(N, L, H, DH)

    qs, ks, vs = to_sub(q), to_sub(k), to_sub(v)
    qb = jnp.pad(qs, ((0, 0), (0, Lp - L), (0, 0), (0, 0))).reshape(N, nb, blk, H, DH)
    pad_kv = ((0, 0), (blk, Lp - L + blk), (0, 0), (0, 0))
    kp = jnp.pad(ks, pad_kv).reshape(N, nb + 2, blk, H, DH)
    vp = jnp.pad(vs, pad_kv).reshape(N, nb + 2, blk, H, DH)
    kb = jnp.concatenate([kp[:, :-2], kp[:, 1:-1], kp[:, 2:]], axis=2)
    vb = jnp.concatenate([vp[:, :-2], vp[:, 1:-1], vp[:, 2:]], axis=2)

    scores = jnp.einsum('nbqhd,nbkhd->nbhqk', qb, kb)
    a = jnp.arange(blk)[:, None]
    c = jnp.arange(3 * blk)[None, :]
    rel = c - blk - a
    key_pos = jnp.arange(nb)[:, None, None] * blk - blk + c[None]
    valid = (jnp.abs(rel)[None] <= radius) & (key_pos >= 0) & (key_pos < L)
    dist = (jnp.abs(rel) * dilation).astype(jnp.float32)
    bias = -slopes[:, None, None] * dist[None]
    scores = jnp.where(valid[None, :, None], scores + bias[None, None], MASK_VALUE)

    m = jnp.max(scores, axis=-1, keepdims=True)
    p = jnp.exp(scores - m)
    s = jnp.sum(p, axis=-1, keepdims=True)
    o = jnp.einsum('nbhqk,nbkhd->nbqhd', p / s, vb)
    lse = (m + jnp.log(s))[..., 0].transpose(0, 1, 3, 2)

    o = o.reshape(N, Lp, H, DH)[:, :L].reshape(B, dilation, L, H, DH).transpose(0, 2, 1, 3, 4).reshape(B, S, H, DH)
    lse = lse.reshape(N, Lp, H)[:, :L].reshape(B, dilation, L, H).transpose(0, 2, 1, 3).reshape(B, S, H)
    return o, lse

def second_inputs(seed: int = 0) -> dict:
    key = jax.random.key(seed)
    ks = jax.random.split(key, 7)
    x = jax.random.normal(ks[0], (BATCH, SEQ, D_MODEL), jnp.float32)
    norm_w = 1.0 + 0.02 * jax.random.normal(ks[1], (D_MODEL,), jnp.float32)
    w_in = jax.random.normal(ks[2], (D_MODEL, IN_WIDTH), jnp.float32) * D_MODEL ** -0.5
    q_norm_w = 1.0 + 0.02 * jax.random.normal(ks[3], (N_ATTN_HEADS, HEAD_DIM), jnp.float32)
    k_norm_w = 1.0 + 0.02 * jax.random.normal(ks[4], (N_ATTN_HEADS, HEAD_DIM), jnp.float32)
    w_fourier = jax.random.normal(ks[5], (N_FOURIER_GROUPS, HEAD_DIM, HEAD_DIM), jnp.float32) * HEAD_DIM ** -0.5
    w_out = jax.random.normal(ks[6], (MIX_WIDTH, D_MODEL), jnp.float32) * MIX_WIDTH ** -0.5
    return {"x": x, "norm_w": norm_w, "w_in": w_in, "q_norm_w": q_norm_w,
            "k_norm_w": k_norm_w, "w_fourier": w_fourier, "w_out": w_out}

def second_block(x, norm_w, w_in, q_norm_w, k_norm_w, w_fourier, w_out):
    B, S, _ = x.shape
    slopes = alibi_slopes(N_SLOTS)
    h = x.astype(jnp.float32)
    for _layer in range(DEPTH):
        hn = rms_norm(h, norm_w)
        proj = hn @ w_in.astype(jnp.float32)
        u_f, g_f, q, k, v, g_a = jnp.split(proj, SPLIT_POINTS, axis=-1)

        u_f = u_f.reshape(B, S, N_FOURIER_GROUPS, HEAD_DIM)
        f = jnp.fft.fft2(u_f, axes=(1, 3), norm="ortho").real.astype(jnp.float32)
        f = jnp.einsum('bsgc,gcd->bsgd', f, w_fourier.astype(jnp.float32)).reshape(B, S, FOURIER_WIDTH)
        y_f = f * jax.nn.silu(g_f)

        q = rms_norm(q.reshape(B, S, N_ATTN_HEADS, HEAD_DIM), q_norm_w) * HEAD_DIM ** -0.5
        k = rms_norm(k.reshape(B, S, N_ATTN_HEADS, HEAD_DIM), k_norm_w)
        v = v.reshape(B, S, N_ATTN_HEADS, HEAD_DIM)
        outs, lses = [], []
        for c, (window, dilation) in enumerate(DILATED_CONFIGS):
            sl = slice(c * N_SLOTS, (c + 1) * N_SLOTS)
            o_c, lse_c = dilated_window_attention(q[:, :, sl], k[:, :, sl], v[:, :, sl], window, dilation, slopes)
            outs.append(o_c)
            lses.append(lse_c)
        alpha = jax.nn.softmax(jnp.stack(lses, axis=0), axis=0)
        o = jnp.sum(alpha[..., None] * jnp.stack(outs, axis=0), axis=0).reshape(B, S, ATTN_WIDTH)
        y_a = o * jax.nn.silu(g_a)

        mixed = jnp.concatenate([y_f, y_a], axis=-1) @ w_out.astype(jnp.float32)
        h = h + mixed
    return h.astype(x.dtype)


def setup_inputs(seed=0):
    out = dict(first_inputs(seed))
    for name, value in second_inputs(seed + 1).items():
        if name != "x":
            out[name + "_2"] = value
    return out


def reference(
    x, c, ada_w, ada_b, mix_pre_g, mix_post_g, w_in, ssd_conv_w, ssd_conv_b, ssd_dt_bias,
    ssd_a_log, ssd_d, ssd_norm_g, w_ssd_out, sc_conv_w, w_sc_out, w_o, ffn_pre_g, ffn_post_g,
    w_up, ffn_conv_w, ffn_conv_b, w_down, norm_w_2, w_in_2, q_norm_w_2, k_norm_w_2, w_fourier_2,
    w_out_2,
):
    x = first_block(
        x, c, ada_w, ada_b, mix_pre_g, mix_post_g, w_in, ssd_conv_w, ssd_conv_b, ssd_dt_bias,
        ssd_a_log, ssd_d, ssd_norm_g, w_ssd_out, sc_conv_w, w_sc_out, w_o, ffn_pre_g,
        ffn_post_g, w_up, ffn_conv_w, ffn_conv_b, w_down,
    )
    return second_block(
        x, norm_w_2, w_in_2, q_norm_w_2, k_norm_w_2, w_fourier_2, w_out_2,
    )


_drawn_inputs = setup_inputs


def setup_inputs(seed=0):
    import zlib

    import numpy as np

    out = dict(_drawn_inputs(seed))
    spreads = {}
    factors = {'mix_post_g': 3.247,
     'ssd_conv_b': 8.0,
     'ssd_d': 4.335,
     'ssd_norm_g': 5.893,
     'ffn_pre_g': 2.853,
     'ffn_post_g': 3.795,
     'ffn_conv_b': 6.899,
     'norm_w_2': 6.819,
     'q_norm_w_2': 8.0,
     'k_norm_w_2': 8.0}
    for name, (base, spread) in spreads.items():
        noise = np.random.default_rng([zlib.crc32(name.encode()), seed]).standard_normal(out[name].shape)
        drawn = base * np.exp(spread * noise) if base else spread * noise
        out[name] = __import__('jax').numpy.asarray(drawn.astype(out[name].dtype))
    for name, factor in factors.items():
        out[name] = (out[name] * factor).astype(out[name].dtype)
    return out
```

```python
from contextlib import ExitStack

import numpy as np

import concourse.bass as bass
from concourse import mybir

ALU = mybir.AluOpType
ACT = mybir.ActivationFunctionType
AX = mybir.AxisListType
F32 = mybir.dt.float32
F32R = mybir.dt.float32r

P = 128
S = 512
NT = S // P
D = 1024
DB = D // P
KT = 8
UW = KT * P
EPS = 1e-6

SSD_HEADS, HEADS_G, GROUPS, HP, NSTATE = 32, 8, 4, 64, 128
FF_PAIRS = 2816 // P
CFG = 3
MASKED = -1e33

U_GRP = 1
N_GRP = 20
U_MIX = U_GRP + GROUPS * N_GRP
U_WO = U_MIX + 3 * DB
U_UP = U_WO + DB
U_DOWN = U_UP + 2 * FF_PAIRS
N_DOWN = 3
U_ATT = U_DOWN + N_DOWN * DB
N_ATT = 12
U_OUT = U_ATT + 4 * N_ATT
U_LAST = U_OUT + DB
UNITS = U_LAST + 1

R_GRP = 1
R_MIX = R_GRP + GROUPS * 24
R_WO = R_MIX + 3 * DB
R_UP = R_WO + DB
R_DOWN = R_UP + 2 * FF_PAIRS
R_ATT = R_DOWN + DB

E_GRP = 1
E_MIX = E_GRP + GROUPS * 16
E_WO = E_MIX + 3 * DB
E_UP = E_WO + DB
E_DOWN = E_UP + 2 * FF_PAIRS
E_ATT = E_DOWN + DB
E_OUT = E_ATT + 4 * N_ATT

OUT_TILES = (0, 1, 2, 4, 5, 6, 3)

_widths = [("ident", P), ("causal", P), ("head_ones", P), ("c", DB), ("ada_b", 48), ("g_pre", DB),
           ("g_post", DB), ("f_pre", DB), ("f_post", DB), ("nw2", DB), ("conv", 24 * 5), ("d_skip", 16),
           ("ssd_g", 16), ("sc_w", DB * 3), ("ffn_w", 2 * FF_PAIRS * 4), ("qk_w", 24), ("dt_bias", 1),
           ("a_log", 1)]
COL = {}
_at = 0
for _n, _w in _widths:
    COL[_n] = _at
    _at += _w
NCOL = _at


def build(nc, arrays):
    with ExitStack() as ctx:
        KB = 1024
        names = set()

        def at(name, offset, shape, dt=F32):
            assert name not in names
            names.add(name)
            n = 4
            for s in shape[1:]:
                n *= s
            assert BASE + offset + n <= 229344, (name, offset, n)
            return nc.alloc_sbuf_tensor_at(name, shape, dt, offset=BASE + offset)

        def area(offset, end):
            pos = [offset]

            def place(name, shape, dt=F32):
                t = at(name, pos[0], shape, dt)
                n = 4
                for s in shape[1:]:
                    n *= s
                pos[0] += (n + 31) // 32 * 32
                assert pos[0] <= end, (name, pos[0], end)
                return t
            place.end = lambda: pos[0]
            return place

        def sem(name):
            return ctx.enter_context(nc.semaphore(name))

        BASE = 16512
        END = 229344 - BASE
        keep = area(0, 70 * KB)
        tab = keep("tab", [P, NCOL])
        ones = keep("ones", [P, P])
        eps = keep("eps", [P, 2])
        mod = keep("mod", [P, 48])
        coef = keep("coef", [P, 4, DB])
        small = keep("small", [P, 32])
        raw = keep("raw", [P, 4, UW])
        w_hi = keep("w_hi", [P, 2, UW], F32R)
        w_lo = keep("w_lo", [P, 2, UW], F32R)
        H_AT = keep.end()
        h_hi = keep("h_hi", [P, DB, S], F32R)
        h_lo = keep("h_lo", [P, DB, S], F32R)
        FREE = keep.end()

        g = area(FREE, END)
        ssd_acc = g("ssd_acc", [P, DB, S])
        ysc = g("ysc", [P, DB, S])
        ada_raw = g("ada_raw", [P, 2, S])
        ada_acc = g("ada_acc", [P, D])
        ev = g("ev", [P, 4, S + 4])
        cv = g("cv", [P, 2, S])
        scp = g("scp", [P, S + 4])
        sct = g("sct", [P, S])
        BT = g("BT", [P, S])
        CT = g("CT", [P, S])
        dtN = g("dtN", [P, NT, SSD_HEADS])
        acsN = g("acsN", [P, NT, SSD_HEADS])
        g_end = g.end()
        g = area(g_end, END)
        xcT = g("xcT", [P, 4, S])
        yg = g("yg", [P, 4, S])
        zs = g("zs", [P, 4, S])
        abc = g("abc", [P, 2, HEADS_G, P])
        dec = g("dec", [P, 2, HEADS_G, P])
        ect = g("ect", [P, 2, HEADS_G, P])
        eld = g("eld", [P, NT, HEADS_G])
        xdt = g("xdt", [P, 2, S])
        xst = g("xst", [P, 2, S])
        scm = g("scm", [P, 2, P])
        bn = g("bn", [P, 2, P])
        hst = g("hst", [P, 2, S])
        y_at = g.end()
        g = area(y_at, END)
        y_hi = g("y_hi", [P, 4, S], F32R)
        y_lo = g("y_lo", [P, 4, S], F32R)
        dtw = at("dtw", y_at, [SSD_HEADS, 8, S])
        g = area(g_end, END)
        x_tok = g("x_tok", [P, NT, D])
        ada0 = g("ada0", [P, 8, D])
        acc0 = g("acc0", [P, 2, D])
        hf = g("hf", [P, 2, S])
        junk = at("junk", FREE, [P, D])

        g = area(FREE + 32 * KB, END)
        mix_hi = g("mix_hi", [P, DB, S], F32R)
        mix_lo = g("mix_lo", [P, DB, S], F32R)
        sc_hi = g("sc_hi", [P, DB, S], F32R)
        sc_lo = g("sc_lo", [P, DB, S], F32R)
        gts = g("gts", [P, 2, 3, S])
        mixf = g("mixf", [P, 2, S])
        x_tok2 = g("x_tok2", [P, NT, D])
        xT = at("xT", FREE, [P, DB, S])
        mo = at("mo", FREE + 16 * KB, [P, DB, S])
        g = area(FREE + 64 * KB, END)
        sq = g("sq", [P, 2, S])
        ssum = g("ssum", [P, S])
        rn = g("rn", [P, S])
        hp = g("hp", [P, 2, S])

        g = area(FREE + 16 * KB, END)
        fe = g("fe", [P, 4, S + 4])
        fcv = g("fcv", [P, 4, S])
        af = g("af", [P, 2, S])
        act_hi = g("act_hi", [P, FF_PAIRS, S], F32R)
        act_lo = g("act_lo", [P, FF_PAIRS, S], F32R)
        fo = at("fo", FREE + 16 * KB, [P, DB, S])
        g = area(FREE + 126 * KB, END)
        sq6 = g("sq6", [P, 2, S])
        ssum6 = g("ssum6", [P, S])
        rn6 = g("rn6", [P, S])
        hp6 = g("hp6", [P, 2, S])
        xN = at("xN", FREE + 110 * KB, [P, NT, D])

        g = area(FREE, END)
        yo_hi = g("yo_hi", [P, DB, S], F32R)
        yo_lo = g("yo_lo", [P, DB, S], F32R)
        dft = g("dft", [P, 2, NT, S])
        bias = g("bias", [P, NT, 6 * P])
        wf = g("wf", [P, 4, 2 * P])
        qk = g("qk", [P, 2 * CFG, S])
        wfb = at("wfb", g.end(), [P, 4, P])
        dhd = at("dhd", g.end() + 2 * KB, [P, 2, P])
        vN = g("vN", [P, CFG, NT, P])
        sga = g("sga", [P, S])
        qk_next = g("qk_next", [P, 2 * CFG, S])
        vN_next = g("vN_next", [P, CFG, NT, P])
        sga_next = g("sga_next", [P, S])
        qsq = g("qsq", [P, S])
        qrt = g("qrt", [P, 3, S])
        vT = g("vT", [P, S])
        ufT = g("ufT", [P, S])
        sgf = g("sgf", [P, S])
        fv = g("fv", [P, NT, 2 * P])
        pr = g("pr", [P, 6 * P])
        yf = g("yf", [P, S])
        ya = g("ya", [P, S])
        stat = g("stat", [P, 4])
        pt = g("pt", [P, 6 * P])
        x_res = at("x_res", H_AT, [P, NT, D])

        ps = ctx.enter_context(nc.psum_tensor("ps", [P, 8, S], F32))
        acs_dram = nc.dram_tensor("acs_dram", (SSD_HEADS, S), F32, kind="Internal").ap()
        x2_dram = nc.dram_tensor("x2_dram", (P, NT, D), F32, kind="Internal").ap()

        raw_landed = [sem(f"raw_landed{i}") for i in range(4)]
        split_hi = sem("split_hi")
        split_done = sem("split_done")
        units_done = sem("units_done")
        half_done = sem("half_done")
        evacuated = sem("evacuated")
        tab_in = sem("tab_in")
        x_in = sem("x_in")
        ada0_in = [sem(f"ada0_in{i}") for i in range(8)]
        setup = sem("setup")
        cact_ready = sem("cact_ready")
        row_stats = sem("row_stats")
        row_scaled = sem("row_scaled")
        ada0_steps = sem("ada0_steps")
        mod0_sums = sem("mod0_sums")
        mod0_ready = sem("mod0_ready")
        x_turned = sem("x_turned")
        h_full = sem("h_full")
        h_hi_ready = sem("h_hi_ready")
        h_lo_ready = sem("h_lo_ready")
        dt_act = sem("dt_act")
        dt_steps = sem("dt_steps")
        acs_stored = sem("acs_stored")
        dt_turned = sem("dt_turned")
        dt_tokens = sem("dt_tokens")
        ada_in = [sem(f"ada_in{i}") for i in range(2)]
        ada_steps = sem("ada_steps")
        mod_sums = sem("mod_sums")
        mod_ready = sem("mod_ready")
        conv_taps = sem("conv_taps")
        conv_out = sem("conv_out")
        skip_ready = sem("skip_ready")
        abc_in = [sem(f"abc_in{i}") for i in range(2)]
        dec_args = sem("dec_args")
        decays = sem("decays")
        chunk_inputs = sem("chunk_inputs")
        chunk_steps = sem("chunk_steps")
        s_done = sem("s_done")
        y_done = sem("y_done")
        state_steps = sem("state_steps")
        gate_steps = sem("gate_steps")
        y_squared = sem("y_squared")
        group_sum = sem("group_sum")
        group_root = sem("group_root")
        y_hi_ready = sem("y_hi_ready")
        sc_steps = sem("sc_steps")
        acc_steps = sem("acc_steps")
        coef_ready = sem("coef_ready")
        sc_hi_ready = sem("sc_hi_ready")
        sc_lo_ready = sem("sc_lo_ready")
        mix_steps = sem("mix_steps")
        mix_hi_ready = sem("mix_hi_ready")
        x2_in = sem("x2_in")
        xt_turned = sem("xt_turned")
        xt_ready = sem("xt_ready")

        def norm_sems(k):
            return {n: sem(f"n{k}_{n}") for n in ("squared", "summed", "total", "root", "steps", "hi", "turned", "out")}
        n1a, n1b, n2a, n2b = norms = tuple(norm_sems(k) for k in ("1a", "1b", "2a", "2b"))
        ffn_taps = sem("ffn_taps")
        ffn_silu = sem("ffn_silu")
        ffn_steps = sem("ffn_steps")
        act_hi_ready = sem("act_hi_ready")
        x2_stored = sem("x2_stored")
        att_in = sem("att_in")
        wf_sums = sem("wf_sums")
        wf_ready = sem("wf_ready")
        bias_scaled = sem("bias_scaled")
        fv_done = sem("fv_done")
        fv_ready = sem("fv_ready")
        ft_done = sem("ft_done")
        yf_steps = sem("yf_steps")
        yf_hi_ready = sem("yf_hi_ready")
        ya_steps = sem("ya_steps")
        ya_hi_ready = sem("ya_hi_ready")
        qk_total = sem("qk_total")
        qk_root = sem("qk_root")
        qk_steps = sem("qk_steps")
        qk_moved = sem("qk_moved")
        v_turned = sem("v_turned")
        v_ready = sem("v_ready")
        v_moved = sem("v_moved")
        gate_moved = sem("gate_moved")
        scored = sem("scored")
        biased = sem("biased")
        exped = sem("exped")
        normed = sem("normed")
        p_turned = sem("p_turned")
        pt_ready = sem("pt_ready")
        attended = sem("attended")
        x_res_in = [sem(f"x_res_in{i}") for i in range(2)]
        out_turned = sem("out_turned")
        out_added = sem("out_added")
        out_sums = sem("out_sums")
        out_steps = sem("out_steps")
        out_stored = sem("out_stored")

        start_at_one = [acc_steps, group_root, chunk_steps, state_steps, mod_ready, gate_steps, biased, pt_ready, decays, sc_steps, y_done, mix_steps, attended, ada_steps, units_done, mod_sums, p_turned, ya_steps] + [n["summed"] for n in norms]

        ident = tab[:, COL["ident"]:COL["ident"] + P]
        causal = tab[:, COL["causal"]:COL["causal"] + P]
        head_ones = tab[:, COL["head_ones"]:COL["head_ones"] + P]

        def col(name, i, n=1):
            return tab[:, bass.ds(COL[name] + i, n)]

        def blocks(t, i):
            return t[:, bass.ds(i, 1), :].rearrange("p o s -> p (o s)")

        def per_token(t, chunk, g):
            return t[:, chunk, bass.ds(HEADS_G * g, HEADS_G)].unsqueeze(2).broadcast_to([P, HEADS_G, HP])

        def by_head(t):
            return t.rearrange("p (h c) -> p h c", h=HEADS_G)

        def permuted(t):
            return t.rearrange("p (r i) -> p i r", r=NT)

        def natural(t):
            return t.rearrange("p (i r) -> p i r", r=NT)

        block = ctx.enter_context(nc.Block())

        @block.sync
        def _(sp):
            for signal in start_at_one:
                sp.sem_inc(signal, 1)
            sp.sem_inc(bias_scaled, NT)
            sp.dma_start(tab[:], arrays["table"]).then_inc(tab_in, 16)
            sp.dma_start(x_tok[:], arrays["x"]).then_inc(x_in, 16)
            for k in range(8):
                sp.dma_start(ada0[:, k], arrays["ada"][k]).then_inc(ada0_in[k], 16)
            for u in range(4):
                sp.dma_start(raw[:, u], arrays["stream"][u]).then_inc(raw_landed[u], 16)
            for k in range(8):
                sp.wait_ge(ada0_steps, k + 1)
                sp.dma_start(ada0[:, k], arrays["ada"][8 + k]).then_inc(ada0_in[k], 16)

            def stream(u, slot):
                sp.wait_ge(split_done, u - 3)
                src = arrays["stream"][bass.ds(u, 1)].rearrange("u p w -> (u p) w")
                sp.dma_start(raw[:, slot], src).then_inc(raw_landed[slot], 16)

            ADA_BEHIND = (0, 1, 2, 3, 4, 5, 9, 11)
            with sp.Fori(0, GROUPS) as g:
                for s in range(N_GRP):
                    stream(4 + N_GRP * g + s, s % 4)
                    if s in ADA_BEHIND:
                        k = ADA_BEHIND.index(s)
                        for hv in range(2):
                            sp.wait_ge(ada_steps, 1 + 16 * g + max(2 * k + hv - 1, 0))
                            src = arrays["ada"][bass.ds(16 + 8 * g + k, 1)].rearrange("m p w -> (m p) w")
                            sp.dma_start(ada_raw[:, hv], src[:, hv * S:(hv + 1) * S]).then_inc(ada_in[hv], 16)
            done = 4 + GROUPS * N_GRP
            loops = (UNITS - done) // 4
            with sp.Fori(0, loops) as i:
                for s in range(4):
                    stream(done + 4 * i + s, s)
            for u in range(done + 4 * loops, UNITS):
                stream(u, u % 4)

        @block.gpsimd
        def _(pool):
            def split(u, raw_slot, slot, landed):
                pool.wait_ge(raw_landed[raw_slot], landed)
                nc.gpsimd.tensor_tensor(w_hi[:, slot], raw[:, raw_slot],
                                        ones[:, 0:1].broadcast_to([P, UW]), ALU.mult).then_inc(split_hi, 1)
                pool.wait_ge(split_hi, u + 1)
                nc.gpsimd.tensor_tensor(w_lo[:, slot], raw[:, raw_slot], w_hi[:, slot].bitcast(F32),
                                        ALU.subtract).then_inc(split_done, 1)

            pool.wait_ge(setup, 1)
            split(0, 0, 0, 16)
            with pool.Fori(0, (UNITS - 1) // 4) as i:
                for s in range(4):
                    u = 1 + 4 * i + s
                    pool.wait_ge(units_done, 1 + 4 * i + s)
                    split(u, (1 + s) % 4, (1 + s) % 2, 16 * i + (16 if s < 3 else 32))
            for u in range(1 + (UNITS - 1) // 4 * 4, UNITS):
                pool.wait_ge(units_done, 1 + u - 1)
                split(u, u % 4, u % 2, 16 * (u // 4 + 1))

        @block.tensor
        def _(pe):
            def unit(u, slot, bank, free=None, x_hi=h_hi, x_lo=h_lo, k0=0, tiles=KT, at_k=0, start=True,
                     stop=True, last=True, signal=None):
                if at_k == 0:
                    pe.wait_ge(split_done, u + 1)
                if free is not None:
                    pe.wait_ge(*free)
                for k in range(tiles):
                    w = slice((at_k + k) * P, (at_k + k + 1) * P)
                    nc.tensor.matmul(ps[:, bank], w_hi[:, slot, w], x_hi[:, k0 + k],
                                     start=start and k == 0, stop=False)
                    nc.tensor.matmul(ps[:, bank], w_hi[:, slot, w], x_lo[:, k0 + k], start=False, stop=False)
                    mm = nc.tensor.matmul(ps[:, bank], w_lo[:, slot, w], x_hi[:, k0 + k],
                                          start=False, stop=stop and k == tiles - 1)
                if signal is not None:
                    mm.then_inc(signal, 1)
                elif last:
                    mm.then_inc(units_done, 1)

            def tiles(u, slot, bank, x_hi, x_lo, at_, of, ready=False, free=None, start=False, signal=None):
                if ready:
                    pe.wait_ge(split_done, u + 1)
                    pe.wait_ge(*free)
                for m, (t, k) in enumerate(zip(at_, of)):
                    w = slice(t * P, (t + 1) * P)
                    nc.tensor.matmul(ps[:, bank], w_hi[:, slot, w], x_hi[:, k], start=start and m == 0, stop=False)
                    nc.tensor.matmul(ps[:, bank], w_hi[:, slot, w], x_lo[:, k], start=False, stop=False)
                    mm = nc.tensor.matmul(ps[:, bank], w_lo[:, slot, w], x_hi[:, k], start=False,
                                          stop=signal is not None and m == len(of) - 1)
                if signal is not None:
                    mm.then_inc(signal, 1)

            pe.wait_ge(tab_in, 16)
            pe.wait_ge(row_scaled, 4)
            for b in range(DB):
                if b >= 4:
                    pe.wait_ge(h_full, b - 3)
                for t in range(NT):
                    mm = nc.tensor.transpose(ps[:, 4 + b % 4, t * P:(t + 1) * P], x_tok[:, t, b * P:(b + 1) * P],
                                             ident)
                mm.then_inc(x_turned, 1)
                if b == 3:
                    pe.wait_ge(setup, 1)
                    pe.wait_ge(ada0_steps, 16)
                    for m in range(16):
                        mm = nc.tensor.matmul(ps[:, 2, m:m + 1], acc0[:, m // 8, (m % 8) * P:(m % 8 + 1) * P],
                                              ones[:, 0:1], start=True, stop=True)
                    mm.then_inc(mod0_sums, 1)

            pe.wait_ge(h_lo_ready, DB)
            unit(0, 0, 0)
            pe.wait_ge(dt_steps, 13)
            for c in range(NT):
                nc.tensor.transpose(ps[:, 5, c * 64:c * 64 + 32], dtw[:, 7, c * P:(c + 1) * P],
                                    ident[0:SSD_HEADS, 0:SSD_HEADS])
            pe.wait_ge(dt_steps, 18)
            for c in range(NT):
                mm = nc.tensor.transpose(ps[:, 5, c * 64 + 32:c * 64 + 64], dtw[:, 0, c * P:(c + 1) * P],
                                         ident[0:SSD_HEADS, 0:SSD_HEADS])
            mm.then_inc(dt_turned, 1)

            with pe.Fori(0, GROUPS) as g:
                def u_(j):
                    return U_GRP + N_GRP * g + j

                def project(j):
                    if j < 2:
                        free = (acc_steps, 1 + 8 * g)
                    else:
                        free = (evacuated, E_GRP + 16 * g + j - 1)
                    unit(u_(j), (1 + j) % 2, (R_GRP + j) % 2, free)

                def turn(c):
                    pe.wait_ge(chunk_steps, 1 + 24 * g + (6 * (c - 1) + 3 if c else 0))
                    if c == 0:
                        pe.wait_ge(dt_tokens, 2)
                        pe.wait_ge(group_root, 1 + g)
                    cols = slice(c * P, (c + 1) * P)
                    pe.wait_ge(conv_out, 6 * g + 6)
                    nc.tensor.matmul(ps[:, 5, 0:P], BT[:, cols], CT[:, cols], start=True, stop=True)
                    nc.tensor.transpose(ps[:, 5, P:2 * P], BT[:, cols], ident)
                    for b in range(4):
                        mm = nc.tensor.transpose(ps[:, 4, b * P:(b + 1) * P], xcT[:, b, cols], ident)
                    mm.then_inc(chunk_inputs, 1)

                def state(c):
                    pe.wait_ge(chunk_steps, 1 + 24 * g + 6 * c + 6)
                    pe.wait_ge(state_steps, 1 + 5 * g + (0, 1, 3)[c])
                    if c == 0:
                        pe.wait_ge(mod_ready, 1 + g)
                    nc.tensor.matmul(ps[:, 7], bn[:, c % 2], xst[:, c % 2], start=True, stop=True).then_inc(s_done, 1)

                def outputs(c):
                    pe.wait_ge(chunk_steps, 1 + 24 * g + 6 * c + 6)
                    pe.wait_ge(gate_steps, 1 + 15 * g + max(c - 1, 0))
                    if c:
                        pe.wait_ge(state_steps, 1 + 5 * g + (1, 3, 5)[c - 1])
                    for h in range(HEADS_G):
                        rows, hc = slice(64 * (h % 2), 64 * (h % 2) + 64), slice(h * HP, (h + 1) * HP)
                        out = ps[rows, 6 - 4 * (c % 2), (h // 2) * P:(h // 2 + 1) * P]
                        mm = nc.tensor.matmul(out, xdt[:, c % 2, hc], dec[:, c % 2, h], start=(h < 2),
                                              stop=(c == 0), skip_group_check=True)
                        if c:
                            mm = nc.tensor.matmul(out, hst[:, c % 2, hc], ect[:, c % 2, h], start=False,
                                                  stop=True, skip_group_check=True)
                    mm.then_inc(y_done, 1)

                for j in range(6):
                    project(j)
                project(6)
                turn(0)
                project(7)
                turn(1)
                project(8)
                state(0)
                outputs(0)
                turn(2)
                project(9)
                state(1)
                outputs(1)
                turn(3)
                project(10)
                state(2)
                outputs(2)
                project(11)
                outputs(3)
                project(12)
                pe.wait_ge(ada_steps, 1 + 16 * g + 16)
                pe.wait_ge(state_steps, 1 + 5 * g + 5)
                for b in range(DB):
                    mm = nc.tensor.matmul(ps[:, 7, b:b + 1], ada_acc[:, b * P:(b + 1) * P], ones[:, 0:1],
                                          start=True, stop=True)
                mm.then_inc(mod_sums, 1)
                project(13)
                pe.wait_ge(gate_steps, 1 + 15 * g + 6)
                nc.tensor.matmul(ps[:, 4], ones[:], sct[:], start=True, stop=True).then_inc(group_sum, 1)
                project(14)
                project(15)
                pe.wait_ge(gate_steps, 1 + 15 * g + 15)
                for n in range(DB):
                    if n < 2:
                        free = (evacuated, E_GRP + 16 * g + 15 + n)
                    else:
                        free = (acc_steps, 1 + 8 * g + n - 1)
                    unit(u_(16 + n // 2), (1 + n // 2) % 2, (R_GRP + 16 + n) % 2, free, y_hi, y_lo,
                         tiles=4, at_k=4 * (n % 2), signal=half_done if n % 2 == 0 else units_done)

            pe.wait_ge(acc_steps, 1 + 8 * GROUPS)
            with pe.Fori(0, 2) as i:
                for j in range(12):
                    if j == 2:
                        pe.wait_ge(sc_lo_ready, 2)
                    sc = j % 3 == 2
                    unit(U_MIX + 12 * i + j, (U_MIX + j) % 2, (R_MIX + j) % 2, (evacuated, E_MIX + 12 * i + j - 1),
                         sc_hi if sc else h_hi, sc_lo if sc else h_lo)

            pe.wait_ge(x2_in, 16)
            for b in range(DB):
                if b >= 2:
                    pe.wait_ge(xt_ready, b - 1)
                for t in range(NT):
                    mm = nc.tensor.transpose(ps[:, 4 + b % 2, t * P:(t + 1) * P], x_tok2[:, t, b * P:(b + 1) * P],
                                             ident)
                mm.then_inc(xt_turned, 1)

            pe.wait_ge(mix_steps, 1 + 32)
            with pe.Fori(0, DB // 2) as i:
                for j in range(2):
                    unit(U_WO + 2 * i + j, (U_WO + j) % 2, (R_WO + j) % 2, (evacuated, E_WO + 2 * i + j - 1),
                         mix_hi, mix_lo)

            def norm_total(n, src):
                pe.wait_ge(n["summed"], 1 + DB)
                nc.tensor.matmul(ps[:, 4], ones[:], src[:], start=True, stop=True).then_inc(n["total"], 1)

            norm_total(n1a, ssum)
            norm_total(n1b, ssum)
            pe.wait_ge(n1b["steps"], 1 + 2 * DB)
            with pe.Fori(0, FF_PAIRS // 2) as i:
                for j in range(4):
                    unit(U_UP + 4 * i + j, (U_UP + j) % 2, (R_UP + j) % 2, (evacuated, E_UP + 4 * i + j - 1))
            pe.wait_ge(ffn_steps, 4 + 2 * FF_PAIRS)
            with pe.Fori(0, 2) as i:
                for n in range(4):
                    bank = (R_DOWN + n) % 2
                    u = U_DOWN + 12 * i + 3 * n
                    for j in range(N_DOWN):
                        unit(u + j, (U_DOWN + 3 * n + j) % 2, bank,
                             (evacuated, E_DOWN + 4 * i + n - 1) if j == 0 else None, act_hi, act_lo, k0=8 * j,
                             tiles=(8, 8, 6)[j], start=(j == 0), stop=(j == 2))
            norm_total(n2a, ssum6)
            norm_total(n2b, ssum6)
            for b in range(DB):
                if b >= 2:
                    pe.wait_ge(n2b["out"], b - 1)
                elif b == 0:
                    pe.wait_ge(n2b["squared"], DB)
                for r in range(NT):
                    mm = nc.tensor.transpose(ps[:, 6 + b % 2, r * P:(r + 1) * P],
                                             xT[:, b].rearrange("p (i r) -> p i r", r=NT)[:, :, r], ident)
                mm.then_inc(n2b["turned"], 1)
            pe.wait_ge(att_in, 16 * 4)
            for b in range(4):
                for m in range(2):
                    mm = nc.tensor.matmul(ps[:, 2 + b // 2, (b % 2) * 256 + m * P:(b % 2) * 256 + (m + 1) * P],
                                          dhd[:, m], wfb[:, b], start=True, stop=True)
            mm.then_inc(wf_sums, 1)
            pe.wait_ge(n2b["steps"], 1 + 2 * DB)
            pe.wait_ge(wf_ready, 2)

            def half(p, x):
                j = x // 2
                u = U_ATT + N_ATT * p + j
                if x % 2 == 0:
                    tiles(u, (U_ATT + j) % 2, (R_ATT + j) % 2, h_hi, h_lo, range(0, 4), range(0, 4),
                          ready=True, free=(evacuated, E_ATT + N_ATT * p + j - 1), start=True)
                    return
                tiles(u, (U_ATT + j) % 2, (R_ATT + j) % 2, h_hi, h_lo, range(4, 8), range(4, 8), signal=units_done)
                if 1 <= j <= 6:
                    m = j - 1
                    pe.wait_ge(evacuated, E_ATT + N_ATT * p + m + 1)
                    if m:
                        pe.wait_ge(qk_root, 6 * p + m)
                    elif not (isinstance(p, int) and p == 0):
                        pe.wait_ge(yf_steps, 2 * p - 1)
                    nc.tensor.matmul(ps[:, 7], head_ones, qsq[:], start=True, stop=True).then_inc(qk_total, 1)
                if 7 <= j <= 9:
                    c = j - 7
                    pe.wait_ge(evacuated, E_ATT + N_ATT * p + 6 + c + 1)
                    if c:
                        pe.wait_ge(v_ready, 3 * p + c)
                    else:
                        pe.wait_ge(qk_root, 6 * p + 6)
                    for t in range(NT):
                        mm = nc.tensor.transpose(ps[:, 7, t * P:(t + 1) * P], vT[:, t * P:(t + 1) * P], ident)
                    mm.then_inc(v_turned, 1)
                if j >= 10:
                    m = j - 10
                    if m:
                        pe.wait_ge(fv_ready, 2 * p + 1)
                    else:
                        pe.wait_ge(v_ready, 3 * p + 3)
                        pe.wait_ge(evacuated, E_ATT + N_ATT * p + 10)
                    for t in range(2 * m, 2 * m + 2):
                        mm = nc.tensor.matmul(ps[:, 7, (t % 2) * 256:(t % 2) * 256 + 256], ufT[:, t * P:(t + 1) * P],
                                              blocks(wf, p), start=True, stop=True)
                    mm.then_inc(fv_done, 1)

            def token_transform(a):
                pe.wait_ge(fv_ready, 2 * a + 2)
                for t in range(NT):
                    nc.tensor.matmul(ps[:, 7], fv[:, t, 0:P], dft[:, 0, t], start=(t == 0), stop=False)
                    mm = nc.tensor.matmul(ps[:, 7], fv[:, t, P:2 * P], dft[:, 1, t], start=False,
                                          stop=(t == NT - 1))
                mm.then_inc(ft_done, 1)

            def scores(a, n):
                rows, r = slice(64 * (n // 4), 64 * (n // 4) + 64), n % 4
                q = slice(r * P, (r + 1) * P)
                if n == 0:
                    pe.wait_ge(qk_moved, a + 1)
                pe.wait_ge(biased, 1 + 8 * a + n)
                nc.tensor.matmul(ps[:, 2], qk[rows, 0, q], qk[rows, CFG], start=True, stop=True)
                nc.tensor.matmul(ps[:, 3, 0:P], qk[rows, 1, q], qk[rows, CFG + 1, q], start=True, stop=True)
                nc.tensor.matmul(ps[:, 3, P:2 * P], qk[rows, 2, q], qk[rows, CFG + 2, q], start=True,
                                 stop=True).then_inc(scored, 1)

            def turn_p(a, n):
                pe.wait_ge(normed, 16 * a + 2 * n + 2)
                pe.wait_ge(pt_ready, 1 + 8 * a + n)
                for m in range(6):
                    mm = nc.tensor.transpose(ps[:, 4 + m // 4, (m % 4) * P:(m % 4 + 1) * P],
                                             pr[:, m * P:(m + 1) * P], ident)
                mm.then_inc(p_turned, 1)

            def attend(a, n):
                rows, r = slice(64 * (n // 4), 64 * (n // 4) + 64), n % 4
                pe.wait_ge(pt_ready, 1 + 8 * a + n + 1)
                if n == 0:
                    pe.wait_ge(v_moved, a + 1)
                    pe.wait_ge(ya_steps, 1 + 2 * a)
                for m in range(6):
                    cfg, tile = (0, m) if m < 4 else (m - 3, r)
                    mm = nc.tensor.matmul(ps[rows, 6, r * P:(r + 1) * P], vN[:, cfg, tile, rows],
                                          pt[:, m * P:(m + 1) * P], start=(r == 0 and m == 0),
                                          stop=(m == 5), skip_group_check=True)
                mm.then_inc(attended, 1)

            for x in range(2 * N_ATT):
                half(0, x)
            with pe.Fori(0, 3) as a:
                for n in range(8):
                    scores(a, n)
                    half(a + 1, 3 * n)
                    half(a + 1, 3 * n + 1)
                    if n == 0:
                        token_transform(a)
                    turn_p(a, n)
                    half(a + 1, 3 * n + 2)
                    attend(a, n)

            def out_turn(n):
                pe.wait_ge(evacuated, E_OUT + n + 1)
                if n:
                    pe.wait_ge(out_added, n)
                else:
                    pe.wait_ge(yf_steps, 2 * 3 + 1)
                src = (ufT, sgf)[n % 2]
                for r in range(NT):
                    mm = nc.tensor.transpose(ps[:, 7, r * P:(r + 1) * P], src[:, r * P:(r + 1) * P], ident)
                mm.then_inc(out_turned, 1)

            for n in range(8):
                u, bank = U_OUT + n, (R_ATT + n) % 2
                scores(3, n)
                if n == 0:
                    token_transform(3)
                    pe.wait_ge(ya_steps, 1 + 2 * 3)
                tiles(u, u % 2, bank, yo_hi, yo_lo, range(0, 4), OUT_TILES[0:4], ready=True,
                      free=(evacuated, E_OUT + n - 1), start=True)
                if n:
                    out_turn(n - 1)
                turn_p(3, n)
                if n == 0:
                    pe.wait_ge(yf_steps, 2 * 4)
                tiles(u, u % 2, bank, yo_hi, yo_lo, range(4, 7), OUT_TILES[4:7], signal=units_done)
                attend(3, n)
            out_turn(7)
            pe.wait_ge(ya_steps, 1 + 2 * 4)
            pe.wait_ge(split_done, U_LAST + 1)
            pe.wait_ge(evacuated, E_OUT + 8)
            slot = U_LAST % 2
            for hv in range(2):
                w = slice(hv * S, (hv + 1) * S)
                for t in range(NT):
                    bank = (0, 1, 2, 3, 4, 5, 6, 7)[4 * hv + t]
                    out, q = ps[:, bank], slice(t * P, (t + 1) * P)
                    if bank == 7:
                        pe.wait_ge(out_added, DB)
                    nc.tensor.matmul(out, yo_hi[:, 7, q], w_hi[:, slot, w], start=True, stop=False)
                    nc.tensor.matmul(out, yo_hi[:, 7, q], w_lo[:, slot, w], start=False, stop=False)
                    nc.tensor.matmul(out, yo_lo[:, 7, q], w_hi[:, slot, w], start=False,
                                     stop=True).then_inc(out_sums, 1)

        @block.scalar
        def _(act):
            A = nc.scalar.activation

            act.wait_ge(tab_in, 16)
            A(small[:, 0:8], col("c", 0, DB), ACT.Silu).then_inc(cact_ready, 1)
            act.wait_ge(x_in, 16)
            for t in range(NT):
                if t:
                    act.wait_ge(row_stats, t)
                A(junk[:], x_tok[:, t], ACT.Square, accum_out=small[:, 8 + t:9 + t]).then_inc(row_stats, 1)
            act.wait_ge(row_stats, 4)
            act.wait_ge(setup, 3)
            A(small[:, 12:16], small[:, 8:12], ACT.Sqrt, bias=eps[:, 0:1], scale=1.0 / D).then_inc(row_stats, 1)
            act.wait_ge(mod0_ready, 2)
            for b in range(DB):
                act.wait_ge(x_turned, b + 1)
                if b >= 2:
                    act.wait_ge(h_lo_ready, b - 1)
                A(hf[:, b % 2], ps[:, 4 + b % 4], ACT.Identity, bias=mod[:, b:b + 1],
                  scale=coef[:, 0, b:b + 1]).then_inc(h_full, 1)
                act.wait_ge(h_full, b + 1)
                A(h_hi[:, b], hf[:, b % 2], ACT.Copy).then_inc(h_hi_ready, 1)

            act.wait_ge(units_done, 1 + 1)
            db = tab[0:SSD_HEADS, COL["dt_bias"]:COL["dt_bias"] + 1]
            A(dtw[:, 0], ps[0:SSD_HEADS, 0], ACT.Identity, bias=db).then_inc(dt_act, 1)
            A(dtw[:, 1], ps[0:SSD_HEADS, 0], ACT.Abs, bias=db).then_inc(evacuated, 1)
            act.wait_ge(dt_act, 1)
            A(dtw[:, 2], dtw[:, 0], ACT.Relu).then_inc(dt_act, 1)
            act.wait_ge(evacuated, 1)
            A(dtw[:, 1], dtw[:, 1], ACT.Exp, scale=-1.0).then_inc(dt_act, 1)
            A(small[0:SSD_HEADS, 20:21], tab[0:SSD_HEADS, COL["a_log"]:COL["a_log"] + 1],
              ACT.Exp).then_inc(dt_act, 1)
            act.wait_ge(dt_steps, 18)
            act.dma_start(acs_dram, dtw[:, 0]).then_inc(acs_stored, 16)
            act.wait_ge(acs_stored, 16)

            with act.Fori(0, GROUPS) as g:
                def load_abc(c):
                    act.wait_ge(decays, 1 + 4 * g + max(c - 1, 0))
                    src = acs_dram[bass.ds(HEADS_G * g, HEADS_G), c * P:(c + 1) * P]
                    act.dma_start(abc[:, c % 2], src.unsqueeze(0).broadcast_to([P, HEADS_G, P])
                                  ).then_inc(abc_in[c % 2], 16)

                def out_of(j, unit_no):
                    act.wait_ge(units_done, 1 + U_GRP + N_GRP * g + unit_no + 1)

                def conv_in(j):
                    out_of(j, j)
                    if j < 4:
                        act.wait_ge(sc_steps, 1 + 10 * g)
                    else:
                        act.wait_ge(conv_taps, 18 * g + 3 * (j - 4) + 3)
                    bank = ps[:, (R_GRP + j) % 2]
                    A(ev[:, j % 4, 3:3 + S], bank, ACT.Copy)
                    if j >= 2:
                        act.wait_ge(conv_out, 6 * g + j - 1)
                    A(cv[:, j % 2], bank, ACT.Identity, bias=col("conv", (6 * g + j) * 5 + 4),
                      scale=col("conv", (6 * g + j) * 5 + 3)).then_inc(evacuated, 1)

                def conv_silu(j):
                    act.wait_ge(conv_taps, 18 * g + 3 * j + 3)
                    dst = (BT[:], CT[:])[j] if j < 2 else xcT[:, j - 2]
                    A(dst, cv[:, j % 2], ACT.Silu).then_inc(conv_out, 1)
                    if j >= 2:
                        act.wait_ge(conv_out, 6 * g + j + 1)
                        A(yg[:, j - 2], xcT[:, j - 2], ACT.Identity,
                          scale=col("d_skip", 4 * g + j - 2)).then_inc(skip_ready, 1)

                def z(b):
                    out_of(6 + b, 6 + b)
                    A(zs[:, b], ps[:, (R_GRP + 6 + b) % 2], ACT.Silu).then_inc(evacuated, 1)

                def chunk(c):
                    if c < 3:
                        load_abc(c + 1)
                    act.wait_ge(abc_in[c % 2], 32 * g + 16 * (c // 2) + 16)
                    act.wait_ge(dt_tokens, 2)
                    act.wait_ge(y_done, 1 + 4 * g + max(c - 1, 0))
                    for h in range(HEADS_G):
                        ins = A(dec[:, c % 2, h], abc[:, c % 2, h], ACT.Relu,
                                bias=acsN[:, c, bass.ds(HEADS_G * g + h, 1)], scale=-1.0)
                    ins.then_inc(dec_args, 1)
                    act.wait_ge(dec_args, 4 * g + c + 1)
                    A(dec[:, c % 2], dec[:, c % 2], ACT.Exp, scale=-1.0)
                    A(eld[:, c], abc[:, c % 2, :, P - 1], ACT.Exp)
                    A(ect[:, c % 2], abc[:, c % 2], ACT.Exp).then_inc(decays, 1)

                def sc_in(e):
                    out_of(10 + e, 10 + e)
                    if e < 4:
                        act.wait_ge(conv_taps, 18 * g + 18)
                    else:
                        act.wait_ge(sc_steps, 1 + 10 * g + 1)
                    A(ev[:, (6 + e) % 4, 3:3 + S], ps[:, (R_GRP + 10 + e) % 2], ACT.Copy).then_inc(evacuated, 1)

                load_abc(0)
                act.wait_ge(gate_steps, 1 + 15 * g)
                conv_in(0)
                conv_in(1)
                for j in range(2, 6):
                    conv_silu(j - 2)
                    conv_in(j)
                    if j == 3:
                        chunk(0)
                conv_silu(4)
                conv_silu(5)
                z(0)
                chunk(1)
                z(1)
                z(2)
                chunk(2)
                z(3)
                chunk(3)
                sc_in(0)
                sc_in(1)
                sc_in(2)
                act.wait_ge(gate_steps, 1 + 15 * g + 5)
                A(xcT[:], yg[:], ACT.Square).then_inc(y_squared, 1)
                sc_in(3)
                act.wait_ge(group_sum, g + 1)
                A(sct[:], ps[:, 4], ACT.Sqrt, bias=eps[:, 0:1], scale=1.0 / S).then_inc(group_root, 1)
                sc_in(4)
                for b in range(4):
                    act.wait_ge(gate_steps, 1 + 15 * g + 8 + b)
                    A(y_hi[:, b], yg[:, b], ACT.Copy).then_inc(y_hi_ready, 1)
                sc_in(5)

            act.wait_ge(sc_steps, 1 + 10 * GROUPS)
            for q in range(2):
                A(sc_hi[:, 4 * q:4 * q + 4], ysc[:, 4 * q:4 * q + 4], ACT.Copy).then_inc(sc_hi_ready, 1)
            act.wait_ge(units_done, 1 + U_MIX)
            act.dma_start(x_tok2[:], arrays["x"]).then_inc(x2_in, 16)
            with act.Fori(0, 2) as i:
                def hi(j):
                    act.wait_ge(mix_steps, 1 + 16 * i + 4 * j + 3)
                    A(blocks(mix_hi, 4 * i + j), mixf[:, j % 2], ACT.Copy).then_inc(mix_hi_ready, 1)
                for j in range(4):
                    for m in range(3):
                        act.wait_ge(units_done, 1 + U_MIX + 12 * i + 3 * j + m + 1)
                        if m == 0 and j < 2:
                            act.wait_ge(mix_steps, 1 + 16 * i)
                        elif m == 0:
                            act.wait_ge(mix_steps, 1 + 16 * i + 4 * (j - 2) + 3)
                        A(gts[:, j % 2, m], ps[:, (R_MIX + 3 * j + m) % 2],
                          ACT.Sigmoid if m < 2 else ACT.Copy).then_inc(evacuated, 1)
                        if m == 0 and j:
                            hi(j - 1)
                hi(3)

            for b in range(DB):
                act.wait_ge(xt_turned, b + 1)
                if b == 0:
                    act.wait_ge(mix_steps, 1 + 32)
                A(xT[:, b], ps[:, 4 + b % 2], ACT.Copy).then_inc(xt_ready, 1)

            with act.Fori(0, DB // 2) as i:
                for j in range(2):
                    act.wait_ge(units_done, 1 + U_WO + 2 * i + j + 1)
                    A(blocks(mo, 2 * i + j), ps[:, (R_WO + j) % 2], ACT.Copy)
                    act.wait_ge(n1a["summed"], 1 + 2 * i)
                    A(sq[:, j], ps[:, (R_WO + j) % 2], ACT.Square).then_inc(evacuated, 1)

            def root(n, dst):
                act.wait_ge(n["total"], 1)
                A(dst[:], ps[:, 4], ACT.Sqrt, bias=eps[:, 0:1], scale=1.0 / D).then_inc(n["root"], 1)

            def residual_squares(n, before, sqt):
                for b in range(DB):
                    act.wait_ge(before["steps"], 1 + 2 * b + 2)
                    if b >= 2:
                        act.wait_ge(n["summed"], 1 + b - 1)
                    A(sqt[:, b % 2], xT[:, b], ACT.Square).then_inc(n["squared"], 1)

            root(n1a, rn)
            residual_squares(n1b, n1a, sq)
            root(n1b, rn)
            for b in range(DB):
                act.wait_ge(n1b["steps"], 1 + 2 * b + 1)
                A(h_hi[:, b], hp[:, b % 2], ACT.Identity, bias=mod[:, 24 + b:25 + b]).then_inc(n1b["hi"], 1)

            with act.Fori(0, FF_PAIRS // 2) as i:
                def tap_in(j):
                    act.wait_ge(units_done, 1 + U_UP + 4 * i + j + 1)
                    act.wait_ge(ffn_taps, 8 * i + 2 * j + 2)
                    act.wait_ge(ffn_steps, 4 * i + 2 * (j // 2) + 1)
                    A(fe[:, j, 2:2 + S], ps[:, (R_UP + j) % 2], ACT.Copy)
                    A(fcv[:, j], ps[:, (R_UP + j) % 2], ACT.Identity, bias=col("ffn_w", 16 * i + 4 * j + 3),
                      scale=col("ffn_w", 16 * i + 4 * j + 2)).then_inc(evacuated, 1)

                def silu(p):
                    act.wait_ge(ffn_taps, 8 + 8 * i + 4 * p + 2)
                    A(fcv[:, 2 * p], fcv[:, 2 * p], ACT.Silu).then_inc(ffn_silu, 1)

                def hi(p):
                    act.wait_ge(ffn_steps, 4 + 4 * i + 2 * p + 1)
                    A(blocks(act_hi, 2 * i + p), af[:, p], ACT.Copy).then_inc(act_hi_ready, 1)

                tap_in(0)
                tap_in(1)
                silu(0)
                tap_in(2)
                hi(0)
                tap_in(3)
                silu(1)
                hi(1)

            with act.Fori(0, 2) as i:
                for n in range(4):
                    act.wait_ge(units_done, 1 + U_DOWN + 12 * i + 3 * n + 3)
                    A(blocks(fo, 4 * i + n), ps[:, (R_DOWN + n) % 2], ACT.Copy)
                    act.wait_ge(n2a["summed"], 1 + 4 * i + max(n - 1, 0))
                    A(sq6[:, n % 2], ps[:, (R_DOWN + n) % 2], ACT.Square).then_inc(evacuated, 1)
            root(n2a, rn6)
            residual_squares(n2b, n2a, sq6)
            act.wait_ge(n2a["steps"], 1 + 2 * DB)
            act.dma_start(dft[:], arrays["dft"]).then_inc(att_in, 16)
            act.dma_start(bias[:], arrays["dist"]).then_inc(att_in, 16)
            act.dma_start(wfb[:], arrays["w_fourier"]).then_inc(att_in, 16)
            act.dma_start(dhd[:], arrays["dft_head"]).then_inc(att_in, 16)
            root(n2b, rn6)
            for b in range(DB):
                act.wait_ge(n2b["steps"], 1 + 2 * b + 1)
                A(permuted(h_hi[:, b]), natural(hp6[:, b % 2]), ACT.Copy).then_inc(n2b["hi"], 1)
            for b in range(DB):
                act.wait_ge(n2b["turned"], b + 1)
                A(xN[:, :, b * P:(b + 1) * P], ps[:, 6 + b % 2].rearrange("p (r c) -> p r c", r=NT),
                  ACT.Copy).then_inc(n2b["out"], 1)
            act.wait_ge(n2b["out"], DB)
            act.dma_start(x2_dram, xN[:]).then_inc(x2_stored, 16)
            act.wait_ge(att_in, 16 * 4)
            act.wait_ge(wf_sums, 1)
            for m in range(2):
                A(wf[:, 2 * m:2 * m + 2], ps[:, 2 + m].rearrange("p (b w) -> p b w", b=2),
                  ACT.Copy).then_inc(wf_ready, 1)
            act.wait_ge(x2_stored, 16)

            def take(p, j):
                act.wait_ge(units_done, 1 + U_ATT + N_ATT * p + j + 1)
                bank = ps[:, (R_ATT + j) % 2]
                first = isinstance(p, int) and p == 0
                if j < 6:
                    if not (first and j == 0):
                        act.wait_ge(qk_total, 6 * p + j)
                    if j == 0 and not first:
                        act.wait_ge(qk_moved, p)
                    A(qk_next[:, j], bank, ACT.Copy)
                    A(qsq[:], bank, ACT.Square).then_inc(evacuated, 1)
                elif j < 9:
                    if not (first and j == 6):
                        act.wait_ge(v_turned, 3 * p + j - 6)
                    A(vT[:], bank, ACT.Copy).then_inc(evacuated, 1)
                elif j == 9:
                    if not first:
                        act.wait_ge(fv_done, 2 * p)
                    A(ufT[:], bank, ACT.Copy).then_inc(evacuated, 1)
                elif j == 10:
                    if not first:
                        act.wait_ge(yf_steps, 2 * p - 1)
                    A(sgf[:], bank, ACT.Silu).then_inc(evacuated, 1)
                else:
                    if not first:
                        act.wait_ge(gate_moved, p)
                    A(sga_next[:], bank, ACT.Silu).then_inc(evacuated, 1)
                if 1 <= j <= 6:
                    m = j - 1
                    act.wait_ge(qk_total, 6 * p + m + 1)
                    if not (first and m < 3):
                        act.wait_ge(qk_steps, 12 * p + 2 * (m - 3) + 2)
                    A(qrt[:, m % 3], ps[:, 7], ACT.Sqrt, bias=eps[:, 1:2] if m < 3 else eps[:, 0:1],
                      scale=1.0 if m < 3 else 1.0 / HP).then_inc(qk_root, 1)
                if 7 <= j <= 9:
                    c = j - 7
                    act.wait_ge(v_turned, 3 * p + c + 1)
                    if c == 0 and not first:
                        act.wait_ge(v_moved, p)
                    A(vN_next[:, c], ps[:, 7].rearrange("p (t w) -> p t w", t=NT), ACT.Copy).then_inc(v_ready, 1)
                if j >= 10:
                    m = j - 10
                    act.wait_ge(fv_done, 2 * p + m + 1)
                    if m == 0 and not first:
                        act.wait_ge(ft_done, p)
                    A(fv[:, 2 * m:2 * m + 2], ps[:, 7].rearrange("p (t w) -> p t w", t=2),
                      ACT.Copy).then_inc(fv_ready, 1)

            def move_v(p):
                act.wait_ge(v_ready, 3 * p + 3)
                if not (isinstance(p, int) and p == 0):
                    act.wait_ge(attended, 1 + 8 * p)
                A(vN[:], vN_next[:], ACT.Copy).then_inc(v_moved, 1)

            def exp(a, n):
                act.wait_ge(biased, 1 + 8 * a + n + 1)
                A(pr[:], pr[:], ACT.Exp, bias=stat[:, 0:1], scale=-1.0,
                  accum_out=stat[:, 1:2]).then_inc(exped, 1)

            def pt_out(a, n):
                act.wait_ge(p_turned, 1 + 8 * a + n + 1)
                act.wait_ge(attended, 1 + 8 * a + n)
                A(pt[:], ps[:, 4:6].rearrange("p b w -> p (b w)")[:, 0:6 * P], ACT.Copy).then_inc(pt_ready, 1)
                A(bias[:, n % 4], bias[:, n % 4], ACT.Copy, scale=0.5).then_inc(bias_scaled, 1)

            def hi_fourier(a):
                act.wait_ge(yf_steps, 2 * a + 1)
                A(blocks(yo_hi, a), yf[:], ACT.Copy).then_inc(yf_hi_ready, 1)

            def hi_attention(a):
                act.wait_ge(ya_steps, 1 + 2 * a + 1)
                A(blocks(yo_hi, 4 + a), ya[:], ACT.Copy).then_inc(ya_hi_ready, 1)

            for j in range(N_ATT):
                take(0, j)
            move_v(0)
            with act.Fori(0, 3) as a:
                for n in range(8):
                    exp(a, n)
                    take(a + 1, 3 * n // 2)
                    pt_out(a, n)
                    if n == 0:
                        hi_fourier(a)
                    if n % 2:
                        take(a + 1, (3 * n + 1) // 2)
                hi_attention(a)
                move_v(a + 1)

            act.wait_ge(units_done, 1 + U_OUT)
            for hv in range(2):
                cols = slice(hv * S, (hv + 1) * S)
                act.dma_start(x_res[:, :, cols], x2_dram[:, :, cols]).then_inc(x_res_in[hv], 16)
            for n in range(8):
                exp(3, n)
                pt_out(3, n)
                if n == 0:
                    hi_fourier(3)
                act.wait_ge(units_done, 1 + U_OUT + n + 1)
                if n >= 2:
                    act.wait_ge(out_turned, n - 1)
                A((ufT, sgf)[n % 2][:], ps[:, (R_ATT + n) % 2], ACT.Copy).then_inc(evacuated, 1)
            hi_attention(3)
            out = arrays["out"].rearrange("(i r) d -> i r d", r=NT)
            for hv in range(2):
                for t in range(NT):
                    cols = slice(hv * S, (hv + 1) * S)
                    act.wait_ge(out_steps, 4 * hv + t + 1)
                    act.dma_start(out[:, t, cols], x_res[:, t, cols]).then_inc(out_stored, 16)
            act.wait_ge(out_stored, 16 * 8)

        @block.vector
        def _(dve):
            V = nc.vector
            TT, STT, TS = V.tensor_tensor, V.scalar_tensor_tensor, V.tensor_scalar

            V.memset(ones[:], 1.0).then_inc(setup, 1)
            V.memset(eps[:, 0:1], EPS).then_inc(setup, 1)
            V.memset(eps[:, 1:2], HP * EPS).then_inc(setup, 1)
            V.memset(ev[:, :, 0:3], 0.0).then_inc(setup, 1)
            V.memset(scp[:, 0:2], 0.0).then_inc(setup, 1)

            def ada_start(m):
                for k in range(8):
                    n = 8 * m + k
                    dve.wait_ge(ada0_in[k], 16 * (m + 1))
                    if k == 0:
                        TS(acc0[:, m], ada0[:, k], small[:, k:k + 1], None, ALU.mult).then_inc(ada0_steps, 1)
                    else:
                        dve.wait_ge(ada0_steps, n)
                        STT(acc0[:, m], ada0[:, k], small[:, k:k + 1], acc0[:, m], ALU.mult,
                            ALU.add).then_inc(ada0_steps, 1)

            dve.wait_ge(cact_ready, 1)
            ada_start(0)
            dve.wait_ge(row_stats, 5)
            V.reciprocal(small[:, 16:20], small[:, 12:16]).then_inc(setup, 1)
            dve.wait_ge(setup, 6)
            for t in range(NT):
                TS(x_tok[:, t], x_tok[:, t], small[:, 16 + t:17 + t], None, ALU.mult).then_inc(row_scaled, 1)
            ada_start(1)
            dve.wait_ge(mod0_sums, 1)
            TT(mod[:, 0:16], ps[:, 2, 0:16], col("ada_b", 0, 16), ALU.add).then_inc(mod0_ready, 1)
            dve.wait_ge(mod0_ready, 1)
            STT(coef[:, 0], mod[:, 8:16], 1.0, col("g_pre", 0, DB), ALU.add, ALU.mult).then_inc(mod0_ready, 1)
            for b in range(DB):
                dve.wait_ge(h_hi_ready, b + 1)
                TT(h_lo[:, b], hf[:, b % 2], h_hi[:, b].bitcast(F32), ALU.subtract).then_inc(h_lo_ready, 1)
            V.memset(ssd_acc[:], 0.0).then_inc(setup, 1)

            n_dt = [0]

            def dt_step(ins):
                ins.then_inc(dt_steps, 1)
                n_dt[0] += 1
                dve.wait_ge(dt_steps, n_dt[0])

            e, z = dtw[:, 1], dtw[:, 4]
            dve.wait_ge(dt_act, 3)
            dt_step(TS(dtw[:, 3], e, 2.0, None, ALU.add))
            dt_step(V.reciprocal(dtw[:, 4], dtw[:, 3]))
            dt_step(TT(dtw[:, 3], e, dtw[:, 4], ALU.mult))
            dt_step(TT(z, dtw[:, 3], dtw[:, 3], ALU.mult))
            dt_step(TS(dtw[:, 5], z, 1.0 / 15, None, ALU.mult))
            for k in (13, 11, 9, 7, 5, 3):
                dt_step(STT(dtw[:, 5], dtw[:, 5], 1.0 / k, z, ALU.add, ALU.mult))
            dt_step(STT(dtw[:, 6], dtw[:, 5], 1.0, dtw[:, 3], ALU.add, ALU.mult))
            dt_step(STT(dtw[:, 7], dtw[:, 6], 2.0, dtw[:, 2], ALU.mult, ALU.add))
            dve.wait_ge(dt_act, 4)
            dt_step(TS(dtw[:, 1], dtw[:, 7], small[0:SSD_HEADS, 20:21], -1.0, ALU.mult, ALU.mult))
            for c in range(NT):
                cols = slice(c * P, (c + 1) * P)
                dt_step(V.tensor_tensor_scan(dtw[:, 0, cols], ones[0:SSD_HEADS, :], dtw[:, 1, cols], 0.0,
                                             ALU.mult, ALU.add))
            dve.wait_ge(dt_turned, 1)
            both = ps[:, 5, 0:4 * 64].rearrange("p (c w) -> p c w", c=NT)
            V.tensor_copy(dtN[:], both[:, :, 0:32]).then_inc(dt_tokens, 1)
            V.tensor_copy(acsN[:], both[:, :, 32:64]).then_inc(dt_tokens, 1)
            dve.wait_ge(dt_tokens, 2)
            dve.wait_ge(setup, 7)

            with dve.Fori(0, GROUPS) as g:
                def ada_piece(n):
                    k, hv = n // 2, n % 2
                    dve.wait_ge(ada_in[hv], 128 * g + 16 * k + 16)
                    part, w = ada_acc[:, hv * S:(hv + 1) * S], small[:, k:k + 1]
                    if k == 0:
                        dve.wait_ge(mod_sums, 1 + g)
                        TS(part, ada_raw[:, hv], w, None, ALU.mult).then_inc(ada_steps, 1)
                    else:
                        dve.wait_ge(ada_steps, 1 + 16 * g + n - 1)
                        STT(part, ada_raw[:, hv], w, part, ALU.mult, ALU.add).then_inc(ada_steps, 1)

                def conv(j):
                    dve.wait_ge(evacuated, E_GRP + 16 * g + j + 1)
                    for k in range(3):
                        if k:
                            dve.wait_ge(conv_taps, 18 * g + 3 * j + k)
                        STT(cv[:, j % 2], ev[:, j % 4, k:k + S], col("conv", (6 * g + j) * 5 + k),
                            cv[:, j % 2], ALU.mult, ALU.add).then_inc(conv_taps, 1)
                        if k < 2 and j < 5:
                            ada_piece(2 * j + k)

                def chunk(c):
                    base = 24 * g + 6 * c
                    dve.wait_ge(chunk_inputs, 4 * g + c + 1)
                    dve.wait_ge(y_done, 1 + 4 * g + max(c - 1, 0))
                    TT(scm[:, c % 2], ps[:, 5, 0:P], causal, ALU.mult).then_inc(chunk_steps, 1)
                    V.tensor_copy(bn[:, c % 2], ps[:, 5, P:2 * P]).then_inc(chunk_steps, 1)
                    TT(by_head(xdt[:, c % 2]), by_head(ps[:, 4]), per_token(dtN, c, g),
                       ALU.mult).then_inc(chunk_steps, 1)
                    dve.wait_ge(decays, 1 + 4 * g + c + 1)
                    dve.wait_ge(chunk_steps, 1 + base + 3)
                    TT(by_head(xst[:, c % 2]), by_head(xdt[:, c % 2]),
                       dec[:, c % 2, :, P - 1:P].broadcast_to([P, HEADS_G, HP]), ALU.mult).then_inc(chunk_steps, 1)
                    dve.wait_ge(chunk_steps, 1 + base + 4)
                    TT(dec[:, c % 2], dec[:, c % 2], scm[:, c % 2].unsqueeze(1).broadcast_to([P, HEADS_G, P]),
                       ALU.mult).then_inc(chunk_steps, 1)
                    TT(ect[:, c % 2], ect[:, c % 2],
                       CT[:, c * P:(c + 1) * P].unsqueeze(1).broadcast_to([P, HEADS_G, P]),
                       ALU.mult).then_inc(chunk_steps, 1)

                def state(c):
                    dve.wait_ge(s_done, 3 * g + c + 1)
                    if c == 0:
                        V.tensor_copy(hst[:, 1], ps[:, 7]).then_inc(state_steps, 1)
                        return
                    new, old = (c + 1) % 2, c % 2
                    if c == 2:
                        dve.wait_ge(y_done, 1 + 4 * g + 2)
                    dve.wait_ge(state_steps, 1 + 5 * g + (1, 3)[c - 1])
                    TT(by_head(hst[:, new]), by_head(hst[:, old]),
                       eld[:, c].unsqueeze(2).broadcast_to([P, HEADS_G, HP]), ALU.mult).then_inc(state_steps, 1)
                    dve.wait_ge(state_steps, 1 + 5 * g + (2, 4)[c - 1])
                    TT(hst[:, new], hst[:, new], ps[:, 7], ALU.add).then_inc(state_steps, 1)

                def add_y(c):
                    dve.wait_ge(y_done, 1 + 4 * g + c + 1)
                    dve.wait_ge(skip_ready, 4 * g + 4)
                    y = yg[:, :, c * P:(c + 1) * P]
                    TT(y, y, ps[:, 6 - 4 * (c % 2)].rearrange("p (b l) -> p b l", b=4), ALU.add).then_inc(gate_steps, 1)

                def short_conv(q):
                    e = 3 * q
                    dve.wait_ge(evacuated, E_GRP + 16 * g + 10 + e + 2)
                    TT(scp[:, 2:2 + S], ev[:, (6 + e) % 4, 3:3 + S], ev[:, (7 + e) % 4, 3:3 + S],
                       ALU.mult).then_inc(sc_steps, 1)
                    y = zs[:, q]
                    for k in (2, 1, 0):
                        dve.wait_ge(sc_steps, 1 + 10 * g + 5 * q + 3 - k)
                        w, u = col("sc_w", (2 * g + q) * 3 + k), scp[:, k:k + S]
                        if k == 2:
                            TS(y, u, w, None, ALU.mult).then_inc(sc_steps, 1)
                        else:
                            STT(y, u, w, y, ALU.mult, ALU.add).then_inc(sc_steps, 1)
                    dve.wait_ge(sc_steps, 1 + 10 * g + 5 * q + 4)
                    dve.wait_ge(evacuated, E_GRP + 16 * g + 10 + e + 3)
                    TT(blocks(ysc, 2 * g + q), y, ev[:, (8 + e) % 4, 3:3 + S], ALU.mult).then_inc(sc_steps, 1)

                for j in range(6):
                    conv(j)
                chunk(0)
                ada_piece(10)
                chunk(1)
                ada_piece(11)
                state(0)
                chunk(2)
                add_y(0)
                state(1)
                ada_piece(12)
                ada_piece(13)
                chunk(3)
                ada_piece(14)
                ada_piece(15)
                add_y(1)
                state(2)
                add_y(2)
                add_y(3)
                dve.wait_ge(gate_steps, 1 + 15 * g + 4)
                TT(yg[:], yg[:], zs[:], ALU.mult).then_inc(gate_steps, 1)
                dve.wait_ge(gate_steps, 1 + 15 * g + 5)
                short_conv(0)
                dve.wait_ge(y_squared, g + 1)
                V.tensor_reduce(sct[:], xcT[:].rearrange("p b t -> p t b"), AX.X, ALU.add).then_inc(gate_steps, 1)
                dve.wait_ge(mod_sums, 1 + g + 1)
                TT(mod[:, bass.ds(16 + 8 * g, 8)], ps[:, 7, 0:8], col("ada_b", 16 + 8 * g, 8),
                   ALU.add).then_inc(mod_ready, 1)
                dve.wait_ge(group_root, 1 + g + 1)
                V.reciprocal(sct[:], sct[:]).then_inc(gate_steps, 1)
                dve.wait_ge(gate_steps, 1 + 15 * g + 7)
                for b in range(4):
                    STT(yg[:, b], yg[:, b], col("ssd_g", 4 * g + b), sct[:], ALU.mult,
                        ALU.mult).then_inc(gate_steps, 1)
                for b in range(4):
                    dve.wait_ge(y_hi_ready, 4 * g + b + 1)
                    TT(y_lo[:, b], yg[:, b], y_hi[:, b].bitcast(F32), ALU.subtract).then_inc(gate_steps, 1)
                short_conv(1)
                for n in range(DB):
                    if n % 2 == 0:
                        dve.wait_ge(half_done, 4 * g + n // 2 + 1)
                    else:
                        dve.wait_ge(units_done, 1 + U_GRP + N_GRP * g + 16 + n // 2 + 1)
                    TT(ssd_acc[:, n], ssd_acc[:, n], ps[:, (R_GRP + 16 + n) % 2], ALU.add).then_inc(acc_steps, 1)

            dve.wait_ge(mod_ready, 1 + 4)
            TT(coef[:, 1], mod[:, 16:24], col("g_post", 0, DB), ALU.mult).then_inc(coef_ready, 1)
            STT(coef[:, 2], mod[:, 32:40], 1.0, col("f_pre", 0, DB), ALU.add, ALU.mult).then_inc(coef_ready, 1)
            TT(coef[:, 3], mod[:, 40:48], col("f_post", 0, DB), ALU.mult).then_inc(coef_ready, 1)
            for q in range(2):
                dve.wait_ge(sc_hi_ready, q + 1)
                TT(sc_lo[:, 4 * q:4 * q + 4], ysc[:, 4 * q:4 * q + 4], sc_hi[:, 4 * q:4 * q + 4].bitcast(F32),
                   ALU.subtract).then_inc(sc_lo_ready, 1)
            dve.wait_ge(acc_steps, 1 + 32)
            with dve.Fori(0, 2) as i:
                for j in range(4):
                    at_ = 16 * i + 4 * j
                    dve.wait_ge(evacuated, E_MIX + 12 * i + 3 * j + 3)
                    TT(gts[:, j % 2, 2], gts[:, j % 2, 2], gts[:, j % 2, 1], ALU.mult).then_inc(mix_steps, 1)
                    TT(gts[:, j % 2, 0], gts[:, j % 2, 0], blocks(ssd_acc, 4 * i + j), ALU.mult).then_inc(mix_steps, 1)
                    dve.wait_ge(mix_steps, 1 + at_ + 2)
                    TT(mixf[:, j % 2], gts[:, j % 2, 0], gts[:, j % 2, 2], ALU.add).then_inc(mix_steps, 1)
                    dve.wait_ge(mix_hi_ready, 4 * i + j + 1)
                    TT(blocks(mix_lo, 4 * i + j), mixf[:, j % 2], blocks(mix_hi, 4 * i + j).bitcast(F32),
                       ALU.subtract).then_inc(mix_steps, 1)

            dve.wait_ge(xt_ready, DB)
            V.memset(ssum[:], 0.0).then_inc(setup, 1)
            dve.wait_ge(setup, 8)
            with dve.Fori(0, DB // 2) as i:
                for j in range(2):
                    dve.wait_ge(evacuated, E_WO + 2 * i + j + 1)
                    dve.wait_ge(n1a["summed"], 1 + 2 * i + j)
                    TT(ssum[:], ssum[:], sq[:, j], ALU.add).then_inc(n1a["summed"], 1)

            def rsqrt(n, r):
                dve.wait_ge(n["root"], 1)
                V.reciprocal(r[:], r[:]).then_inc(n["steps"], 1)
                dve.wait_ge(n["steps"], 1)

            def add_branch(n, branch, r, k):
                rsqrt(n, r)
                for b in range(DB):
                    STT(branch[:, b], branch[:, b], coef[:, k, b:b + 1], r[:], ALU.mult,
                        ALU.mult).then_inc(n["steps"], 1)
                    dve.wait_ge(n["steps"], 1 + 2 * b + 1)
                    TT(xT[:, b], xT[:, b], branch[:, b], ALU.add).then_inc(n["steps"], 1)

            def sum_squares(n, sqt, total):
                for b in range(DB):
                    dve.wait_ge(n["squared"], b + 1)
                    if b == 0:
                        V.tensor_copy(total[:], sqt[:, 0]).then_inc(n["summed"], 1)
                    else:
                        dve.wait_ge(n["summed"], 1 + b)
                        TT(total[:], total[:], sqt[:, b % 2], ALU.add).then_inc(n["summed"], 1)

            dve.wait_ge(coef_ready, 3)
            add_branch(n1a, mo, rn, 1)
            sum_squares(n1b, sq, ssum)
            rsqrt(n1b, rn)
            for b in range(DB):
                STT(hp[:, b % 2], xT[:, b], coef[:, 2, b:b + 1], rn[:], ALU.mult, ALU.mult).then_inc(n1b["steps"], 1)
                dve.wait_ge(n1b["hi"], b + 1)
                STT(h_lo[:, b], hp[:, b % 2], mod[:, 24 + b:25 + b], h_hi[:, b].bitcast(F32), ALU.add,
                    ALU.subtract).then_inc(n1b["steps"], 1)

            for j in range(4):
                V.memset(fe[:, j, 0:2], 0.0).then_inc(ffn_taps, 2)
            V.memset(af[:, 0, 0:1], 0.0).then_inc(ffn_steps, 4)
            with dve.Fori(0, FF_PAIRS // 2) as i:
                for p in range(2):
                    for j in (2 * p, 2 * p + 1):
                        dve.wait_ge(evacuated, E_UP + 4 * i + j + 1)
                        for k in range(2):
                            if k:
                                dve.wait_ge(ffn_taps, 8 + 8 * i + 2 * j + 1)
                            STT(fcv[:, j], fe[:, j, k:k + S], col("ffn_w", 16 * i + 4 * j + k), fcv[:, j],
                                ALU.mult, ALU.add).then_inc(ffn_taps, 1)
                    dve.wait_ge(ffn_taps, 8 + 8 * i + 4 * p + 4)
                    dve.wait_ge(ffn_silu, 2 * i + p + 1)
                    TT(af[:, p], fcv[:, 2 * p], fcv[:, 2 * p + 1], ALU.mult).then_inc(ffn_steps, 1)
                    dve.wait_ge(act_hi_ready, 2 * i + p + 1)
                    TT(blocks(act_lo, 2 * i + p), af[:, p], blocks(act_hi, 2 * i + p).bitcast(F32),
                       ALU.subtract).then_inc(ffn_steps, 1)

            V.memset(ssum6[:], 0.0).then_inc(setup, 1)
            dve.wait_ge(setup, 9)
            with dve.Fori(0, 2) as i:
                for n in range(4):
                    dve.wait_ge(evacuated, E_DOWN + 4 * i + n + 1)
                    dve.wait_ge(n2a["summed"], 1 + 4 * i + n)
                    TT(ssum6[:], ssum6[:], sq6[:, n % 2], ALU.add).then_inc(n2a["summed"], 1)
            add_branch(n2a, fo, rn6, 3)
            sum_squares(n2b, sq6, ssum6)
            rsqrt(n2b, rn6)
            for b in range(DB):
                STT(hp6[:, b % 2], xT[:, b], col("nw2", b), rn6[:], ALU.mult, ALU.mult).then_inc(n2b["steps"], 1)
                dve.wait_ge(n2b["hi"], b + 1)
                TT(permuted(h_lo[:, b]), natural(hp6[:, b % 2]), permuted(h_hi[:, b]).bitcast(F32),
                   ALU.subtract).then_inc(n2b["steps"], 1)

            def scale_qk(p, j):
                dve.wait_ge(qk_root, 6 * p + j + 1)
                V.reciprocal(qrt[:, j % 3], qrt[:, j % 3]).then_inc(qk_steps, 1)
                dve.wait_ge(qk_steps, 12 * p + 2 * j + 1)
                STT(qk_next[:, j], qk_next[:, j], col("qk_w", 6 * p + j), qrt[:, j % 3], ALU.mult,
                    ALU.mult).then_inc(qk_steps, 1)

            def move_qk(p):
                dve.wait_ge(qk_steps, 12 * p + 12)
                if not (isinstance(p, int) and p == 0):
                    dve.wait_ge(scored, 8 * p)
                V.tensor_copy(qk[:], qk_next[:]).then_inc(qk_moved, 1)

            def move_gate(p):
                dve.wait_ge(evacuated, E_ATT + N_ATT * p + 12)
                V.tensor_copy(sga[:], sga_next[:]).then_inc(gate_moved, 1)

            def split_y(source, gate, y, steps, step, hi_ready, pair, at_block):
                TT(y[:], source, gate, ALU.mult).then_inc(steps, 1)
                dve.wait_ge(hi_ready, pair + 1)
                TT(blocks(yo_lo, at_block), y[:], blocks(yo_hi, at_block).bitcast(F32),
                   ALU.subtract).then_inc(steps, 1)

            def fourier(a):
                dve.wait_ge(ft_done, a + 1)
                dve.wait_ge(evacuated, E_ATT + N_ATT * a + 11)
                split_y(ps[:, 7], sgf[:], yf, yf_steps, 2 * a, yf_hi_ready, a, a)

            def attention(a):
                dve.wait_ge(attended, 1 + 8 * a + 8)
                dve.wait_ge(gate_moved, a + 1)
                split_y(ps[:, 6], sga[:], ya, ya_steps, 2 * a, ya_hi_ready, a, 4 + a)

            def add_bias(a, n):
                dve.wait_ge(scored, 8 * a + n + 1)
                dve.wait_ge(bias_scaled, 8 * a + n + 1)
                dve.wait_ge(p_turned, 1 + 8 * a + n)
                V.memset(stat[:, 3:4], 0.0)
                V.tensor_tensor_reduce(
                    pr[:], ps[:, 2:4].rearrange("p b w -> p (b w)")[:, 0:6 * P], bias[:, n % 4],
                    -1.0, 3e38, ALU.add, ALU.min, stat[:, 0:1]).then_inc(biased, 1)

            def normalise(a, n):
                dve.wait_ge(exped, 8 * a + n + 1)
                V.reciprocal(stat[:, 2:3], stat[:, 1:2]).then_inc(normed, 1)
                dve.wait_ge(normed, 16 * a + 2 * n + 1)
                TS(pr[:], pr[:], stat[:, 2:3], None, ALU.mult).then_inc(normed, 1)

            for j in range(6):
                scale_qk(0, j)
            move_qk(0)
            move_gate(0)
            with dve.Fori(0, 3) as a:
                for n in range(8):
                    add_bias(a, n)
                    normalise(a, n)
                    if n == 0:
                        fourier(a)
                    elif n < 7:
                        scale_qk(a + 1, n - 1)
                move_qk(a + 1)
                attention(a)
                move_gate(a + 1)

            def add_block(n):
                dve.wait_ge(out_turned, n + 1)
                dve.wait_ge(x_res_in[n // 4], 16)
                x = x_res[:, :, n * P:(n + 1) * P]
                TT(x, x, ps[:, 7].rearrange("p (r c) -> p r c", r=NT), ALU.add).then_inc(out_added, 1)

            for n in range(8):
                add_bias(3, n)
                normalise(3, n)
                if n == 0:
                    fourier(3)
                else:
                    add_block(n - 1)
            attention(3)
            add_block(7)
            dve.wait_ge(out_added, DB)
            for m in range(8):
                hv, t = m // 4, m % 4
                dve.wait_ge(out_sums, m + 1)
                x = x_res[:, t, hv * S:(hv + 1) * S]
                TT(x, x, ps[:, m], ALU.add).then_inc(out_steps, 1)


def lay_out(i):
    f = {k: np.ascontiguousarray(np.asarray(v, np.float32)) for k, v in i.items()}

    def blocks_of(w):
        k, n = w.shape
        return w.reshape(k // P, P, n // P, P).transpose(2, 1, 0, 3)

    def column(v):
        return v.reshape(-1, P).T

    zero = np.zeros
    w_in = f["w_in"][0]
    cut = np.cumsum([2048, 3072, SSD_HEADS, D, D, D])
    z, xbc, dt, scb, scc, sch, gates = (w_in[:, x:y] for x, y in zip([0, *cut], [*cut, w_in.shape[1]]))
    z, xbc, scb, scc, sch, gates = map(blocks_of, (z, xbc, scb, scc, sch, gates))
    units = []
    units.append(blocks_of(np.concatenate([dt, zero((D, P - SSD_HEADS), np.float32)], 1))[0])
    w_ssd = blocks_of(f["w_ssd_out"][0])
    for g in range(GROUPS):
        units += [xbc[16 + g], xbc[20 + g]] + [xbc[4 * g + b] for b in range(4)] + [z[4 * g + b] for b in range(4)]
        for q in range(2):
            units += [scc[2 * g + q], sch[2 * g + q], scb[2 * g + q]]
        for n in range(0, DB, 2):
            units.append(np.concatenate([w_ssd[n][:, 4 * g:4 * g + 4], w_ssd[n + 1][:, 4 * g:4 * g + 4]], 1))
    w_sc = blocks_of(f["w_sc_out"][0])
    for j in range(DB):
        units += [gates[j], gates[DB + j], w_sc[j]]
    units += list(blocks_of(f["w_o"][0]))
    up = blocks_of(f["w_up"][0])
    for p in range(FF_PAIRS):
        units += [up[p], up[FF_PAIRS + p]]
    down = blocks_of(f["w_down"][0])
    for n in range(DB):
        units += [down[n][:, 0:8], down[n][:, 8:16],
                  np.concatenate([down[n][:, 16:22], zero((P, 2, P), np.float32)], 1)]
    w2 = f["w_in_2"]
    qkv = CFG * S
    uf, gf = blocks_of(w2[:, :S]), blocks_of(w2[:, S:2 * S])
    q, k, v = (blocks_of(w2[:, 2 * S + n * qkv:2 * S + (n + 1) * qkv]) for n in range(3))
    ga = blocks_of(w2[:, 2 * S + 3 * qkv:])
    for i2 in range(4):
        for m in (q, k, v):
            units += [m[4 * c + i2] for c in range(CFG)]
        units += [uf[i2], gf[i2], ga[i2]]
    out2 = blocks_of(f["w_out_2"])
    for n in range(DB):
        units.append(np.concatenate([out2[n][:, OUT_TILES], zero((P, 1, P), np.float32)], 1))
    units.append(out2[:, :, 7].transpose(1, 0, 2))
    stream = np.stack([u.reshape(P, UW) for u in units])
    assert len(units) == UNITS

    t = {}
    t["ident"] = np.eye(P, dtype=np.float32)
    t["causal"] = np.triu(np.ones((P, P), np.float32))
    t["head_ones"] = np.kron(np.eye(2, dtype=np.float32), np.ones((HP, HP), np.float32))
    t["c"] = column(f["c"][0])
    t["ada_b"] = column(f["ada_b"][0])
    t["g_pre"], t["g_post"] = column(f["mix_pre_g"][0]), column(f["mix_post_g"][0])
    t["f_pre"], t["f_post"] = column(f["ffn_pre_g"][0]), column(f["ffn_post_g"][0])
    t["nw2"] = column(f["norm_w_2"])
    cw = np.concatenate([f["ssd_conv_w"][0], f["ssd_conv_b"]], 0).reshape(5, 24, P)
    order = [b for g in range(GROUPS) for b in (16 + g, 20 + g, 4 * g, 4 * g + 1, 4 * g + 2, 4 * g + 3)]
    t["conv"] = cw[:, order].transpose(2, 1, 0).reshape(P, 120)
    t["d_skip"] = column(np.repeat(f["ssd_d"][0], HP))
    t["ssd_g"] = column(f["ssd_norm_g"][0])
    t["sc_w"] = f["sc_conv_w"][0].reshape(3, DB, P).transpose(2, 1, 0).reshape(P, 3 * DB)
    fw = np.concatenate([f["ffn_conv_w"][0], f["ffn_conv_b"]], 0).reshape(4, 2, FF_PAIRS, P)
    t["ffn_w"] = fw.transpose(3, 2, 1, 0).reshape(P, 8 * FF_PAIRS)
    qk = [f[n].reshape(CFG, 4, P) for n in ("q_norm_w_2", "k_norm_w_2")]
    t["qk_w"] = np.stack(qk).transpose(3, 2, 0, 1).reshape(P, 24)
    for name, key in (("dt_bias", "ssd_dt_bias"), ("a_log", "ssd_a_log")):
        t[name] = np.concatenate([f[key][0], zero(P - SSD_HEADS, np.float32)])[:, None]
    table = np.concatenate([t[n] for n, _ in _widths], 1)
    assert table.shape == (P, NCOL)

    tok = np.arange(S).reshape(P, NT).T.reshape(-1)
    angle = 2 * np.pi * (np.outer(tok, tok) % S) / S
    dft = np.stack([np.cos(angle), np.sin(angle)]).reshape(2, NT, P, S).transpose(2, 0, 1, 3)
    ch = 2 * np.pi * (np.outer(np.arange(HP), np.arange(HP)) % HP) / HP
    scale = 1 / np.sqrt(S * HP)
    dft_head = np.stack([np.kron(np.eye(2), m) for m in (np.cos(ch) * scale, -np.sin(ch) * scale)], 1)
    i1 = np.arange(P)
    dist = np.full((P, NT, 6 * P), MASKED)
    near = np.abs(i1[:, None] - i1[None])
    for r in range(NT):
        far = np.abs((4 * i1 + r)[:, None] - tok[None])
        dist[:, r, :S] = np.where(far <= 64, -far, MASKED)
        dist[:, r, S:S + P] = np.where(near <= 64, -4.0 * near, MASKED)
        dist[:, r, S + P:] = np.where(near % 4 == 0, -4.0 * near, MASKED)
    wfo = zero((P, 4, P), np.float32)
    wfo[:HP, :, :HP] = f["w_fourier_2"][0::2].transpose(1, 0, 2)
    wfo[HP:, :, HP:] = f["w_fourier_2"][1::2].transpose(1, 0, 2)
    dist *= 0.5
    return {
        "stream": stream,
        "ada": f["ada_w"][0].reshape(8, P, 6, D).transpose(2, 0, 1, 3).reshape(48, P, D),
        "table": table,
        "x": f["x"][0].reshape(NT, P, D).transpose(1, 0, 2),
        "dft": dft.astype(np.float32),
        "dft_head": dft_head.astype(np.float32),
        "dist": dist.reshape(P, -1).astype(np.float32),
        "w_fourier": wfo,
    }


def kernel(**inputs):
    import concourse.bacc as bacc
    from concourse.bass_utils import run_bass_kernel_spmd

    arrays = {k: np.ascontiguousarray(v) for k, v in lay_out(inputs).items()}
    nc = bacc.Bacc("TRN2", target_bir_lowering=False, num_devices=1)
    a = {k: nc.dram_tensor(k, v.shape, F32, kind="ExternalInput").ap() for k, v in arrays.items()}
    a["out"] = nc.dram_tensor("out", (S, D), F32, kind="ExternalOutput").ap()
    build(nc, a)
    r = run_bass_kernel_spmd(nc, [arrays], core_ids=[0])
    return r.results[0]["out"].reshape(1, S, D)
```

```python
from contextlib import ExitStack

import numpy as np

import concourse.bass as bass
from concourse import mybir

ALU = mybir.AluOpType
ACT = mybir.ActivationFunctionType
AX = mybir.AxisListType
F32 = mybir.dt.float32
F32R = mybir.dt.float32r

P = 128
S = 512
NT = S // P
D = 1024
DB = D // P
KT = 8
UW = KT * P
EPS = 1e-6

SSD_HEADS, HEADS_G, GROUPS, HP, NSTATE = 32, 8, 4, 64, 128
FF_PAIRS = 2816 // P
CFG = 3
MASKED = -1e33

U_GRP = 1
N_GRP = 20
U_MIX = U_GRP + GROUPS * N_GRP
U_WO = U_MIX + 3 * DB
U_UP = U_WO + DB
U_DOWN = U_UP + 2 * FF_PAIRS
N_DOWN = 3
U_ATT = U_DOWN + N_DOWN * DB
N_ATT = 12
U_OUT = U_ATT + 4 * N_ATT
U_LAST = U_OUT + DB
UNITS = U_LAST + 1

R_GRP = 1
R_MIX = R_GRP + GROUPS * 24
R_WO = R_MIX + 3 * DB
R_UP = R_WO + DB
R_DOWN = R_UP + 2 * FF_PAIRS
R_ATT = R_DOWN + DB

E_GRP = 1
E_MIX = E_GRP + GROUPS * 16
E_WO = E_MIX + 3 * DB
E_UP = E_WO + DB
E_DOWN = E_UP + 2 * FF_PAIRS
E_ATT = E_DOWN + DB
E_OUT = E_ATT + 4 * N_ATT

OUT_TILES = (0, 1, 2, 4, 5, 6, 3)

_widths = [("ident", P), ("causal", P), ("head_ones", P), ("c", DB), ("ada_b", 48), ("g_pre", DB),
           ("g_post", DB), ("f_pre", DB), ("f_post", DB), ("nw2", DB), ("conv", 24 * 5), ("d_skip", 16),
           ("ssd_g", 16), ("sc_w", DB * 3), ("ffn_w", 2 * FF_PAIRS * 4), ("qk_w", 24), ("dt_bias", 1),
           ("a_log", SSD_HEADS)]
COL = {}
_at = 0
for _n, _w in _widths:
    COL[_n] = _at
    _at += _w
NCOL = _at


def build(nc, arrays):
    with ExitStack() as ctx:
        KB = 1024
        names = set()

        def at(name, offset, shape, dt=F32):
            assert name not in names
            names.add(name)
            n = 4
            for s in shape[1:]:
                n *= s
            assert BASE + offset + n <= 229344, (name, offset, n)
            return nc.alloc_sbuf_tensor_at(name, shape, dt, offset=BASE + offset)

        def area(offset, end):
            pos = [offset]

            def place(name, shape, dt=F32):
                t = at(name, pos[0], shape, dt)
                n = 4
                for s in shape[1:]:
                    n *= s
                pos[0] += (n + 31) // 32 * 32
                assert pos[0] <= end, (name, pos[0], end)
                return t
            place.end = lambda: pos[0]
            return place

        def sem(name):
            return ctx.enter_context(nc.semaphore(name))

        BASE = 16512
        END = 229344 - BASE
        keep = area(0, 70 * KB)
        tab = keep("tab", [P, NCOL])
        ones = keep("ones", [P, P])
        eps = keep("eps", [P, 2])
        mod = keep("mod", [P, 48])
        coef = keep("coef", [P, 4, DB])
        small = keep("small", [P, 32])
        raw = keep("raw", [P, 4, UW])
        w_hi = keep("w_hi", [P, 2, UW], F32R)
        w_lo = keep("w_lo", [P, 2, UW], F32R)
        H_AT = keep.end()
        h_hi = keep("h_hi", [P, DB, S], F32R)
        h_lo = keep("h_lo", [P, DB, S], F32R)
        FREE = keep.end()

        g = area(FREE, END)
        ssd_acc = g("ssd_acc", [P, DB, S])
        ysc = g("ysc", [P, DB, S])
        ada_raw = g("ada_raw", [P, 2, S])
        ada_acc = g("ada_acc", [P, D])
        ev = g("ev", [P, 4, S + 4])
        cv = g("cv", [P, 2, S])
        scp = g("scp", [P, S + 4])
        sct = g("sct", [P, S])
        BT = g("BT", [P, S])
        CT = g("CT", [P, S])
        dtN = g("dtN", [P, NT, SSD_HEADS])
        acsN = g("acsN", [P, NT, SSD_HEADS])
        g_end = g.end()
        g = area(g_end, END)
        xcT = g("xcT", [P, 4, S])
        yg = g("yg", [P, 4, S])
        zs = g("zs", [P, 4, S])
        abc = g("abc", [P, 2, HEADS_G, P])
        dec = g("dec", [P, 2, HEADS_G, P])
        ect = g("ect", [P, 2, HEADS_G, P])
        eld = g("eld", [P, NT, HEADS_G])
        xdt = g("xdt", [P, 2, S])
        xst = g("xst", [P, 2, S])
        scm = g("scm", [P, 2, P])
        bn = g("bn", [P, 2, P])
        hst = g("hst", [P, 2, S])
        y_at = g.end()
        g = area(y_at, END)
        y_hi = g("y_hi", [P, 4, S], F32R)
        y_lo = g("y_lo", [P, 4, S], F32R)
        dtw = at("dtw", g_end, [P, 8, NT * SSD_HEADS])
        dtr = at("dtr", g_end + 4 * KB, [SSD_HEADS, 2, S])
        g = area(g_end, END)
        x_tok = g("x_tok", [P, NT, D])
        ada0 = g("ada0", [P, 8, D])
        acc0 = g("acc0", [P, 2, D])
        xn = g("xn", [P, DB, S])
        hf = at("hf", FREE + 4 * KB, [P, 2, S])
        junk = at("junk", FREE, [P, D])

        g = area(FREE + 32 * KB, END)
        mix_hi = g("mix_hi", [P, DB, S], F32R)
        mix_lo = g("mix_lo", [P, DB, S], F32R)
        sc_hi = g("sc_hi", [P, DB, S], F32R)
        sc_lo = g("sc_lo", [P, DB, S], F32R)
        gts = g("gts", [P, 2, 3, S])
        mixf = g("mixf", [P, 2, S])
        x_tok2 = g("x_tok2", [P, NT, D])
        xT = at("xT", FREE, [P, DB, S])
        mo = at("mo", FREE + 16 * KB, [P, DB, S])
        g = area(FREE + 64 * KB, END)
        sq = g("sq", [P, 2, S])
        ssum = g("ssum", [P, S])
        diag = g("diag", [P, NT, P])
        rcol = g("rcol", [P, 2 * NT])
        hp = g("hp", [P, 2, S])

        g = area(FREE + 16 * KB, END)
        fe = g("fe", [P, 4, S + 4])
        fcv = g("fcv", [P, 4, S])
        af = g("af", [P, 2, S])
        act_hi = g("act_hi", [P, FF_PAIRS, S], F32R)
        act_lo = g("act_lo", [P, FF_PAIRS, S], F32R)
        fo = at("fo", FREE + 16 * KB, [P, DB, S])
        g = area(FREE + 126 * KB, END)
        sq6 = g("sq6", [P, 2, S])
        ssum6 = g("ssum6", [P, S])
        diag6 = g("diag6", [P, NT, P])
        rcol6 = g("rcol6", [P, 2 * NT])
        hp6 = g("hp6", [P, 2, S])
        xN = at("xN", FREE + 16 * KB, [P, NT, D])

        g = area(FREE, END)
        yo_hi = g("yo_hi", [P, DB, S], F32R)
        yo_lo = g("yo_lo", [P, DB, S], F32R)
        dft = g("dft", [P, 2, NT, S])
        bias = g("bias", [P, NT, 6 * P])
        wf = g("wf", [P, 4, 2 * P])
        qk = g("qk", [P, 2 * CFG, S])
        wfb = at("wfb", g.end(), [P, 4, P])
        dhd = at("dhd", g.end() + 2 * KB, [P, 2, P])
        vN = g("vN", [P, CFG, NT, P])
        sga = g("sga", [P, S])
        qk_next = g("qk_next", [P, 2 * CFG, S])
        vN_next = g("vN_next", [P, CFG, NT, P])
        sga_next = g("sga_next", [P, S])
        qsq = g("qsq", [P, S])
        qrt = g("qrt", [P, 3, S])
        vT = g("vT", [P, S])
        ufT = g("ufT", [P, S])
        sgf = g("sgf", [P, S])
        fv = g("fv", [P, NT, 2 * P])
        pr = g("pr", [P, 6 * P])
        yf = g("yf", [P, S])
        ya = g("ya", [P, S])
        stat = g("stat", [P, 4])
        pt = g("pt", [P, 6 * P])
        x_res = at("x_res", H_AT, [P, NT, D])

        ps = ctx.enter_context(nc.psum_tensor("ps", [P, 8, S], F32))
        acs_dram = nc.dram_tensor("acs_dram", (SSD_HEADS, S), F32, kind="Internal").ap()
        x2_dram = nc.dram_tensor("x2_dram", (P, NT, D), F32, kind="Internal").ap()

        raw_landed = [sem(f"raw_landed{i}") for i in range(4)]
        split_hi = sem("split_hi")
        split_done = sem("split_done")
        units_done = sem("units_done")
        half_done = sem("half_done")
        evacuated = sem("evacuated")
        tab_in = sem("tab_in")
        x_in = sem("x_in")
        ada0_in = [sem(f"ada0_in{i}") for i in range(8)]
        setup = sem("setup")
        acc_cleared = sem("acc_cleared")
        cact_ready = sem("cact_ready")
        row_stats = sem("row_stats")
        row_scaled = sem("row_scaled")
        ada0_steps = sem("ada0_steps")
        mod0_sums = sem("mod0_sums")
        mod0_ready = sem("mod0_ready")
        x_turned = sem("x_turned")
        xn_ready = sem("xn_ready")
        hf_ready = sem("hf_ready")
        h_hi_ready = sem("h_hi_ready")
        h_lo_ready = sem("h_lo_ready")
        dt_act = sem("dt_act")
        dt_steps = sem("dt_steps")
        acs_stored = sem("acs_stored")
        dt_turned = sem("dt_turned")
        dt_tokens = sem("dt_tokens")
        ada_in = [sem(f"ada_in{i}") for i in range(2)]
        ada_steps = sem("ada_steps")
        mod_sums = sem("mod_sums")
        mod_ready = sem("mod_ready")
        conv_taps = sem("conv_taps")
        conv_out = sem("conv_out")
        skip_ready = sem("skip_ready")
        abc_in = [sem(f"abc_in{i}") for i in range(2)]
        dec_args = sem("dec_args")
        decays = sem("decays")
        chunk_inputs = sem("chunk_inputs")
        chunk_steps = sem("chunk_steps")
        s_done = sem("s_done")
        y_done = sem("y_done")
        state_steps = sem("state_steps")
        gate_steps = sem("gate_steps")
        y_squared = sem("y_squared")
        group_sum = sem("group_sum")
        group_root = sem("group_root")
        y_hi_ready = sem("y_hi_ready")
        sc_steps = sem("sc_steps")
        acc_steps = sem("acc_steps")
        coef_ready = sem("coef_ready")
        sc_hi_ready = sem("sc_hi_ready")
        sc_lo_ready = sem("sc_lo_ready")
        mix_steps = sem("mix_steps")
        mix_hi_ready = sem("mix_hi_ready")
        x2_in = sem("x2_in")
        xt_turned = sem("xt_turned")
        xt_ready = sem("xt_ready")

        def norm_sems(k, *more):
            names = ("summed", "total", "root", "inverse", "diag", "spread", "scaled") + more
            return {n: sem(f"n{k}_{n}") for n in names}
        n1a, n2a = (norm_sems(k, "added") for k in ("1a", "2a"))
        n1b, n2b = (norm_sems(k, "squared", "hi", "lo") for k in ("1b", "2b"))
        norms = (n1a, n1b, n2a, n2b)
        x2_turned = sem("x2_turned")
        x2_out = sem("x2_out")
        ffn_taps = sem("ffn_taps")
        ffn_silu = sem("ffn_silu")
        ffn_steps = sem("ffn_steps")
        act_hi_ready = sem("act_hi_ready")
        x2_stored = sem("x2_stored")
        att_in = sem("att_in")
        wf_sums = sem("wf_sums")
        wf_ready = sem("wf_ready")
        bias_scaled = sem("bias_scaled")
        fv_done = sem("fv_done")
        fv_ready = sem("fv_ready")
        ft_done = sem("ft_done")
        yf_steps = sem("yf_steps")
        yf_hi_ready = sem("yf_hi_ready")
        ya_steps = sem("ya_steps")
        ya_hi_ready = sem("ya_hi_ready")
        qk_total = sem("qk_total")
        qk_root = sem("qk_root")
        qk_steps = sem("qk_steps")
        qk_moved = sem("qk_moved")
        v_turned = sem("v_turned")
        v_ready = sem("v_ready")
        v_moved = sem("v_moved")
        gate_moved = sem("gate_moved")
        scored = sem("scored")
        biased = sem("biased")
        exped = sem("exped")
        normed = sem("normed")
        p_turned = sem("p_turned")
        pt_ready = sem("pt_ready")
        attended = sem("attended")
        x_res_in = [sem(f"x_res_in{i}") for i in range(2)]
        out_turned = sem("out_turned")
        out_added = sem("out_added")
        out_sums = sem("out_sums")
        out_steps = sem("out_steps")
        out_stored = sem("out_stored")

        start_at_one = [acc_steps, group_root, chunk_steps, state_steps, mod_ready, gate_steps, biased, pt_ready, decays, sc_steps, y_done, mix_steps, attended, ada_steps, units_done, mod_sums, p_turned, ya_steps] + [n["summed"] for n in norms]

        ident = tab[:, COL["ident"]:COL["ident"] + P]
        causal = tab[:, COL["causal"]:COL["causal"] + P]
        head_ones = tab[:, COL["head_ones"]:COL["head_ones"] + P]

        def col(name, i, n=1):
            return tab[:, bass.ds(COL[name] + i, n)]

        def blocks(t, i):
            return t[:, bass.ds(i, 1), :].rearrange("p o s -> p (o s)")

        def per_token(t, chunk, g):
            return t[:, chunk, bass.ds(HEADS_G * g, HEADS_G)].unsqueeze(2).broadcast_to([P, HEADS_G, HP])

        def by_head(t):
            return t.rearrange("p (h c) -> p h c", h=HEADS_G)

        def permuted(t):
            return t.rearrange("p (r i) -> p i r", r=NT)

        def natural(t):
            return t.rearrange("p (i r) -> p i r", r=NT)

        block = ctx.enter_context(nc.Block())

        @block.sync
        def _(sp):
            for signal in start_at_one:
                sp.sem_inc(signal, 1)
            sp.sem_inc(bias_scaled, NT)
            sp.dma_start(tab[:], arrays["table"]).then_inc(tab_in, 16)
            sp.dma_start(x_tok[:], arrays["x"]).then_inc(x_in, 16)
            for k in range(8):
                sp.dma_start(ada0[:, k], arrays["ada"][k]).then_inc(ada0_in[k], 16)
            for k in range(8):
                sp.wait_ge(ada0_steps, k + 1)
                sp.dma_start(ada0[:, k], arrays["ada"][8 + k]).then_inc(ada0_in[k], 16)
            for u in range(4):
                sp.dma_start(raw[:, u], arrays["stream"][u]).then_inc(raw_landed[u], 16)

            def stream(u, slot):
                sp.wait_ge(split_done, u - 3)
                src = arrays["stream"][bass.ds(u, 1)].rearrange("u p w -> (u p) w")
                sp.dma_start(raw[:, slot], src).then_inc(raw_landed[slot], 16)

            ADA_BEHIND = (0, 1, 2, 3, 4, 5, 9, 11)
            with sp.Fori(0, GROUPS) as g:
                for s in range(N_GRP):
                    stream(4 + N_GRP * g + s, s % 4)
                    if s in ADA_BEHIND:
                        k = ADA_BEHIND.index(s)
                        for hv in range(2):
                            sp.wait_ge(ada_steps, 1 + 16 * g + max(2 * k + hv - 1, 0))
                            src = arrays["ada"][bass.ds(16 + 8 * g + k, 1)].rearrange("m p w -> (m p) w")
                            sp.dma_start(ada_raw[:, hv], src[:, hv * S:(hv + 1) * S]).then_inc(ada_in[hv], 16)
            done = 4 + GROUPS * N_GRP
            loops = (UNITS - done) // 4
            with sp.Fori(0, loops) as i:
                for s in range(4):
                    stream(done + 4 * i + s, s)
            for u in range(done + 4 * loops, UNITS):
                stream(u, u % 4)

        @block.gpsimd
        def _(pool):
            def split(u, raw_slot, slot, landed):
                pool.wait_ge(raw_landed[raw_slot], landed)
                nc.gpsimd.tensor_tensor(w_hi[:, slot], raw[:, raw_slot],
                                        ones[:, 0:1].broadcast_to([P, UW]), ALU.mult).then_inc(split_hi, 1)
                pool.wait_ge(split_hi, u + 1)
                nc.gpsimd.tensor_tensor(w_lo[:, slot], raw[:, raw_slot], w_hi[:, slot].bitcast(F32),
                                        ALU.subtract).then_inc(split_done, 1)

            pool.wait_ge(setup, 1)
            split(0, 0, 0, 16)
            pool.wait_ge(row_stats, 4)
            pool.wait_ge(h_lo_ready, DB)
            nc.gpsimd.memset(ssd_acc[:], 0.0).then_inc(acc_cleared, 1)
            with pool.Fori(0, (UNITS - 1) // 4) as i:
                for s in range(4):
                    u = 1 + 4 * i + s
                    pool.wait_ge(units_done, 1 + 4 * i + s)
                    split(u, (1 + s) % 4, (1 + s) % 2, 16 * i + (16 if s < 3 else 32))
            for u in range(1 + (UNITS - 1) // 4 * 4, UNITS):
                pool.wait_ge(units_done, 1 + u - 1)
                split(u, u % 4, u % 2, 16 * (u // 4 + 1))

        @block.tensor
        def _(pe):
            def unit(u, slot, bank, free=None, x_hi=h_hi, x_lo=h_lo, k0=0, tiles=KT, at_k=0, start=True,
                     stop=True, last=True, signal=None, each=None):
                if at_k == 0:
                    pe.wait_ge(split_done, u + 1)
                if free is not None:
                    pe.wait_ge(*free)
                for k in range(tiles):
                    if each is not None:
                        pe.wait_ge(each[0], each[1] + each[2] * k)
                    w = slice((at_k + k) * P, (at_k + k + 1) * P)
                    nc.tensor.matmul(ps[:, bank], w_hi[:, slot, w], x_hi[:, k0 + k],
                                     start=start and k == 0, stop=False)
                    nc.tensor.matmul(ps[:, bank], w_hi[:, slot, w], x_lo[:, k0 + k], start=False, stop=False)
                    mm = nc.tensor.matmul(ps[:, bank], w_lo[:, slot, w], x_hi[:, k0 + k],
                                          start=False, stop=stop and k == tiles - 1)
                if signal is not None:
                    mm.then_inc(signal, 1)
                elif last:
                    mm.then_inc(units_done, 1)

            def tiles(u, slot, bank, x_hi, x_lo, at_, of, ready=False, free=None, start=False, signal=None):
                if ready:
                    pe.wait_ge(split_done, u + 1)
                    pe.wait_ge(*free)
                for m, (t, k) in enumerate(zip(at_, of)):
                    w = slice(t * P, (t + 1) * P)
                    nc.tensor.matmul(ps[:, bank], w_hi[:, slot, w], x_hi[:, k], start=start and m == 0, stop=False)
                    nc.tensor.matmul(ps[:, bank], w_hi[:, slot, w], x_lo[:, k], start=False, stop=False)
                    mm = nc.tensor.matmul(ps[:, bank], w_lo[:, slot, w], x_hi[:, k], start=False,
                                          stop=signal is not None and m == len(of) - 1)
                if signal is not None:
                    mm.then_inc(signal, 1)

            def opening(units, results, x_hi, x_lo, sem_, first, step, free0, free1):
                for n, free in enumerate((free0, free1)):
                    pe.wait_ge(split_done, units[n] + 1)
                    pe.wait_ge(*free)
                for k in range(KT):
                    pe.wait_ge(sem_, first + step * k)
                    w = slice(k * P, (k + 1) * P)
                    for n in range(2):
                        bank, slot = results[n] % 2, units[n] % 2
                        nc.tensor.matmul(ps[:, bank], w_hi[:, slot, w], x_hi[:, k], start=(k == 0), stop=False,
                                         skip_group_check=True)
                        nc.tensor.matmul(ps[:, bank], w_hi[:, slot, w], x_lo[:, k], start=False, stop=False,
                                         skip_group_check=True)
                        mm = nc.tensor.matmul(ps[:, bank], w_lo[:, slot, w], x_hi[:, k], start=False,
                                              stop=(k == KT - 1), skip_group_check=True)
                        if k == KT - 1:
                            mm.then_inc(units_done, 1)

            pe.wait_ge(tab_in, 16)
            pe.wait_ge(setup, 1)

            def mod_sum(m):
                pe.wait_ge(ada0_steps, 8 * (m + 1))
                for b in range(DB):
                    mm = nc.tensor.matmul(ps[:, 2, 8 * m + b:8 * m + b + 1], acc0[:, m, b * P:(b + 1) * P],
                                          ones[:, 0:1], start=True, stop=True)
                mm.then_inc(mod0_sums, 1)

            mod_sum(0)
            pe.wait_ge(row_scaled, 4)
            for b in range(DB):
                if b >= 4:
                    pe.wait_ge(xn_ready, b - 3)
                for t in range(NT):
                    mm = nc.tensor.transpose(ps[:, 4 + b % 4, t * P:(t + 1) * P], x_tok[:, t, b * P:(b + 1) * P],
                                             ident)
                mm.then_inc(x_turned, 1)
            mod_sum(1)

            unit(0, 0, 0, each=(h_lo_ready, 1, 1))
            pe.wait_ge(evacuated, 1)
            pe.wait_ge(xn_ready, DB)
            for c in range(NT):
                mm = nc.tensor.transpose(ps[:, 5, c * SSD_HEADS:(c + 1) * SSD_HEADS], dtr[:, 0, c * P:(c + 1) * P],
                                         ident[0:SSD_HEADS, 0:SSD_HEADS])
            mm.then_inc(dt_turned, 1)
            pe.wait_ge(dt_steps, 15)
            nc.tensor.matmul(ps[:, 5, P:2 * P], causal, dtw[:, 0], start=True, stop=True)
            for c in range(NT):
                mm = nc.tensor.matmul(ps[0:SSD_HEADS, 3, c * P:(c + 1) * P],
                                      dtw[:, 0, c * SSD_HEADS:(c + 1) * SSD_HEADS], causal, start=True, stop=True)
            mm.then_inc(dt_turned, 1)

            with pe.Fori(0, GROUPS) as g:
                def u_(j):
                    return U_GRP + N_GRP * g + j

                def project(j):
                    if j < 2:
                        free = (acc_steps, 1 + 8 * g)
                    else:
                        free = (evacuated, E_GRP + 16 * g + j - 1)
                    unit(u_(j), (1 + j) % 2, (R_GRP + j) % 2, free)

                def turn(c):
                    pe.wait_ge(chunk_steps, 1 + 24 * g + (6 * (c - 1) + 3 if c else 0))
                    if c == 0:
                        pe.wait_ge(dt_tokens, 1)
                        pe.wait_ge(group_root, 1 + g)
                    cols = slice(c * P, (c + 1) * P)
                    pe.wait_ge(conv_out, 6 * g + 6)
                    nc.tensor.matmul(ps[:, 5, 0:P], BT[:, cols], CT[:, cols], start=True, stop=True)
                    nc.tensor.transpose(ps[:, 5, P:2 * P], BT[:, cols], ident)
                    for b in range(4):
                        mm = nc.tensor.transpose(ps[:, 4, b * P:(b + 1) * P], xcT[:, b, cols], ident)
                    mm.then_inc(chunk_inputs, 1)

                def state(c):
                    pe.wait_ge(chunk_steps, 1 + 24 * g + 6 * c + 6)
                    pe.wait_ge(state_steps, 1 + 5 * g + (0, 1, 3)[c])
                    if c == 0:
                        pe.wait_ge(mod_ready, 1 + g)
                    nc.tensor.matmul(ps[:, 7], bn[:, c % 2], xst[:, c % 2], start=True, stop=True).then_inc(s_done, 1)

                def outputs(c):
                    pe.wait_ge(chunk_steps, 1 + 24 * g + 6 * c + 6)
                    pe.wait_ge(gate_steps, 1 + 15 * g + max(c - 1, 0))
                    if c:
                        pe.wait_ge(state_steps, 1 + 5 * g + (1, 3, 5)[c - 1])
                    for h in range(HEADS_G):
                        rows, hc = slice(64 * (h % 2), 64 * (h % 2) + 64), slice(h * HP, (h + 1) * HP)
                        out = ps[rows, 6 - 4 * (c % 2), (h // 2) * P:(h // 2 + 1) * P]
                        mm = nc.tensor.matmul(out, xdt[:, c % 2, hc], dec[:, c % 2, h], start=(h < 2),
                                              stop=(c == 0), skip_group_check=True)
                        if c:
                            mm = nc.tensor.matmul(out, hst[:, c % 2, hc], ect[:, c % 2, h], start=False,
                                                  stop=True, skip_group_check=True)
                    mm.then_inc(y_done, 1)

                for j in range(6):
                    project(j)
                project(6)
                turn(0)
                project(7)
                turn(1)
                project(8)
                state(0)
                outputs(0)
                turn(2)
                project(9)
                state(1)
                outputs(1)
                turn(3)
                project(10)
                state(2)
                outputs(2)
                project(11)
                outputs(3)
                project(12)
                pe.wait_ge(ada_steps, 1 + 16 * g + 16)
                pe.wait_ge(state_steps, 1 + 5 * g + 5)
                for b in range(DB):
                    mm = nc.tensor.matmul(ps[:, 7, b:b + 1], ada_acc[:, b * P:(b + 1) * P], ones[:, 0:1],
                                          start=True, stop=True)
                mm.then_inc(mod_sums, 1)
                project(13)
                pe.wait_ge(gate_steps, 1 + 15 * g + 6)
                nc.tensor.matmul(ps[:, 4], ones[:], sct[:], start=True, stop=True).then_inc(group_sum, 1)
                project(14)
                project(15)
                pe.wait_ge(gate_steps, 1 + 15 * g + 15)
                for n in range(DB):
                    if n < 2:
                        free = (evacuated, E_GRP + 16 * g + 15 + n)
                    else:
                        free = (acc_steps, 1 + 8 * g + n - 1)
                    unit(u_(16 + n // 2), (1 + n // 2) % 2, (R_GRP + 16 + n) % 2, free, y_hi, y_lo,
                         tiles=4, at_k=4 * (n % 2), signal=half_done if n % 2 == 0 else units_done)

            pe.wait_ge(acc_steps, 1 + 8 * GROUPS)
            with pe.Fori(0, 2) as i:
                for j in range(12):
                    if j == 2:
                        pe.wait_ge(sc_lo_ready, 2)
                    sc = j % 3 == 2
                    unit(U_MIX + 12 * i + j, (U_MIX + j) % 2, (R_MIX + j) % 2, (evacuated, E_MIX + 12 * i + j - 1),
                         sc_hi if sc else h_hi, sc_lo if sc else h_lo)

            unit(U_WO, U_WO % 2, R_WO % 2, (evacuated, E_WO - 1), mix_hi, mix_lo,
                 each=(mix_steps, 1 + 4, 4))
            unit(U_WO + 1, (U_WO + 1) % 2, (R_WO + 1) % 2, (evacuated, E_WO), mix_hi, mix_lo)
            with pe.Fori(1, DB // 2) as i:
                for j in range(2):
                    unit(U_WO + 2 * i + j, (U_WO + j) % 2, (R_WO + j) % 2, (evacuated, E_WO + 2 * i + j - 1),
                         mix_hi, mix_lo)

            def norm_total(src, first, last):
                for t in range(NT):
                    mm = nc.tensor.matmul(ps[:, 4, t:t + 1], src[:, t * P:(t + 1) * P], ones[:, 0:1],
                                          start=first and t == 0, stop=last, skip_group_check=True)
                return mm

            def norm_spread(n, dg):
                pe.wait_ge(n["diag"], 1)
                nc.tensor.matmul(ps[:, 5], ones[:], dg[:].rearrange("p t c -> p (t c)"), start=True,
                                 stop=True).then_inc(n["spread"], 1)

            def norm_branch(n, total, dg):
                pe.wait_ge(n["summed"], 1 + DB)
                norm_total(total, True, True).then_inc(n["total"], 1)
                norm_spread(n, dg)

            def norm_residual(n, before, squares, dg):
                for b in range(0, DB, 2):
                    pe.wait_ge(n["summed"], 1 + b // 2 + 1)
                    if b == 0:
                        pe.wait_ge(before["root"], 1)
                    norm_total(squares[:, b], b == 0, b == DB - 2).then_inc(n["total"], 1)
                pe.wait_ge(before["added"], DB)
                norm_spread(n, dg)

            pe.wait_ge(x2_in, 16)
            for b in range(DB):
                if b == 2:
                    norm_branch(n1a, ssum, diag)
                if b >= 2:
                    pe.wait_ge(xt_ready, b - 1)
                for t in range(NT):
                    mm = nc.tensor.transpose(ps[:, 2 + b % 2, t * P:(t + 1) * P], x_tok2[:, t, b * P:(b + 1) * P],
                                             ident)
                mm.then_inc(xt_turned, 1)
            norm_residual(n1b, n1a, mo, diag)
            opening((U_UP, U_UP + 1), (R_UP, R_UP + 1), h_hi, h_lo, n1b["lo"], 1, 1,
                    (evacuated, E_UP - 1), (evacuated, E_UP))
            for j in (2, 3):
                unit(U_UP + j, (U_UP + j) % 2, (R_UP + j) % 2, (evacuated, E_UP + j - 1))
            with pe.Fori(1, FF_PAIRS // 2) as i:
                for j in range(4):
                    unit(U_UP + 4 * i + j, (U_UP + j) % 2, (R_UP + j) % 2, (evacuated, E_UP + 4 * i + j - 1))
            pe.wait_ge(ffn_steps, 4 + 2 * (FF_PAIRS - 2))
            with pe.Fori(0, 2) as i:
                for n in range(4):
                    bank = (R_DOWN + n) % 2
                    u = U_DOWN + 12 * i + 3 * n
                    for j in range(N_DOWN):
                        if n == 0 and j == 2:
                            pe.wait_ge(ffn_steps, 4 + 2 * FF_PAIRS)
                        unit(u + j, (U_DOWN + 3 * n + j) % 2, bank,
                             (evacuated, E_DOWN + 4 * i + n - 1) if j == 0 else None, act_hi, act_lo, k0=8 * j,
                             tiles=(8, 8, 6)[j], start=(j == 0), stop=(j == 2))
            norm_branch(n2a, ssum6, diag6)
            norm_residual(n2b, n2a, fo, diag6)

            def beside(j):
                if j == 1:
                    pe.wait_ge(att_in, 16 * 4)
                    for b in range(4):
                        for m in range(2):
                            out = ps[:, 2 + b // 2, (b % 2) * 256 + m * P:(b % 2) * 256 + (m + 1) * P]
                            mm = nc.tensor.matmul(out, dhd[:, m], wfb[:, b], start=True, stop=True)
                    mm.then_inc(wf_sums, 1)
                if 2 <= j < 2 + DB:
                    b = j - 2
                    if b >= 2:
                        pe.wait_ge(x2_out, b - 1)
                    else:
                        pe.wait_ge(n2b["lo"], DB)
                    for r in range(NT):
                        mm = nc.tensor.transpose(ps[:, 4 + b % 2, r * P:(r + 1) * P],
                                                 xT[:, b].rearrange("p (i r) -> p i r", r=NT)[:, :, r], ident)
                    mm.then_inc(x2_turned, 1)

            def half(p, x):
                j = x // 2
                u = U_ATT + N_ATT * p + j
                if x % 2 == 0:
                    tiles(u, (U_ATT + j) % 2, (R_ATT + j) % 2, h_hi, h_lo, range(0, 4), range(0, 4),
                          ready=True, free=(evacuated, E_ATT + N_ATT * p + j - 1), start=True)
                    return
                tiles(u, (U_ATT + j) % 2, (R_ATT + j) % 2, h_hi, h_lo, range(4, 8), range(4, 8), signal=units_done)
                follow(p, j)

            def follow(p, j):
                if 1 <= j <= 6:
                    m = j - 1
                    pe.wait_ge(evacuated, E_ATT + N_ATT * p + m + 1)
                    if m:
                        pe.wait_ge(qk_root, 6 * p + m)
                    elif not (isinstance(p, int) and p == 0):
                        pe.wait_ge(yf_steps, 2 * p - 1)
                    nc.tensor.matmul(ps[:, 7], head_ones, qsq[:], start=True, stop=True).then_inc(qk_total, 1)
                if 7 <= j <= 9:
                    c = j - 7
                    pe.wait_ge(evacuated, E_ATT + N_ATT * p + 6 + c + 1)
                    if c:
                        pe.wait_ge(v_ready, 3 * p + c)
                    else:
                        pe.wait_ge(qk_root, 6 * p + 6)
                    for t in range(NT):
                        mm = nc.tensor.transpose(ps[:, 7, t * P:(t + 1) * P], vT[:, t * P:(t + 1) * P], ident)
                    mm.then_inc(v_turned, 1)
                if j >= 10:
                    m = j - 10
                    if m:
                        pe.wait_ge(fv_ready, 2 * p + 1)
                    else:
                        pe.wait_ge(v_ready, 3 * p + 3)
                        pe.wait_ge(wf_ready, 2)
                        pe.wait_ge(evacuated, E_ATT + N_ATT * p + 10)
                    for t in range(2 * m, 2 * m + 2):
                        mm = nc.tensor.matmul(ps[:, 7, (t % 2) * 256:(t % 2) * 256 + 256], ufT[:, t * P:(t + 1) * P],
                                              blocks(wf, p), start=True, stop=True)
                    mm.then_inc(fv_done, 1)

            def token_transform(a):
                pe.wait_ge(fv_ready, 2 * a + 2)
                for t in range(NT):
                    nc.tensor.matmul(ps[:, 7], fv[:, t, 0:P], dft[:, 0, t], start=(t == 0), stop=False)
                    mm = nc.tensor.matmul(ps[:, 7], fv[:, t, P:2 * P], dft[:, 1, t], start=False,
                                          stop=(t == NT - 1))
                mm.then_inc(ft_done, 1)

            def scores(a, n):
                rows, r = slice(64 * (n // 4), 64 * (n // 4) + 64), n % 4
                q = slice(r * P, (r + 1) * P)
                if n == 0:
                    pe.wait_ge(qk_moved, a + 1)
                pe.wait_ge(biased, 1 + 8 * a + n)
                nc.tensor.matmul(ps[:, 2], qk[rows, 0, q], qk[rows, CFG], start=True, stop=True)
                nc.tensor.matmul(ps[:, 3, 0:P], qk[rows, 1, q], qk[rows, CFG + 1, q], start=True, stop=True)
                nc.tensor.matmul(ps[:, 3, P:2 * P], qk[rows, 2, q], qk[rows, CFG + 2, q], start=True,
                                 stop=True).then_inc(scored, 1)

            def turn_p(a, n):
                pe.wait_ge(normed, 16 * a + 2 * n + 2)
                pe.wait_ge(pt_ready, 1 + 8 * a + n)
                for m in range(6):
                    mm = nc.tensor.transpose(ps[:, 4 + m // 4, (m % 4) * P:(m % 4 + 1) * P],
                                             pr[:, m * P:(m + 1) * P], ident)
                mm.then_inc(p_turned, 1)

            def attend(a, n):
                rows, r = slice(64 * (n // 4), 64 * (n // 4) + 64), n % 4
                pe.wait_ge(pt_ready, 1 + 8 * a + n + 1)
                if n == 0:
                    pe.wait_ge(v_moved, a + 1)
                    pe.wait_ge(ya_steps, 1 + 2 * a)
                for m in range(6):
                    cfg, tile = (0, m) if m < 4 else (m - 3, r)
                    mm = nc.tensor.matmul(ps[rows, 6, r * P:(r + 1) * P], vN[:, cfg, tile, rows],
                                          pt[:, m * P:(m + 1) * P], start=(r == 0 and m == 0),
                                          stop=(m == 5), skip_group_check=True)
                mm.then_inc(attended, 1)

            opening((U_ATT, U_ATT + 1), (R_ATT, R_ATT + 1), h_hi, h_lo, n2b["lo"], 1, 1,
                    (evacuated, E_ATT - 1), (evacuated, E_ATT))
            follow(0, 1)
            for x in range(4, 2 * N_ATT):
                half(0, x)
                if x % 2:
                    beside(x // 2 - 1)
            with pe.Fori(0, 3) as a:
                for n in range(8):
                    scores(a, n)
                    half(a + 1, 3 * n)
                    half(a + 1, 3 * n + 1)
                    if n == 0:
                        token_transform(a)
                    turn_p(a, n)
                    half(a + 1, 3 * n + 2)
                    attend(a, n)

            def out_turn(n):
                pe.wait_ge(evacuated, E_OUT + n + 1)
                if n:
                    pe.wait_ge(out_added, n)
                else:
                    pe.wait_ge(yf_steps, 2 * 3 + 1)
                src = (ufT, sgf)[n % 2]
                for r in range(NT):
                    mm = nc.tensor.transpose(ps[:, 7, r * P:(r + 1) * P], src[:, r * P:(r + 1) * P], ident)
                mm.then_inc(out_turned, 1)

            for n in range(8):
                u, bank = U_OUT + n, (R_ATT + n) % 2
                scores(3, n)
                if n == 0:
                    token_transform(3)
                    pe.wait_ge(ya_steps, 1 + 2 * 3)
                tiles(u, u % 2, bank, yo_hi, yo_lo, range(0, 4), OUT_TILES[0:4], ready=True,
                      free=(evacuated, E_OUT + n - 1), start=True)
                if n:
                    out_turn(n - 1)
                turn_p(3, n)
                if n == 0:
                    pe.wait_ge(yf_steps, 2 * 4)
                tiles(u, u % 2, bank, yo_hi, yo_lo, range(4, 7), OUT_TILES[4:7], signal=units_done)
                attend(3, n)
            out_turn(7)
            pe.wait_ge(ya_steps, 1 + 2 * 4)
            pe.wait_ge(split_done, U_LAST + 1)
            pe.wait_ge(evacuated, E_OUT + 8)
            slot = U_LAST % 2
            for hv in range(2):
                w = slice(hv * S, (hv + 1) * S)
                for t in range(NT):
                    bank = (0, 1, 2, 3, 4, 5, 6, 7)[4 * hv + t]
                    out, q = ps[:, bank], slice(t * P, (t + 1) * P)
                    if bank == 7:
                        pe.wait_ge(out_added, DB)
                    nc.tensor.matmul(out, yo_hi[:, 7, q], w_hi[:, slot, w], start=True, stop=False)
                    nc.tensor.matmul(out, yo_hi[:, 7, q], w_lo[:, slot, w], start=False, stop=False)
                    nc.tensor.matmul(out, yo_lo[:, 7, q], w_hi[:, slot, w], start=False,
                                     stop=True).then_inc(out_sums, 1)

        @block.scalar
        def _(act):
            A = nc.scalar.activation

            act.wait_ge(tab_in, 16)
            A(small[:, 0:8], col("c", 0, DB), ACT.Silu).then_inc(cact_ready, 1)
            act.wait_ge(x_in, 16)
            for t in range(NT):
                if t:
                    act.wait_ge(row_stats, t)
                A(junk[:], x_tok[:, t], ACT.Square, accum_out=small[:, 8 + t:9 + t]).then_inc(row_stats, 1)
            act.wait_ge(row_stats, 4)
            act.wait_ge(setup, 3)
            A(small[:, 12:16], small[:, 8:12], ACT.Sqrt, bias=eps[:, 0:1], scale=1.0 / D).then_inc(row_stats, 1)
            for b in range(DB):
                act.wait_ge(x_turned, b + 1)
                A(xn[:, b], ps[:, 4 + b % 4], ACT.Copy).then_inc(xn_ready, 1)
            act.wait_ge(mod0_ready, 2)
            act.wait_ge(xn_ready, DB)
            for b in range(DB):
                A(h_hi[:, b], xn[:, b], ACT.Identity, bias=mod[:, b:b + 1],
                  scale=coef[:, 0, b:b + 1]).then_inc(h_hi_ready, 1)
            A(dtw[:, 7, 0:SSD_HEADS], col("a_log", 0, SSD_HEADS), ACT.Exp).then_inc(dt_act, 1)

            act.wait_ge(units_done, 1 + 1)
            A(dtr[:, 0], ps[0:SSD_HEADS, 0], ACT.Identity,
              bias=tab[0:SSD_HEADS, COL["dt_bias"]:COL["dt_bias"] + 1]).then_inc(evacuated, 1)
            act.wait_ge(dt_turned, 1)
            A(dtw[:, 1], ps[:, 5, 0:P], ACT.Abs).then_inc(dt_act, 1)
            act.wait_ge(dt_act, 2)
            A(dtw[:, 1], dtw[:, 1], ACT.Exp, scale=-1.0).then_inc(dt_act, 1)
            act.wait_ge(dt_turned, 2)
            A(dtr[:, 1], ps[0:SSD_HEADS, 3], ACT.Copy).then_inc(dt_act, 1)
            act.wait_ge(dt_act, 4)
            act.dma_start(acs_dram, dtr[:, 1]).then_inc(acs_stored, 16)
            act.wait_ge(acs_stored, 16)

            with act.Fori(0, GROUPS) as g:
                def load_abc(c):
                    act.wait_ge(decays, 1 + 4 * g + max(c - 1, 0))
                    src = acs_dram[bass.ds(HEADS_G * g, HEADS_G), c * P:(c + 1) * P]
                    act.dma_start(abc[:, c % 2], src.unsqueeze(0).broadcast_to([P, HEADS_G, P])
                                  ).then_inc(abc_in[c % 2], 16)

                def out_of(j, unit_no):
                    act.wait_ge(units_done, 1 + U_GRP + N_GRP * g + unit_no + 1)

                def conv_in(j):
                    out_of(j, j)
                    if j < 4:
                        act.wait_ge(sc_steps, 1 + 10 * g)
                    else:
                        act.wait_ge(conv_taps, 18 * g + 3 * (j - 4) + 3)
                    bank = ps[:, (R_GRP + j) % 2]
                    A(ev[:, j % 4, 3:3 + S], bank, ACT.Copy)
                    if j >= 2:
                        act.wait_ge(conv_out, 6 * g + j - 1)
                    A(cv[:, j % 2], bank, ACT.Identity, bias=col("conv", (6 * g + j) * 5 + 4),
                      scale=col("conv", (6 * g + j) * 5 + 3)).then_inc(evacuated, 1)

                def conv_silu(j):
                    act.wait_ge(conv_taps, 18 * g + 3 * j + 3)
                    dst = (BT[:], CT[:])[j] if j < 2 else xcT[:, j - 2]
                    A(dst, cv[:, j % 2], ACT.Silu).then_inc(conv_out, 1)
                    if j >= 2:
                        act.wait_ge(conv_out, 6 * g + j + 1)
                        A(yg[:, j - 2], xcT[:, j - 2], ACT.Identity,
                          scale=col("d_skip", 4 * g + j - 2)).then_inc(skip_ready, 1)

                def z(b):
                    out_of(6 + b, 6 + b)
                    A(zs[:, b], ps[:, (R_GRP + 6 + b) % 2], ACT.Silu).then_inc(evacuated, 1)

                def chunk(c):
                    if c < 3:
                        load_abc(c + 1)
                    act.wait_ge(abc_in[c % 2], 32 * g + 16 * (c // 2) + 16)
                    act.wait_ge(dt_tokens, 1)
                    act.wait_ge(y_done, 1 + 4 * g + max(c - 1, 0))
                    for h in range(HEADS_G):
                        ins = A(dec[:, c % 2, h], abc[:, c % 2, h], ACT.Relu,
                                bias=acsN[:, c, bass.ds(HEADS_G * g + h, 1)], scale=-1.0)
                    ins.then_inc(dec_args, 1)
                    act.wait_ge(dec_args, 4 * g + c + 1)
                    A(dec[:, c % 2], dec[:, c % 2], ACT.Exp, scale=-1.0)
                    A(eld[:, c], abc[:, c % 2, :, P - 1], ACT.Exp)
                    A(ect[:, c % 2], abc[:, c % 2], ACT.Exp).then_inc(decays, 1)

                def sc_in(e):
                    out_of(10 + e, 10 + e)
                    if e < 4:
                        act.wait_ge(conv_taps, 18 * g + 18)
                    else:
                        act.wait_ge(sc_steps, 1 + 10 * g + 1)
                    A(ev[:, (6 + e) % 4, 3:3 + S], ps[:, (R_GRP + 10 + e) % 2], ACT.Copy).then_inc(evacuated, 1)

                load_abc(0)
                act.wait_ge(gate_steps, 1 + 15 * g)
                conv_in(0)
                conv_in(1)
                for j in range(2, 6):
                    conv_silu(j - 2)
                    conv_in(j)
                    if j == 3:
                        chunk(0)
                conv_silu(4)
                conv_silu(5)
                z(0)
                chunk(1)
                z(1)
                z(2)
                chunk(2)
                z(3)
                chunk(3)
                sc_in(0)
                sc_in(1)
                sc_in(2)
                act.wait_ge(gate_steps, 1 + 15 * g + 5)
                A(xcT[:], yg[:], ACT.Square).then_inc(y_squared, 1)
                sc_in(3)
                act.wait_ge(group_sum, g + 1)
                A(sct[:], ps[:, 4], ACT.Sqrt, bias=eps[:, 0:1], scale=1.0 / S).then_inc(group_root, 1)
                sc_in(4)
                for b in range(4):
                    act.wait_ge(gate_steps, 1 + 15 * g + 8 + b)
                    A(y_hi[:, b], yg[:, b], ACT.Copy).then_inc(y_hi_ready, 1)
                sc_in(5)

            act.wait_ge(sc_steps, 1 + 10 * GROUPS)
            for q in range(2):
                A(sc_hi[:, 4 * q:4 * q + 4], ysc[:, 4 * q:4 * q + 4], ACT.Copy).then_inc(sc_hi_ready, 1)
            act.wait_ge(units_done, 1 + U_MIX)
            act.dma_start(x_tok2[:], arrays["x"]).then_inc(x2_in, 16)
            with act.Fori(0, 2) as i:
                def hi(j):
                    act.wait_ge(mix_steps, 1 + 16 * i + 4 * j + 3)
                    A(blocks(mix_hi, 4 * i + j), mixf[:, j % 2], ACT.Copy).then_inc(mix_hi_ready, 1)
                for j in range(4):
                    for m in range(3):
                        act.wait_ge(units_done, 1 + U_MIX + 12 * i + 3 * j + m + 1)
                        if m == 0 and j < 2:
                            act.wait_ge(mix_steps, 1 + 16 * i)
                        elif m == 0:
                            act.wait_ge(mix_steps, 1 + 16 * i + 4 * (j - 2) + 3)
                        A(gts[:, j % 2, m], ps[:, (R_MIX + 3 * j + m) % 2],
                          ACT.Sigmoid if m < 2 else ACT.Copy).then_inc(evacuated, 1)
                        if m == 0 and j:
                            hi(j - 1)
                hi(3)

            act.wait_ge(mix_steps, 1 + 32)
            act.wait_ge(coef_ready, 3)
            A(small[:, 24:25], eps[:, 0:1], ACT.Sqrt)
            with act.Fori(0, DB // 2) as i:
                for j in range(2):
                    act.wait_ge(units_done, 1 + U_WO + 2 * i + j + 1)
                    A(blocks(mo, 2 * i + j), ps[:, (R_WO + j) % 2], ACT.Copy, scale=coef[:, 1, bass.ds(2 * i + j, 1)])
                    act.wait_ge(n1a["summed"], 1 + 2 * i)
                    A(sq[:, j], ps[:, (R_WO + j) % 2], ACT.Square).then_inc(evacuated, 1)

            def root(n, count, dst):
                act.wait_ge(n["total"], count)
                A(dst[:, 0:NT], ps[:, 4, 0:NT], ACT.Sqrt, bias=eps[:, 0:1], scale=1.0 / D).then_inc(n["root"], 1)

            def residual_squares(n, before, branch):
                for b in range(DB):
                    act.wait_ge(before["added"], b + 1)
                    A(branch[:, b], xT[:, b], ACT.Square).then_inc(n["squared"], 1)

            for b in range(DB):
                if b == 2:
                    root(n1a, 1, rcol)
                act.wait_ge(xt_turned, b + 1)
                A(xT[:, b], ps[:, 2 + b % 2], ACT.Copy).then_inc(xt_ready, 1)
            residual_squares(n1b, n1a, mo)
            root(n1b, DB // 2, rcol)
            for b in range(DB):
                act.wait_ge(n1b["scaled"], b + 1)
                A(h_hi[:, b], hp[:, b % 2], ACT.Identity, bias=mod[:, 24 + b:25 + b]).then_inc(n1b["hi"], 1)

            with act.Fori(0, FF_PAIRS // 2) as i:
                def tap_in(j):
                    act.wait_ge(units_done, 1 + U_UP + 4 * i + j + 1)
                    act.wait_ge(ffn_taps, 8 * i + 2 * j + 2)
                    act.wait_ge(ffn_steps, 4 * i + 2 * (j // 2) + 1)
                    A(fe[:, j, 2:2 + S], ps[:, (R_UP + j) % 2], ACT.Copy)
                    A(fcv[:, j], ps[:, (R_UP + j) % 2], ACT.Identity, bias=col("ffn_w", 16 * i + 4 * j + 3),
                      scale=col("ffn_w", 16 * i + 4 * j + 2)).then_inc(evacuated, 1)

                def silu(p):
                    act.wait_ge(ffn_taps, 8 + 8 * i + 4 * p + 2)
                    A(fcv[:, 2 * p], fcv[:, 2 * p], ACT.Silu).then_inc(ffn_silu, 1)

                def hi(p):
                    act.wait_ge(ffn_steps, 4 + 4 * i + 2 * p + 1)
                    A(blocks(act_hi, 2 * i + p), af[:, p], ACT.Copy).then_inc(act_hi_ready, 1)

                tap_in(0)
                tap_in(1)
                silu(0)
                tap_in(2)
                hi(0)
                tap_in(3)
                silu(1)
                hi(1)

            act.wait_ge(act_hi_ready, FF_PAIRS)
            A(small[:, 24:25], eps[:, 0:1], ACT.Sqrt)
            with act.Fori(0, 2) as i:
                for n in range(4):
                    act.wait_ge(units_done, 1 + U_DOWN + 12 * i + 3 * n + 3)
                    A(blocks(fo, 4 * i + n), ps[:, (R_DOWN + n) % 2], ACT.Copy, scale=coef[:, 3, bass.ds(4 * i + n, 1)])
                    act.wait_ge(n2a["summed"], 1 + 4 * i + max(n - 1, 0))
                    A(sq6[:, n % 2], ps[:, (R_DOWN + n) % 2], ACT.Square).then_inc(evacuated, 1)
            root(n2a, 1, rcol6)
            residual_squares(n2b, n2a, fo)
            root(n2b, DB // 2, rcol6)
            act.dma_start(wfb[:], arrays["w_fourier"]).then_inc(att_in, 16)
            act.dma_start(dhd[:], arrays["dft_head"]).then_inc(att_in, 16)
            act.dma_start(dft[:], arrays["dft"]).then_inc(att_in, 16)
            act.dma_start(bias[:], arrays["dist"]).then_inc(att_in, 16)
            for b in range(DB):
                act.wait_ge(n2b["scaled"], b + 1)
                A(permuted(h_hi[:, b]), natural(hp6[:, b % 2]), ACT.Copy).then_inc(n2b["hi"], 1)

            def take_beside(j):
                if j == 1:
                    act.wait_ge(wf_sums, 1)
                    for m in range(2):
                        A(wf[:, 2 * m:2 * m + 2], ps[:, 2 + m].rearrange("p (b w) -> p b w", b=2),
                          ACT.Copy).then_inc(wf_ready, 1)
                if 2 <= j < 2 + DB:
                    b = j - 2
                    act.wait_ge(x2_turned, b + 1)
                    A(xN[:, :, b * P:(b + 1) * P], ps[:, 4 + b % 2].rearrange("p (r c) -> p r c", r=NT),
                      ACT.Copy).then_inc(x2_out, 1)
                    if b == DB - 1:
                        act.wait_ge(x2_out, DB)
                        act.dma_start(x2_dram, xN[:]).then_inc(x2_stored, 16)

            def take(p, j):
                act.wait_ge(units_done, 1 + U_ATT + N_ATT * p + j + 1)
                bank = ps[:, (R_ATT + j) % 2]
                first = isinstance(p, int) and p == 0
                if j < 6:
                    if not (first and j == 0):
                        act.wait_ge(qk_total, 6 * p + j)
                    if j == 0 and not first:
                        act.wait_ge(qk_moved, p)
                    A(qk_next[:, j], bank, ACT.Copy)
                    A(qsq[:], bank, ACT.Square).then_inc(evacuated, 1)
                elif j < 9:
                    if not (first and j == 6):
                        act.wait_ge(v_turned, 3 * p + j - 6)
                    A(vT[:], bank, ACT.Copy).then_inc(evacuated, 1)
                elif j == 9:
                    if not first:
                        act.wait_ge(fv_done, 2 * p)
                    A(ufT[:], bank, ACT.Copy).then_inc(evacuated, 1)
                elif j == 10:
                    if not first:
                        act.wait_ge(yf_steps, 2 * p - 1)
                    A(sgf[:], bank, ACT.Silu).then_inc(evacuated, 1)
                else:
                    if not first:
                        act.wait_ge(gate_moved, p)
                    A(sga_next[:], bank, ACT.Silu).then_inc(evacuated, 1)
                if 1 <= j <= 6:
                    m = j - 1
                    act.wait_ge(qk_total, 6 * p + m + 1)
                    if not (first and m < 3):
                        act.wait_ge(qk_steps, 12 * p + 2 * (m - 3) + 2)
                    A(qrt[:, m % 3], ps[:, 7], ACT.Sqrt, bias=eps[:, 1:2] if m < 3 else eps[:, 0:1],
                      scale=1.0 if m < 3 else 1.0 / HP).then_inc(qk_root, 1)
                if 7 <= j <= 9:
                    c = j - 7
                    act.wait_ge(v_turned, 3 * p + c + 1)
                    if c == 0 and not first:
                        act.wait_ge(v_moved, p)
                    A(vN_next[:, c], ps[:, 7].rearrange("p (t w) -> p t w", t=NT), ACT.Copy).then_inc(v_ready, 1)
                if j >= 10:
                    m = j - 10
                    act.wait_ge(fv_done, 2 * p + m + 1)
                    if m == 0 and not first:
                        act.wait_ge(ft_done, p)
                    A(fv[:, 2 * m:2 * m + 2], ps[:, 7].rearrange("p (t w) -> p t w", t=2),
                      ACT.Copy).then_inc(fv_ready, 1)

            def move_v(p):
                act.wait_ge(v_ready, 3 * p + 3)
                if not (isinstance(p, int) and p == 0):
                    act.wait_ge(attended, 1 + 8 * p)
                A(vN[:], vN_next[:], ACT.Copy).then_inc(v_moved, 1)

            def exp(a, n):
                act.wait_ge(biased, 1 + 8 * a + n + 1)
                A(pr[:], pr[:], ACT.Exp, bias=stat[:, 0:1], scale=-1.0,
                  accum_out=stat[:, 1:2]).then_inc(exped, 1)

            def pt_out(a, n):
                act.wait_ge(p_turned, 1 + 8 * a + n + 1)
                act.wait_ge(attended, 1 + 8 * a + n)
                A(pt[:], ps[:, 4:6].rearrange("p b w -> p (b w)")[:, 0:6 * P], ACT.Copy).then_inc(pt_ready, 1)
                A(bias[:, n % 4], bias[:, n % 4], ACT.Copy, scale=0.5).then_inc(bias_scaled, 1)

            def hi_fourier(a):
                act.wait_ge(yf_steps, 2 * a + 1)
                A(blocks(yo_hi, a), yf[:], ACT.Copy).then_inc(yf_hi_ready, 1)

            def hi_attention(a):
                act.wait_ge(ya_steps, 1 + 2 * a + 1)
                A(blocks(yo_hi, 4 + a), ya[:], ACT.Copy).then_inc(ya_hi_ready, 1)

            for j in range(N_ATT):
                take(0, j)
                if j >= 2:
                    take_beside(j - 1)
            act.wait_ge(x2_stored, 16)
            move_v(0)
            with act.Fori(0, 3) as a:
                for n in range(8):
                    exp(a, n)
                    take(a + 1, 3 * n // 2)
                    pt_out(a, n)
                    if n == 0:
                        hi_fourier(a)
                    if n % 2:
                        take(a + 1, (3 * n + 1) // 2)
                hi_attention(a)
                move_v(a + 1)

            act.wait_ge(units_done, 1 + U_OUT)
            for hv in range(2):
                cols = slice(hv * S, (hv + 1) * S)
                act.dma_start(x_res[:, :, cols], x2_dram[:, :, cols]).then_inc(x_res_in[hv], 16)
            for n in range(8):
                exp(3, n)
                pt_out(3, n)
                if n == 0:
                    hi_fourier(3)
                act.wait_ge(units_done, 1 + U_OUT + n + 1)
                if n >= 2:
                    act.wait_ge(out_turned, n - 1)
                A((ufT, sgf)[n % 2][:], ps[:, (R_ATT + n) % 2], ACT.Copy).then_inc(evacuated, 1)
            hi_attention(3)
            out = arrays["out"].rearrange("(i r) d -> i r d", r=NT)
            for hv in range(2):
                for t in range(NT):
                    cols = slice(hv * S, (hv + 1) * S)
                    act.wait_ge(out_steps, 4 * hv + t + 1)
                    act.dma_start(out[:, t, cols], x_res[:, t, cols]).then_inc(out_stored, 16)
            act.wait_ge(out_stored, 16 * 8)

        @block.vector
        def _(dve):
            V = nc.vector
            TT, STT, TS = V.tensor_tensor, V.scalar_tensor_tensor, V.tensor_scalar

            V.memset(ones[:], 1.0).then_inc(setup, 1)
            V.memset(eps[:, 0:1], EPS).then_inc(setup, 1)
            V.memset(eps[:, 1:2], HP * EPS).then_inc(setup, 1)
            V.memset(ev[:, :, 0:3], 0.0).then_inc(setup, 1)
            V.memset(scp[:, 0:2], 0.0).then_inc(setup, 1)

            def ada_start(m):
                for k in range(8):
                    n = 8 * m + k
                    dve.wait_ge(ada0_in[k], 16 * (m + 1))
                    if k == 0:
                        TS(acc0[:, m], ada0[:, k], small[:, k:k + 1], None, ALU.mult).then_inc(ada0_steps, 1)
                    else:
                        dve.wait_ge(ada0_steps, n)
                        STT(acc0[:, m], ada0[:, k], small[:, k:k + 1], acc0[:, m], ALU.mult,
                            ALU.add).then_inc(ada0_steps, 1)

            dve.wait_ge(cact_ready, 1)
            ada_start(0)
            dve.wait_ge(row_stats, 5)
            V.reciprocal(small[:, 16:20], small[:, 12:16]).then_inc(setup, 1)
            dve.wait_ge(setup, 6)
            for t in range(NT):
                TS(x_tok[:, t], x_tok[:, t], small[:, 16 + t:17 + t], None, ALU.mult).then_inc(row_scaled, 1)
            ada_start(1)
            dve.wait_ge(mod0_sums, 2)
            TT(mod[:, 0:16], ps[:, 2, 0:16], col("ada_b", 0, 16), ALU.add).then_inc(mod0_ready, 1)
            dve.wait_ge(mod0_ready, 1)
            STT(coef[:, 0], mod[:, 8:16], 1.0, col("g_pre", 0, DB), ALU.add, ALU.mult).then_inc(mod0_ready, 1)
            dve.wait_ge(mod0_ready, 2)
            dve.wait_ge(xn_ready, DB)
            for b in range(DB + 1):
                if b < DB:
                    if b >= 2:
                        dve.wait_ge(h_lo_ready, b - 1)
                    TS(hf[:, b % 2], xn[:, b], coef[:, 0, b:b + 1], mod[:, b:b + 1], ALU.mult,
                       ALU.add).then_inc(hf_ready, 1)
                if b:
                    dve.wait_ge(hf_ready, b)
                    dve.wait_ge(h_hi_ready, b)
                    TT(h_lo[:, b - 1], hf[:, (b - 1) % 2], h_hi[:, b - 1].bitcast(F32),
                       ALU.subtract).then_inc(h_lo_ready, 1)

            n_dt = [0]

            def dt_step(ins):
                ins.then_inc(dt_steps, 1)
                n_dt[0] += 1
                dve.wait_ge(dt_steps, n_dt[0])

            e, z, dt = dtw[:, 1], dtw[:, 4], dtN[:].rearrange("p c h -> p (c h)")
            dve.wait_ge(dt_act, 2)
            dt_step(TS(dtw[:, 2], ps[:, 5, 0:P], 0.0, None, ALU.max))
            dve.wait_ge(dt_act, 3)
            dt_step(TS(dtw[:, 3], e, 2.0, None, ALU.add))
            dt_step(V.reciprocal(dtw[:, 4], dtw[:, 3]))
            dt_step(TT(dtw[:, 3], e, dtw[:, 4], ALU.mult))
            dt_step(TT(z, dtw[:, 3], dtw[:, 3], ALU.mult))
            dt_step(TS(dtw[:, 5], z, 1.0 / 15, None, ALU.mult))
            for k in (13, 11, 9, 7, 5, 3):
                dt_step(STT(dtw[:, 5], dtw[:, 5], 1.0 / k, z, ALU.add, ALU.mult))
            dt_step(STT(dtw[:, 6], dtw[:, 5], 1.0, dtw[:, 3], ALU.add, ALU.mult))
            dt_step(STT(dt, dtw[:, 6], 2.0, dtw[:, 2], ALU.mult, ALU.add))
            dt_step(STT(dtw[:, 0].rearrange("p (c h) -> p c h", c=NT), dtN[:], -1.0,
                        dtw[:, 7, 0:SSD_HEADS].unsqueeze(1).broadcast_to([P, NT, SSD_HEADS]), ALU.mult, ALU.mult))
            dve.wait_ge(dt_turned, 2)
            V.tensor_copy(acsN[:].rearrange("p c h -> p (c h)"), ps[:, 5, P:2 * P]).then_inc(dt_tokens, 1)
            dve.wait_ge(dt_tokens, 1)
            dve.wait_ge(acc_cleared, 1)

            with dve.Fori(0, GROUPS) as g:
                def ada_piece(n):
                    k, hv = n // 2, n % 2
                    dve.wait_ge(ada_in[hv], 128 * g + 16 * k + 16)
                    part, w = ada_acc[:, hv * S:(hv + 1) * S], small[:, k:k + 1]
                    if k == 0:
                        dve.wait_ge(mod_sums, 1 + g)
                        TS(part, ada_raw[:, hv], w, None, ALU.mult).then_inc(ada_steps, 1)
                    else:
                        dve.wait_ge(ada_steps, 1 + 16 * g + n - 1)
                        STT(part, ada_raw[:, hv], w, part, ALU.mult, ALU.add).then_inc(ada_steps, 1)

                def conv(j):
                    dve.wait_ge(evacuated, E_GRP + 16 * g + j + 1)
                    for k in range(3):
                        if k:
                            dve.wait_ge(conv_taps, 18 * g + 3 * j + k)
                        STT(cv[:, j % 2], ev[:, j % 4, k:k + S], col("conv", (6 * g + j) * 5 + k),
                            cv[:, j % 2], ALU.mult, ALU.add).then_inc(conv_taps, 1)
                        if k < 2 and j < 5:
                            ada_piece(2 * j + k)

                def chunk(c):
                    base = 24 * g + 6 * c
                    dve.wait_ge(chunk_inputs, 4 * g + c + 1)
                    dve.wait_ge(y_done, 1 + 4 * g + max(c - 1, 0))
                    TT(scm[:, c % 2], ps[:, 5, 0:P], causal, ALU.mult).then_inc(chunk_steps, 1)
                    V.tensor_copy(bn[:, c % 2], ps[:, 5, P:2 * P]).then_inc(chunk_steps, 1)
                    TT(by_head(xdt[:, c % 2]), by_head(ps[:, 4]), per_token(dtN, c, g),
                       ALU.mult).then_inc(chunk_steps, 1)
                    dve.wait_ge(decays, 1 + 4 * g + c + 1)
                    dve.wait_ge(chunk_steps, 1 + base + 3)
                    TT(by_head(xst[:, c % 2]), by_head(xdt[:, c % 2]),
                       dec[:, c % 2, :, P - 1:P].broadcast_to([P, HEADS_G, HP]), ALU.mult).then_inc(chunk_steps, 1)
                    dve.wait_ge(chunk_steps, 1 + base + 4)
                    TT(dec[:, c % 2], dec[:, c % 2], scm[:, c % 2].unsqueeze(1).broadcast_to([P, HEADS_G, P]),
                       ALU.mult).then_inc(chunk_steps, 1)
                    TT(ect[:, c % 2], ect[:, c % 2],
                       CT[:, c * P:(c + 1) * P].unsqueeze(1).broadcast_to([P, HEADS_G, P]),
                       ALU.mult).then_inc(chunk_steps, 1)

                def state(c):
                    dve.wait_ge(s_done, 3 * g + c + 1)
                    if c == 0:
                        V.tensor_copy(hst[:, 1], ps[:, 7]).then_inc(state_steps, 1)
                        return
                    new, old = (c + 1) % 2, c % 2
                    if c == 2:
                        dve.wait_ge(y_done, 1 + 4 * g + 2)
                    dve.wait_ge(state_steps, 1 + 5 * g + (1, 3)[c - 1])
                    TT(by_head(hst[:, new]), by_head(hst[:, old]),
                       eld[:, c].unsqueeze(2).broadcast_to([P, HEADS_G, HP]), ALU.mult).then_inc(state_steps, 1)
                    dve.wait_ge(state_steps, 1 + 5 * g + (2, 4)[c - 1])
                    TT(hst[:, new], hst[:, new], ps[:, 7], ALU.add).then_inc(state_steps, 1)

                def add_y(c):
                    dve.wait_ge(y_done, 1 + 4 * g + c + 1)
                    dve.wait_ge(skip_ready, 4 * g + 4)
                    y = yg[:, :, c * P:(c + 1) * P]
                    TT(y, y, ps[:, 6 - 4 * (c % 2)].rearrange("p (b l) -> p b l", b=4), ALU.add).then_inc(gate_steps, 1)

                def short_conv(q):
                    e = 3 * q
                    dve.wait_ge(evacuated, E_GRP + 16 * g + 10 + e + 2)
                    TT(scp[:, 2:2 + S], ev[:, (6 + e) % 4, 3:3 + S], ev[:, (7 + e) % 4, 3:3 + S],
                       ALU.mult).then_inc(sc_steps, 1)
                    y = zs[:, q]
                    for k in (2, 1, 0):
                        dve.wait_ge(sc_steps, 1 + 10 * g + 5 * q + 3 - k)
                        w, u = col("sc_w", (2 * g + q) * 3 + k), scp[:, k:k + S]
                        if k == 2:
                            TS(y, u, w, None, ALU.mult).then_inc(sc_steps, 1)
                        else:
                            STT(y, u, w, y, ALU.mult, ALU.add).then_inc(sc_steps, 1)
                    dve.wait_ge(sc_steps, 1 + 10 * g + 5 * q + 4)
                    dve.wait_ge(evacuated, E_GRP + 16 * g + 10 + e + 3)
                    TT(blocks(ysc, 2 * g + q), y, ev[:, (8 + e) % 4, 3:3 + S], ALU.mult).then_inc(sc_steps, 1)

                for j in range(6):
                    conv(j)
                chunk(0)
                ada_piece(10)
                chunk(1)
                ada_piece(11)
                state(0)
                chunk(2)
                add_y(0)
                state(1)
                ada_piece(12)
                ada_piece(13)
                chunk(3)
                ada_piece(14)
                ada_piece(15)
                add_y(1)
                state(2)
                add_y(2)
                add_y(3)
                dve.wait_ge(gate_steps, 1 + 15 * g + 4)
                TT(yg[:], yg[:], zs[:], ALU.mult).then_inc(gate_steps, 1)
                dve.wait_ge(gate_steps, 1 + 15 * g + 5)
                short_conv(0)
                dve.wait_ge(y_squared, g + 1)
                V.tensor_reduce(sct[:], xcT[:].rearrange("p b t -> p t b"), AX.X, ALU.add).then_inc(gate_steps, 1)
                dve.wait_ge(mod_sums, 1 + g + 1)
                TT(mod[:, bass.ds(16 + 8 * g, 8)], ps[:, 7, 0:8], col("ada_b", 16 + 8 * g, 8),
                   ALU.add).then_inc(mod_ready, 1)
                dve.wait_ge(group_root, 1 + g + 1)
                V.reciprocal(sct[:], sct[:]).then_inc(gate_steps, 1)
                dve.wait_ge(gate_steps, 1 + 15 * g + 7)
                for b in range(4):
                    STT(yg[:, b], yg[:, b], col("ssd_g", 4 * g + b), sct[:], ALU.mult,
                        ALU.mult).then_inc(gate_steps, 1)
                for b in range(4):
                    dve.wait_ge(y_hi_ready, 4 * g + b + 1)
                    TT(y_lo[:, b], yg[:, b], y_hi[:, b].bitcast(F32), ALU.subtract).then_inc(gate_steps, 1)
                short_conv(1)
                for n in range(DB):
                    if n % 2 == 0:
                        dve.wait_ge(half_done, 4 * g + n // 2 + 1)
                    else:
                        dve.wait_ge(units_done, 1 + U_GRP + N_GRP * g + 16 + n // 2 + 1)
                    TT(ssd_acc[:, n], ssd_acc[:, n], ps[:, (R_GRP + 16 + n) % 2], ALU.add).then_inc(acc_steps, 1)

            dve.wait_ge(mod_ready, 1 + 4)
            TT(coef[:, 1], mod[:, 16:24], col("g_post", 0, DB), ALU.mult).then_inc(coef_ready, 1)
            STT(coef[:, 2], mod[:, 32:40], 1.0, col("f_pre", 0, DB), ALU.add, ALU.mult).then_inc(coef_ready, 1)
            TT(coef[:, 3], mod[:, 40:48], col("f_post", 0, DB), ALU.mult).then_inc(coef_ready, 1)
            for q in range(2):
                dve.wait_ge(sc_hi_ready, q + 1)
                TT(sc_lo[:, 4 * q:4 * q + 4], ysc[:, 4 * q:4 * q + 4], sc_hi[:, 4 * q:4 * q + 4].bitcast(F32),
                   ALU.subtract).then_inc(sc_lo_ready, 1)
            dve.wait_ge(acc_steps, 1 + 32)
            with dve.Fori(0, 2) as i:
                for j in range(4):
                    at_ = 16 * i + 4 * j
                    dve.wait_ge(evacuated, E_MIX + 12 * i + 3 * j + 3)
                    TT(gts[:, j % 2, 2], gts[:, j % 2, 2], gts[:, j % 2, 1], ALU.mult).then_inc(mix_steps, 1)
                    TT(gts[:, j % 2, 0], gts[:, j % 2, 0], blocks(ssd_acc, 4 * i + j), ALU.mult).then_inc(mix_steps, 1)
                    dve.wait_ge(mix_steps, 1 + at_ + 2)
                    TT(mixf[:, j % 2], gts[:, j % 2, 0], gts[:, j % 2, 2], ALU.add).then_inc(mix_steps, 1)
                    dve.wait_ge(mix_hi_ready, 4 * i + j + 1)
                    TT(blocks(mix_lo, 4 * i + j), mixf[:, j % 2], blocks(mix_hi, 4 * i + j).bitcast(F32),
                       ALU.subtract).then_inc(mix_steps, 1)

            dve.wait_ge(mix_steps, 1 + 32)
            dve.wait_ge(units_done, 1 + U_WO)
            V.memset(ssum[:], 0.0).then_inc(setup, 1)
            dve.wait_ge(setup, 7)
            with dve.Fori(0, DB // 2) as i:
                for j in range(2):
                    dve.wait_ge(evacuated, E_WO + 2 * i + j + 1)
                    dve.wait_ge(n1a["summed"], 1 + 2 * i + j)
                    TT(ssum[:], ssum[:], sq[:, j], ALU.add).then_inc(n1a["summed"], 1)

            def rsqrt(n, rc, dg):
                dve.wait_ge(n["root"], 1)
                V.reciprocal(rc[:, NT:2 * NT], rc[:, 0:NT]).then_inc(n["inverse"], 1)
                dve.wait_ge(n["inverse"], 1)
                TT(dg[:], ident.unsqueeze(1).broadcast_to([P, NT, P]),
                   rc[:, NT:2 * NT].unsqueeze(2).broadcast_to([P, NT, P]), ALU.mult).then_inc(n["diag"], 1)
                dve.wait_ge(n["spread"], 1)

            def add_branch(n, branch, rc, dg, after):
                rsqrt(n, rc, dg)

                def pair(b):
                    dve.wait_ge(after["squared"], b + 2)
                    TT(branch[:, b], branch[:, b], branch[:, b + 1], ALU.add).then_inc(after["summed"], 1)

                for b in range(DB + 1):
                    if b >= 4 and b % 2 == 0:
                        pair(b - 4)
                    if b < DB:
                        TT(branch[:, b], branch[:, b], ps[:, 5], ALU.mult).then_inc(n["scaled"], 1)
                    if b:
                        dve.wait_ge(n["scaled"], b)
                        if n is n1a:
                            dve.wait_ge(xt_ready, b)
                        TT(xT[:, b - 1], xT[:, b - 1], branch[:, b - 1], ALU.add).then_inc(n["added"], 1)
                pair(DB - 2)

            def scale(n, b, hp_, w):
                if b >= 2:
                    dve.wait_ge(n["lo"], b - 1)
                STT(hp_[:, b % 2], xT[:, b], w, ps[:, 5], ALU.mult, ALU.mult).then_inc(n["scaled"], 1)

            add_branch(n1a, mo, rcol, diag, n1b)
            rsqrt(n1b, rcol, diag)
            scale(n1b, 0, hp, coef[:, 2, 0:1])
            for b in range(DB):
                if b + 1 < DB:
                    scale(n1b, b + 1, hp, coef[:, 2, b + 1:b + 2])
                dve.wait_ge(n1b["hi"], b + 1)
                STT(h_lo[:, b], hp[:, b % 2], mod[:, 24 + b:25 + b], h_hi[:, b].bitcast(F32), ALU.add,
                    ALU.subtract).then_inc(n1b["lo"], 1)

            for j in range(4):
                V.memset(fe[:, j, 0:2], 0.0).then_inc(ffn_taps, 2)
            V.memset(af[:, 0, 0:1], 0.0).then_inc(ffn_steps, 4)
            with dve.Fori(0, FF_PAIRS // 2) as i:
                for p in range(2):
                    for j in (2 * p, 2 * p + 1):
                        dve.wait_ge(evacuated, E_UP + 4 * i + j + 1)
                        for k in range(2):
                            if k:
                                dve.wait_ge(ffn_taps, 8 + 8 * i + 2 * j + 1)
                            STT(fcv[:, j], fe[:, j, k:k + S], col("ffn_w", 16 * i + 4 * j + k), fcv[:, j],
                                ALU.mult, ALU.add).then_inc(ffn_taps, 1)
                    dve.wait_ge(ffn_taps, 8 + 8 * i + 4 * p + 4)
                    dve.wait_ge(ffn_silu, 2 * i + p + 1)
                    TT(af[:, p], fcv[:, 2 * p], fcv[:, 2 * p + 1], ALU.mult).then_inc(ffn_steps, 1)
                    dve.wait_ge(act_hi_ready, 2 * i + p + 1)
                    TT(blocks(act_lo, 2 * i + p), af[:, p], blocks(act_hi, 2 * i + p).bitcast(F32),
                       ALU.subtract).then_inc(ffn_steps, 1)

            V.memset(ssum6[:], 0.0).then_inc(setup, 1)
            dve.wait_ge(setup, 8)
            with dve.Fori(0, 2) as i:
                for n in range(4):
                    dve.wait_ge(evacuated, E_DOWN + 4 * i + n + 1)
                    dve.wait_ge(n2a["summed"], 1 + 4 * i + n)
                    TT(ssum6[:], ssum6[:], sq6[:, n % 2], ALU.add).then_inc(n2a["summed"], 1)
            add_branch(n2a, fo, rcol6, diag6, n2b)
            rsqrt(n2b, rcol6, diag6)
            scale(n2b, 0, hp6, col("nw2", 0))
            for b in range(DB):
                if b + 1 < DB:
                    scale(n2b, b + 1, hp6, col("nw2", b + 1))
                dve.wait_ge(n2b["hi"], b + 1)
                TT(permuted(h_lo[:, b]), natural(hp6[:, b % 2]), permuted(h_hi[:, b]).bitcast(F32),
                   ALU.subtract).then_inc(n2b["lo"], 1)

            def scale_qk(p, j):
                dve.wait_ge(qk_root, 6 * p + j + 1)
                V.reciprocal(qrt[:, j % 3], qrt[:, j % 3]).then_inc(qk_steps, 1)
                dve.wait_ge(qk_steps, 12 * p + 2 * j + 1)
                STT(qk_next[:, j], qk_next[:, j], col("qk_w", 6 * p + j), qrt[:, j % 3], ALU.mult,
                    ALU.mult).then_inc(qk_steps, 1)

            def move_qk(p):
                dve.wait_ge(qk_steps, 12 * p + 12)
                if not (isinstance(p, int) and p == 0):
                    dve.wait_ge(scored, 8 * p)
                V.tensor_copy(qk[:], qk_next[:]).then_inc(qk_moved, 1)

            def move_gate(p):
                dve.wait_ge(evacuated, E_ATT + N_ATT * p + 12)
                V.tensor_copy(sga[:], sga_next[:]).then_inc(gate_moved, 1)

            def split_y(source, gate, y, steps, step, hi_ready, pair, at_block):
                TT(y[:], source, gate, ALU.mult).then_inc(steps, 1)
                dve.wait_ge(hi_ready, pair + 1)
                TT(blocks(yo_lo, at_block), y[:], blocks(yo_hi, at_block).bitcast(F32),
                   ALU.subtract).then_inc(steps, 1)

            def fourier(a):
                dve.wait_ge(ft_done, a + 1)
                dve.wait_ge(evacuated, E_ATT + N_ATT * a + 11)
                split_y(ps[:, 7], sgf[:], yf, yf_steps, 2 * a, yf_hi_ready, a, a)

            def attention(a):
                dve.wait_ge(attended, 1 + 8 * a + 8)
                dve.wait_ge(gate_moved, a + 1)
                split_y(ps[:, 6], sga[:], ya, ya_steps, 2 * a, ya_hi_ready, a, 4 + a)

            def add_bias(a, n):
                dve.wait_ge(scored, 8 * a + n + 1)
                dve.wait_ge(bias_scaled, 8 * a + n + 1)
                dve.wait_ge(p_turned, 1 + 8 * a + n)
                V.memset(stat[:, 3:4], 0.0)
                V.tensor_tensor_reduce(
                    pr[:], ps[:, 2:4].rearrange("p b w -> p (b w)")[:, 0:6 * P], bias[:, n % 4],
                    -1.0, 3e38, ALU.add, ALU.min, stat[:, 0:1]).then_inc(biased, 1)

            def normalise(a, n):
                dve.wait_ge(exped, 8 * a + n + 1)
                V.reciprocal(stat[:, 2:3], stat[:, 1:2]).then_inc(normed, 1)
                dve.wait_ge(normed, 16 * a + 2 * n + 1)
                TS(pr[:], pr[:], stat[:, 2:3], None, ALU.mult).then_inc(normed, 1)

            for j in range(6):
                scale_qk(0, j)
            move_qk(0)
            move_gate(0)
            with dve.Fori(0, 3) as a:
                for n in range(8):
                    add_bias(a, n)
                    normalise(a, n)
                    if n == 0:
                        fourier(a)
                    elif n < 7:
                        scale_qk(a + 1, n - 1)
                move_qk(a + 1)
                attention(a)
                move_gate(a + 1)

            def add_block(n):
                dve.wait_ge(out_turned, n + 1)
                dve.wait_ge(x_res_in[n // 4], 16)
                x = x_res[:, :, n * P:(n + 1) * P]
                TT(x, x, ps[:, 7].rearrange("p (r c) -> p r c", r=NT), ALU.add).then_inc(out_added, 1)

            for n in range(8):
                add_bias(3, n)
                normalise(3, n)
                if n == 0:
                    fourier(3)
                else:
                    add_block(n - 1)
            attention(3)
            add_block(7)
            dve.wait_ge(out_added, DB)
            for m in range(8):
                hv, t = m // 4, m % 4
                dve.wait_ge(out_sums, m + 1)
                x = x_res[:, t, hv * S:(hv + 1) * S]
                TT(x, x, ps[:, m], ALU.add).then_inc(out_steps, 1)


def lay_out(i):
    f = {k: np.ascontiguousarray(np.asarray(v, np.float32)) for k, v in i.items()}

    def blocks_of(w):
        k, n = w.shape
        return w.reshape(k // P, P, n // P, P).transpose(2, 1, 0, 3)

    def column(v):
        return v.reshape(-1, P).T

    zero = np.zeros
    w_in = f["w_in"][0]
    cut = np.cumsum([2048, 3072, SSD_HEADS, D, D, D])
    z, xbc, dt, scb, scc, sch, gates = (w_in[:, x:y] for x, y in zip([0, *cut], [*cut, w_in.shape[1]]))
    z, xbc, scb, scc, sch, gates = map(blocks_of, (z, xbc, scb, scc, sch, gates))
    units = []
    units.append(blocks_of(np.concatenate([dt, zero((D, P - SSD_HEADS), np.float32)], 1))[0])
    w_ssd = blocks_of(f["w_ssd_out"][0])
    for g in range(GROUPS):
        units += [xbc[16 + g], xbc[20 + g]] + [xbc[4 * g + b] for b in range(4)] + [z[4 * g + b] for b in range(4)]
        for q in range(2):
            units += [scc[2 * g + q], sch[2 * g + q], scb[2 * g + q]]
        for n in range(0, DB, 2):
            units.append(np.concatenate([w_ssd[n][:, 4 * g:4 * g + 4], w_ssd[n + 1][:, 4 * g:4 * g + 4]], 1))
    w_sc = blocks_of(f["w_sc_out"][0])
    for j in range(DB):
        units += [gates[j], gates[DB + j], w_sc[j]]
    units += list(blocks_of(f["w_o"][0]))
    up = blocks_of(f["w_up"][0])
    for p in range(FF_PAIRS):
        units += [up[p], up[FF_PAIRS + p]]
    down = blocks_of(f["w_down"][0])
    for n in range(DB):
        units += [down[n][:, 0:8], down[n][:, 8:16],
                  np.concatenate([down[n][:, 16:22], zero((P, 2, P), np.float32)], 1)]
    w2 = f["w_in_2"]
    qkv = CFG * S
    uf, gf = blocks_of(w2[:, :S]), blocks_of(w2[:, S:2 * S])
    q, k, v = (blocks_of(w2[:, 2 * S + n * qkv:2 * S + (n + 1) * qkv]) for n in range(3))
    ga = blocks_of(w2[:, 2 * S + 3 * qkv:])
    for i2 in range(4):
        for m in (q, k, v):
            units += [m[4 * c + i2] for c in range(CFG)]
        units += [uf[i2], gf[i2], ga[i2]]
    out2 = blocks_of(f["w_out_2"])
    for n in range(DB):
        units.append(np.concatenate([out2[n][:, OUT_TILES], zero((P, 1, P), np.float32)], 1))
    units.append(out2[:, :, 7].transpose(1, 0, 2))
    stream = np.stack([u.reshape(P, UW) for u in units])
    assert len(units) == UNITS

    t = {}
    t["ident"] = np.eye(P, dtype=np.float32)
    t["causal"] = np.triu(np.ones((P, P), np.float32))
    t["head_ones"] = np.kron(np.eye(2, dtype=np.float32), np.ones((HP, HP), np.float32))
    t["c"] = column(f["c"][0])
    t["ada_b"] = column(f["ada_b"][0])
    t["g_pre"], t["g_post"] = column(f["mix_pre_g"][0]), column(f["mix_post_g"][0])
    t["f_pre"], t["f_post"] = column(f["ffn_pre_g"][0]), column(f["ffn_post_g"][0])
    t["nw2"] = column(f["norm_w_2"])
    cw = np.concatenate([f["ssd_conv_w"][0], f["ssd_conv_b"]], 0).reshape(5, 24, P)
    order = [b for g in range(GROUPS) for b in (16 + g, 20 + g, 4 * g, 4 * g + 1, 4 * g + 2, 4 * g + 3)]
    t["conv"] = cw[:, order].transpose(2, 1, 0).reshape(P, 120)
    t["d_skip"] = column(np.repeat(f["ssd_d"][0], HP))
    t["ssd_g"] = column(f["ssd_norm_g"][0])
    t["sc_w"] = f["sc_conv_w"][0].reshape(3, DB, P).transpose(2, 1, 0).reshape(P, 3 * DB)
    fw = np.concatenate([f["ffn_conv_w"][0], f["ffn_conv_b"]], 0).reshape(4, 2, FF_PAIRS, P)
    t["ffn_w"] = fw.transpose(3, 2, 1, 0).reshape(P, 8 * FF_PAIRS)
    qk = [f[n].reshape(CFG, 4, P) for n in ("q_norm_w_2", "k_norm_w_2")]
    t["qk_w"] = np.stack(qk).transpose(3, 2, 0, 1).reshape(P, 24)
    t["dt_bias"] = np.concatenate([f["ssd_dt_bias"][0], zero(P - SSD_HEADS, np.float32)])[:, None]
    t["a_log"] = np.repeat(f["ssd_a_log"], P, 0)
    table = np.concatenate([t[n] for n, _ in _widths], 1)
    assert table.shape == (P, NCOL)

    tok = np.arange(S).reshape(P, NT).T.reshape(-1)
    angle = 2 * np.pi * (np.outer(tok, tok) % S) / S
    dft = np.stack([np.cos(angle), np.sin(angle)]).reshape(2, NT, P, S).transpose(2, 0, 1, 3)
    ch = 2 * np.pi * (np.outer(np.arange(HP), np.arange(HP)) % HP) / HP
    scale = 1 / np.sqrt(S * HP)
    dft_head = np.stack([np.kron(np.eye(2), m) for m in (np.cos(ch) * scale, -np.sin(ch) * scale)], 1)
    i1 = np.arange(P)
    dist = np.full((P, NT, 6 * P), MASKED)
    near = np.abs(i1[:, None] - i1[None])
    for r in range(NT):
        far = np.abs((4 * i1 + r)[:, None] - tok[None])
        dist[:, r, :S] = np.where(far <= 64, -far, MASKED)
        dist[:, r, S:S + P] = np.where(near <= 64, -4.0 * near, MASKED)
        dist[:, r, S + P:] = np.where(near % 4 == 0, -4.0 * near, MASKED)
    wfo = zero((P, 4, P), np.float32)
    wfo[:HP, :, :HP] = f["w_fourier_2"][0::2].transpose(1, 0, 2)
    wfo[HP:, :, HP:] = f["w_fourier_2"][1::2].transpose(1, 0, 2)
    dist *= 0.5
    return {
        "stream": stream,
        "ada": f["ada_w"][0].reshape(8, P, 6, D).transpose(2, 0, 1, 3).reshape(48, P, D),
        "table": table,
        "x": f["x"][0].reshape(NT, P, D).transpose(1, 0, 2),
        "dft": dft.astype(np.float32),
        "dft_head": dft_head.astype(np.float32),
        "dist": dist.reshape(P, -1).astype(np.float32),
        "w_fourier": wfo,
    }


def kernel(**inputs):
    import concourse.bacc as bacc
    from concourse.bass_utils import run_bass_kernel_spmd

    arrays = {k: np.ascontiguousarray(v) for k, v in lay_out(inputs).items()}
    nc = bacc.Bacc("TRN2", target_bir_lowering=False, num_devices=1)
    a = {k: nc.dram_tensor(k, v.shape, F32, kind="ExternalInput").ap() for k, v in arrays.items()}
    a["out"] = nc.dram_tensor("out", (S, D), F32, kind="ExternalOutput").ap()
    build(nc, a)
    r = run_bass_kernel_spmd(nc, [arrays], core_ids=[0])
    return r.results[0]["out"].reshape(1, S, D)
```

```python
from contextlib import ExitStack

import numpy as np

import concourse.bass as bass
from concourse import mybir

ALU = mybir.AluOpType
ACT = mybir.ActivationFunctionType
AX = mybir.AxisListType
F32 = mybir.dt.float32
F32R = mybir.dt.float32r

P = 128
S = 512
NT = S // P
D = 1024
DB = D // P
KT = 8
UW = KT * P
EPS = 1e-6

SSD_HEADS, HEADS_G, GROUPS, HP, NSTATE = 32, 8, 4, 64, 128
FF_PAIRS = 2816 // P
CFG = 3
MASKED = -1e33

U_GRP = 1
N_GRP = 20
U_MIX = U_GRP + GROUPS * N_GRP
U_WO = U_MIX + 3 * DB
U_UP = U_WO + DB
U_DOWN = U_UP + 2 * FF_PAIRS
U_ATT = U_DOWN + FF_PAIRS
N_ATT = 12
U_OUT = U_ATT + 4 * N_ATT
U_LAST = U_OUT + DB
UNITS = U_LAST + 1

R_GRP = 1
R_MIX = R_GRP + GROUPS * 24
R_UP = R_MIX + 3 * DB
R_ATT = R_UP + 2 * FF_PAIRS

E_GRP = 1
E_MIX = E_GRP + GROUPS * 16
E_UP = E_MIX + 3 * DB
E_ATT = E_UP + 2 * FF_PAIRS
E_OUT = E_ATT + 4 * N_ATT

NORM_A, NORM_B = (0, 1, 2, 4), (3, 5, 6, 7)
OUT_TILES = (0, 1, 2, 4, 5, 6, 3)

_widths = [("ident", P), ("causal", P), ("head_ones", P), ("c", DB), ("ada_b", 48), ("g_pre", DB),
           ("g_post", DB), ("f_pre", DB), ("f_post", DB), ("nw2", DB), ("conv", 24 * 5), ("d_skip", 16),
           ("ssd_g", 16), ("sc_w", DB * 3), ("ffn_w", 2 * FF_PAIRS * 4), ("qk_w", 24), ("dt_bias", 1),
           ("a_log", SSD_HEADS)]
COL = {}
_at = 0
for _n, _w in _widths:
    COL[_n] = _at
    _at += _w
NCOL = _at


def build(nc, arrays):
    with ExitStack() as ctx:
        KB = 1024
        names = set()

        def at(name, offset, shape, dt=F32):
            assert name not in names
            names.add(name)
            n = 4
            for s in shape[1:]:
                n *= s
            assert BASE + offset + n <= 229344, (name, offset, n)
            return nc.alloc_sbuf_tensor_at(name, shape, dt, offset=BASE + offset)

        def area(offset, end):
            pos = [offset]

            def place(name, shape, dt=F32):
                t = at(name, pos[0], shape, dt)
                n = 4
                for s in shape[1:]:
                    n *= s
                pos[0] += (n + 31) // 32 * 32
                assert pos[0] <= end, (name, pos[0], end)
                return t
            place.end = lambda: pos[0]
            return place

        def sem(name):
            return ctx.enter_context(nc.semaphore(name))

        BASE = 16512
        END = 229344 - BASE
        keep = area(0, 70 * KB)
        tab = keep("tab", [P, NCOL])
        ones = keep("ones", [P, P])
        eps = keep("eps", [P, 2])
        mod = keep("mod", [P, 48])
        coef = keep("coef", [P, 4, DB])
        small = keep("small", [P, 32])
        raw = keep("raw", [P, 4, UW])
        w_hi = keep("w_hi", [P, 2, UW], F32R)
        w_lo = keep("w_lo", [P, 2, UW], F32R)
        H_AT = keep.end()
        h_hi = keep("h_hi", [P, DB, S], F32R)
        h_lo = keep("h_lo", [P, DB, S], F32R)
        FREE = keep.end()

        g = area(FREE, END)
        ssd_acc = g("ssd_acc", [P, DB, S])
        ysc = g("ysc", [P, DB, S])
        ada_raw = g("ada_raw", [P, 2, S])
        ada_acc = g("ada_acc", [P, D])
        ev = g("ev", [P, 4, S + 4])
        cv = g("cv", [P, 2, S])
        scp = g("scp", [P, S + 4])
        sct = g("sct", [P, S])
        BT = g("BT", [P, S])
        CT = g("CT", [P, S])
        dtN = g("dtN", [P, NT, SSD_HEADS])
        acsN = g("acsN", [P, NT, SSD_HEADS])
        g_end = g.end()
        g = area(g_end, END)
        xcT = g("xcT", [P, 4, S])
        yg = g("yg", [P, 4, S])
        zs = g("zs", [P, 4, S])
        abc = g("abc", [P, 2, HEADS_G, P])
        dec = g("dec", [P, 2, HEADS_G, P])
        ect = g("ect", [P, 2, HEADS_G, P])
        eld = g("eld", [P, NT, HEADS_G])
        xdt = g("xdt", [P, 2, S])
        xst = g("xst", [P, 2, S])
        scm = g("scm", [P, 2, P])
        bn = g("bn", [P, 2, P])
        hst = g("hst", [P, 2, S])
        y_at = g.end()
        g = area(y_at, END)
        y_hi = g("y_hi", [P, 4, S], F32R)
        y_lo = g("y_lo", [P, 4, S], F32R)
        dtw = at("dtw", g_end, [P, 8, NT * SSD_HEADS])
        dtr = at("dtr", g_end + 4 * KB, [SSD_HEADS, 2, S])
        g = area(g_end, END)
        x_tok = g("x_tok", [P, NT, D])
        ada0 = g("ada0", [P, 8, D])
        acc0 = g("acc0", [P, 2, D])
        xn = g("xn", [P, DB, S])
        hf = at("hf", FREE + 4 * KB, [P, 2, S])
        junk = at("junk", FREE, [P, D])

        g = area(FREE + 32 * KB, END)
        mix_hi = g("mix_hi", [P, DB, S], F32R)
        mix_lo = g("mix_lo", [P, DB, S], F32R)
        sc_hi = g("sc_hi", [P, DB, S], F32R)
        sc_lo = g("sc_lo", [P, DB, S], F32R)
        gts = g("gts", [P, 2, 3, S])
        mixf = g("mixf", [P, 2, S])
        xr = at("xr", FREE, [P, NT, D])
        br = at("br", FREE + 16 * KB, [P, NT, D])
        hn = at("hn", FREE + 104 * KB, [P, 4, S])
        dgc = at("dgc", FREE + 116 * KB, [P, 2, D])
        GG_AT = FREE + 128 * KB + 128
        gg = at("gg", GG_AT, [P, 2, D])

        g = area(FREE + 16 * KB, GG_AT)
        fe = g("fe", [P, 4, S + 4])
        fcv = g("fcv", [P, 4, S])
        af = g("af", [P, 2, S])
        act_hi = g("act_hi", [P, FF_PAIRS, S], F32R)
        act_lo = g("act_lo", [P, FF_PAIRS, S], F32R)
        at_hi = g("at_hi", [P, 2, S], F32R)
        at_lo = at("at_lo", GG_AT, [P, 2, S], F32R)

        g = area(FREE, END)
        yo_hi = g("yo_hi", [P, DB, S], F32R)
        yo_lo = g("yo_lo", [P, DB, S], F32R)
        dft = g("dft", [P, 2, NT, S])
        bias = g("bias", [P, NT, 6 * P])
        wf = g("wf", [P, 4, 2 * P])
        qk = g("qk", [P, 2 * CFG, S])
        wfb = at("wfb", g.end(), [P, 4, P])
        dhd = at("dhd", g.end() + 2 * KB, [P, 2, P])
        vN = g("vN", [P, CFG, NT, P])
        sga = g("sga", [P, S])
        qk_next = g("qk_next", [P, 2 * CFG, S])
        vN_next = g("vN_next", [P, CFG, NT, P])
        sga_next = g("sga_next", [P, S])
        qsq = g("qsq", [P, S])
        qsq_hi = g("qsq_hi", [P, S], F32R)
        qsq_lo = g("qsq_lo", [P, S], F32R)
        head_r = g("head_r", [P, P], F32R)
        qrt = g("qrt", [P, 3, S])
        vT = g("vT", [P, S])
        ufT = g("ufT", [P, S])
        sgf = g("sgf", [P, S])
        fv = g("fv", [P, NT, 2 * P])
        pr = g("pr", [P, 6 * P])
        yf = g("yf", [P, S])
        ya = g("ya", [P, S])
        stat = g("stat", [P, 4])
        pt = g("pt", [P, 6 * P])
        x_res = at("x_res", H_AT, [P, NT, D])

        ps = ctx.enter_context(nc.psum_tensor("ps", [P, 8, S], F32))
        acs_dram = nc.dram_tensor("acs_dram", (SSD_HEADS, S), F32, kind="Internal").ap()
        x2_dram = nc.dram_tensor("x2_dram", (P, NT, D), F32, kind="Internal").ap()

        raw_landed = [sem(f"raw_landed{i}") for i in range(4)]
        split_hi = sem("split_hi")
        split_done = sem("split_done")
        units_done = sem("units_done")
        half_done = sem("half_done")
        evacuated = sem("evacuated")
        tab_in = sem("tab_in")
        x_in = sem("x_in")
        ada0_in = [sem(f"ada0_in{i}") for i in range(8)]
        setup = sem("setup")
        acc_cleared = sem("acc_cleared")
        cact_ready = sem("cact_ready")
        row_stats = sem("row_stats")
        row_scaled = sem("row_scaled")
        ada0_steps = sem("ada0_steps")
        mod0_sums = sem("mod0_sums")
        mod0_ready = sem("mod0_ready")
        x_turned = sem("x_turned")
        xn_ready = sem("xn_ready")
        hf_ready = sem("hf_ready")
        h_hi_ready = sem("h_hi_ready")
        h_lo_ready = sem("h_lo_ready")
        dt_act = sem("dt_act")
        dt_steps = sem("dt_steps")
        acs_stored = sem("acs_stored")
        dt_turned = sem("dt_turned")
        dt_tokens = sem("dt_tokens")
        ada_in = [sem(f"ada_in{i}") for i in range(2)]
        ada_steps = sem("ada_steps")
        mod_sums = sem("mod_sums")
        mod_ready = sem("mod_ready")
        conv_taps = sem("conv_taps")
        conv_out = sem("conv_out")
        skip_ready = sem("skip_ready")
        abc_in = [sem(f"abc_in{i}") for i in range(2)]
        dec_args = sem("dec_args")
        decays = sem("decays")
        chunk_inputs = sem("chunk_inputs")
        chunk_steps = sem("chunk_steps")
        s_done = sem("s_done")
        y_done = sem("y_done")
        state_steps = sem("state_steps")
        gate_steps = sem("gate_steps")
        y_squared = sem("y_squared")
        group_sum = sem("group_sum")
        group_root = sem("group_root")
        y_hi_ready = sem("y_hi_ready")
        sc_steps = sem("sc_steps")
        acc_steps = [sem(f"acc_steps{i}") for i in range(2)]
        coef_ready = sem("coef_ready")
        sc_hi_ready = sem("sc_hi_ready")
        sc_lo_ready = sem("sc_lo_ready")
        mix_steps = sem("mix_steps")
        mix_hi_ready = sem("mix_hi_ready")
        x2_in = sem("x2_in")

        def norm_sems(k):
            return {n: sem(f"n{k}_{n}") for n in
                    ("product", "squared", "root", "inverse", "scaled", "added", "rows", "rows_act", "turned",
                     "full_act", "full_dve", "hi", "lo")}
        n1, n2 = norm_sems(1), norm_sems(2)
        gg_diag = sem("gg_diag")
        gg_spread = sem("gg_spread")
        gg_ready = sem("gg_ready")
        staged_hi = sem("staged_hi")
        staged_lo = sem("staged_lo")
        ffn_taps = sem("ffn_taps")
        ffn_silu = sem("ffn_silu")
        ffn_steps = sem("ffn_steps")
        act_hi_ready = sem("act_hi_ready")
        x2_stored = sem("x2_stored")
        att_in = sem("att_in")
        wf_in = sem("wf_in")
        wf_sums = sem("wf_sums")
        wf_ready = sem("wf_ready")
        bias_scaled = sem("bias_scaled")
        fv_done = sem("fv_done")
        fv_ready = sem("fv_ready")
        ft_done = sem("ft_done")
        yf_steps = sem("yf_steps")
        yf_hi_ready = sem("yf_hi_ready")
        ya_steps = sem("ya_steps")
        ya_hi_ready = sem("ya_hi_ready")
        head_ready = sem("head_ready")
        qsq_split = sem("qsq_split")
        qk_total = sem("qk_total")
        qk_root = sem("qk_root")
        qk_steps = sem("qk_steps")
        qk_moved = sem("qk_moved")
        v_turned = sem("v_turned")
        v_ready = sem("v_ready")
        v_moved = sem("v_moved")
        gate_moved = sem("gate_moved")
        scored = sem("scored")
        biased = sem("biased")
        exped = sem("exped")
        normed = sem("normed")
        p_turned = sem("p_turned")
        pt_ready = sem("pt_ready")
        attended = sem("attended")
        x_res_in = [sem(f"x_res_in{i}") for i in range(2)]
        out_turned = sem("out_turned")
        out_added = sem("out_added")
        out_sums = sem("out_sums")
        out_steps = sem("out_steps")
        out_stored = sem("out_stored")

        start_at_one = [*acc_steps, group_root, chunk_steps, state_steps, mod_ready, gate_steps, biased,
                        pt_ready, decays, sc_steps, y_done, mix_steps, attended, ada_steps, units_done,
                        mod_sums, p_turned, ya_steps]

        ident = tab[:, COL["ident"]:COL["ident"] + P]
        causal = tab[:, COL["causal"]:COL["causal"] + P]
        head_ones = tab[:, COL["head_ones"]:COL["head_ones"] + P]

        def col(name, i, n=1):
            return tab[:, bass.ds(COL[name] + i, n)]

        def blocks(t, i):
            return t[:, bass.ds(i, 1), :].rearrange("p o s -> p (o s)")

        def per_token(t, chunk, g):
            return t[:, chunk, bass.ds(HEADS_G * g, HEADS_G)].unsqueeze(2).broadcast_to([P, HEADS_G, HP])

        def by_head(t):
            return t.rearrange("p (h c) -> p h c", h=HEADS_G)

        def permuted(t):
            return t.rearrange("p (r i) -> p i r", r=NT)

        def natural(t):
            return t.rearrange("p (i r) -> p i r", r=NT)

        def halves(t):
            return t.rearrange("p (h s) -> p h s", h=2)

        def banks_of(r):
            return ps[:, 2 * r:2 * r + 2]

        def is_first(p):
            return isinstance(p, int) and p == 0

        block = ctx.enter_context(nc.Block())

        @block.sync
        def _(sp):
            for signal in start_at_one:
                sp.sem_inc(signal, 1)
            sp.sem_inc(bias_scaled, NT)
            sp.dma_start(tab[:], arrays["table"]).then_inc(tab_in, 16)
            sp.dma_start(x_tok[:], arrays["x"]).then_inc(x_in, 16)
            for k in range(8):
                sp.dma_start(ada0[:, k], arrays["ada"][k]).then_inc(ada0_in[k], 16)
            for k in range(8):
                sp.wait_ge(ada0_steps, k + 1)
                sp.dma_start(ada0[:, k], arrays["ada"][8 + k]).then_inc(ada0_in[k], 16)
            for u in range(4):
                sp.dma_start(raw[:, u], arrays["stream"][u]).then_inc(raw_landed[u], 16)

            def stream(u, slot):
                sp.wait_ge(split_done, u - 3)
                src = arrays["stream"][bass.ds(u, 1)].rearrange("u p w -> (u p) w")
                sp.dma_start(raw[:, slot], src).then_inc(raw_landed[slot], 16)

            ADA_BEHIND = (0, 1, 2, 3, 4, 5, 9, 11)
            with sp.Fori(0, GROUPS) as g:
                for s in range(N_GRP):
                    stream(4 + N_GRP * g + s, s % 4)
                    if s in ADA_BEHIND:
                        k = ADA_BEHIND.index(s)
                        for hv in range(2):
                            sp.wait_ge(ada_steps, 1 + 16 * g + max(2 * k + hv - 1, 0))
                            src = arrays["ada"][bass.ds(16 + 8 * g + k, 1)].rearrange("m p w -> (m p) w")
                            sp.dma_start(ada_raw[:, hv], src[:, hv * S:(hv + 1) * S]).then_inc(ada_in[hv], 16)
            done = 4 + GROUPS * N_GRP
            loops = (UNITS - done) // 4
            with sp.Fori(0, loops) as i:
                for s in range(4):
                    stream(done + 4 * i + s, s)
            for u in range(done + 4 * loops, UNITS):
                stream(u, u % 4)

        @block.gpsimd
        def _(pool):
            def split(u, raw_slot, slot, landed):
                pool.wait_ge(raw_landed[raw_slot], landed)
                nc.gpsimd.tensor_tensor(w_hi[:, slot], raw[:, raw_slot],
                                        ones[:, 0:1].broadcast_to([P, UW]), ALU.mult).then_inc(split_hi, 1)
                pool.wait_ge(split_hi, u + 1)
                nc.gpsimd.tensor_tensor(w_lo[:, slot], raw[:, raw_slot], w_hi[:, slot].bitcast(F32),
                                        ALU.subtract).then_inc(split_done, 1)

            pool.wait_ge(setup, 1)
            split(0, 0, 0, 16)
            split(1, 1, 1, 16)
            pool.wait_ge(row_stats, 4)
            pool.wait_ge(h_lo_ready, DB)
            nc.gpsimd.memset(ssd_acc[:], 0.0).then_inc(acc_cleared, 1)
            with pool.Fori(0, (UNITS - 2) // 4) as i:
                for s in range(4):
                    pool.wait_ge(units_done, 1 + 4 * i + s + 1)
                    split(2 + 4 * i + s, (2 + s) % 4, s % 2, 16 * i + (16 if s < 2 else 32))
            for u in range(2 + (UNITS - 2) // 4 * 4, UNITS):
                pool.wait_ge(units_done, 1 + u - 1)
                split(u, u % 4, u % 2, 16 * (u // 4 + 1))

        @block.tensor
        def _(pe):
            def unit(u, slot, bank, free=None, x_hi=h_hi, x_lo=h_lo, k0=0, tiles=KT, at_k=0, start=True,
                     stop=True, last=True, signal=None, each=None):
                if at_k == 0:
                    pe.wait_ge(split_done, u + 1)
                if free is not None:
                    pe.wait_ge(*free)
                for k in range(tiles):
                    if each is not None:
                        pe.wait_ge(each[0], each[1] + each[2] * k)
                    w = slice((at_k + k) * P, (at_k + k + 1) * P)
                    nc.tensor.matmul(ps[:, bank], w_hi[:, slot, w], x_hi[:, k0 + k],
                                     start=start and k == 0, stop=False)
                    nc.tensor.matmul(ps[:, bank], w_hi[:, slot, w], x_lo[:, k0 + k], start=False, stop=False)
                    mm = nc.tensor.matmul(ps[:, bank], w_lo[:, slot, w], x_hi[:, k0 + k],
                                          start=False, stop=stop and k == tiles - 1)
                if signal is not None:
                    mm.then_inc(signal, 1)
                elif last:
                    mm.then_inc(units_done, 1)

            def tiles(u, slot, bank, x_hi, x_lo, at_, of, ready=False, free=None, start=False, signal=None):
                if ready:
                    pe.wait_ge(split_done, u + 1)
                    pe.wait_ge(*free)
                for m, (t, k) in enumerate(zip(at_, of)):
                    w = slice(t * P, (t + 1) * P)
                    nc.tensor.matmul(ps[:, bank], w_hi[:, slot, w], x_hi[:, k], start=start and m == 0, stop=False)
                    nc.tensor.matmul(ps[:, bank], w_hi[:, slot, w], x_lo[:, k], start=False, stop=False)
                    mm = nc.tensor.matmul(ps[:, bank], w_lo[:, slot, w], x_hi[:, k], start=False,
                                          stop=signal is not None and m == len(of) - 1)
                if signal is not None:
                    mm.then_inc(signal, 1)

            def opening(units, results, x_hi, x_lo, sem_, first, step, free0, free1):
                for k in range(KT + 4):
                    if k < KT:
                        pe.wait_ge(sem_, first + step * k)
                    for n in range(2):
                        t = k - 4 * n
                        if not 0 <= t < KT:
                            continue
                        if t == 0:
                            pe.wait_ge(split_done, units[n] + 1)
                            pe.wait_ge(*(free0, free1)[n])
                        bank, slot, w = results[n] % 2, units[n] % 2, slice(t * P, (t + 1) * P)
                        nc.tensor.matmul(ps[:, bank], w_hi[:, slot, w], x_hi[:, t], start=(t == 0), stop=False,
                                         skip_group_check=True)
                        nc.tensor.matmul(ps[:, bank], w_hi[:, slot, w], x_lo[:, t], start=False, stop=False,
                                         skip_group_check=True)
                        mm = nc.tensor.matmul(ps[:, bank], w_lo[:, slot, w], x_hi[:, t], start=False,
                                              stop=(t == KT - 1), skip_group_check=True)
                        if t == KT - 1:
                            mm.then_inc(units_done, 1)

            pe.wait_ge(tab_in, 16)
            pe.wait_ge(setup, 1)

            def mod_sum(m):
                pe.wait_ge(ada0_steps, 8 * (m + 1))
                for b in range(DB):
                    mm = nc.tensor.matmul(ps[:, 2, 8 * m + b:8 * m + b + 1], acc0[:, m, b * P:(b + 1) * P],
                                          ones[:, 0:1], start=True, stop=True)
                mm.then_inc(mod0_sums, 1)

            mod_sum(0)
            pe.wait_ge(row_scaled, 4)
            for b in range(DB):
                if b >= 4:
                    pe.wait_ge(xn_ready, b - 3)
                for t in range(NT):
                    mm = nc.tensor.transpose(ps[:, 4 + b % 4, t * P:(t + 1) * P], x_tok[:, t, b * P:(b + 1) * P],
                                             ident)
                mm.then_inc(x_turned, 1)
            mod_sum(1)

            unit(0, 0, 0, each=(h_lo_ready, 1, 1))

            def turn_dt():
                pe.wait_ge(evacuated, 1)
                pe.wait_ge(xn_ready, DB)
                for c in range(NT):
                    mm = nc.tensor.transpose(ps[:, 5, c * SSD_HEADS:(c + 1) * SSD_HEADS],
                                             dtr[:, 0, c * P:(c + 1) * P], ident[0:SSD_HEADS, 0:SSD_HEADS])
                mm.then_inc(dt_turned, 1)

            def sum_dt():
                pe.wait_ge(dt_steps, 15)
                nc.tensor.matmul(ps[:, 5, P:2 * P], causal, dtw[:, 0], start=True, stop=True)
                for c in range(NT):
                    mm = nc.tensor.matmul(ps[0:SSD_HEADS, 3, c * P:(c + 1) * P],
                                          dtw[:, 0, c * SSD_HEADS:(c + 1) * SSD_HEADS], causal, start=True,
                                          stop=True)
                mm.then_inc(dt_turned, 1)

            def group(g, behind):
                def u_(j):
                    return U_GRP + N_GRP * g + j

                def project(j):
                    if j < 2:
                        free = (acc_steps[j], 1 + 4 * g)
                    else:
                        free = (evacuated, E_GRP + 16 * g + j - 1)
                    unit(u_(j), (1 + j) % 2, (R_GRP + j) % 2, free)

                def turn(c):
                    pe.wait_ge(chunk_steps, 1 + 24 * g + (6 * (c - 1) + 3 if c else 0))
                    if c == 0:
                        pe.wait_ge(dt_tokens, 1)
                        pe.wait_ge(group_root, 1 + g)
                    cols = slice(c * P, (c + 1) * P)
                    pe.wait_ge(conv_out, 6 * g + 6)
                    nc.tensor.matmul(ps[:, 5, 0:P], BT[:, cols], CT[:, cols], start=True, stop=True)
                    nc.tensor.transpose(ps[:, 5, P:2 * P], BT[:, cols], ident)
                    for b in range(4):
                        mm = nc.tensor.transpose(ps[:, 4, b * P:(b + 1) * P], xcT[:, b, cols], ident)
                    mm.then_inc(chunk_inputs, 1)

                def state(c):
                    pe.wait_ge(chunk_steps, 1 + 24 * g + 6 * c + 6)
                    pe.wait_ge(state_steps, 1 + 5 * g + (0, 1, 3)[c])
                    if c == 0:
                        pe.wait_ge(mod_ready, 1 + g)
                    nc.tensor.matmul(ps[:, 7], bn[:, c % 2], xst[:, c % 2], start=True, stop=True).then_inc(s_done, 1)

                def outputs(c):
                    pe.wait_ge(chunk_steps, 1 + 24 * g + 6 * c + 6)
                    pe.wait_ge(gate_steps, 1 + 15 * g + max(c - 1, 0))
                    if c:
                        pe.wait_ge(state_steps, 1 + 5 * g + (1, 3, 5)[c - 1])
                    for h in range(HEADS_G):
                        rows, hc = slice(64 * (h % 2), 64 * (h % 2) + 64), slice(h * HP, (h + 1) * HP)
                        out = ps[rows, 6 - 4 * (c % 2), (h // 2) * P:(h // 2 + 1) * P]
                        mm = nc.tensor.matmul(out, xdt[:, c % 2, hc], dec[:, c % 2, h], start=(h < 2),
                                              stop=(c == 0), skip_group_check=True)
                        if c:
                            mm = nc.tensor.matmul(out, hst[:, c % 2, hc], ect[:, c % 2, h], start=False,
                                                  stop=True, skip_group_check=True)
                    mm.then_inc(y_done, 1)

                for j in range(6):
                    project(j)
                    if j in behind:
                        behind[j]()
                project(6)
                turn(0)
                project(7)
                turn(1)
                project(8)
                state(0)
                outputs(0)
                turn(2)
                project(9)
                state(1)
                outputs(1)
                turn(3)
                project(10)
                state(2)
                outputs(2)
                project(11)
                outputs(3)
                project(12)
                pe.wait_ge(ada_steps, 1 + 16 * g + 16)
                pe.wait_ge(state_steps, 1 + 5 * g + 5)
                for b in range(DB):
                    mm = nc.tensor.matmul(ps[:, 7, b:b + 1], ada_acc[:, b * P:(b + 1) * P], ones[:, 0:1],
                                          start=True, stop=True)
                mm.then_inc(mod_sums, 1)
                project(13)
                pe.wait_ge(gate_steps, 1 + 15 * g + 6)
                nc.tensor.matmul(ps[:, 4], ones[:], sct[:], start=True, stop=True).then_inc(group_sum, 1)
                project(14)
                project(15)
                pe.wait_ge(gate_steps, 1 + 15 * g + 15)
                for n in range(DB):
                    if n < 2:
                        free = (evacuated, E_GRP + 16 * g + 15 + n)
                    else:
                        free = (acc_steps[n % 2], 1 + 4 * g + n // 2)
                    unit(u_(16 + n // 2), (1 + n // 2) % 2, (R_GRP + 16 + n) % 2, free, y_hi, y_lo,
                         tiles=4, at_k=4 * (n % 2), signal=half_done if n % 2 == 0 else units_done)

            turn_dt()
            group(0, {0: sum_dt})
            with pe.Fori(1, GROUPS) as g:
                group(g, {})

            for parity in acc_steps:
                pe.wait_ge(parity, 1 + 4 * GROUPS)
            with pe.Fori(0, 2) as i:
                for j in range(12):
                    if j == 2:
                        pe.wait_ge(sc_lo_ready, 2)
                    if j == 6:
                        pe.wait_ge(gg_diag, i + 1)
                        for hv in range(2):
                            mm = nc.tensor.matmul(ps[:, 2 + hv], ones[:], blocks(dgc, i)[:, hv * S:(hv + 1) * S],
                                                  start=True, stop=True)
                        mm.then_inc(gg_spread, 1)
                    sc = j % 3 == 2
                    unit(U_MIX + 12 * i + j, (U_MIX + j) % 2, (R_MIX + j) % 2, (evacuated, E_MIX + 12 * i + j - 1),
                         sc_hi if sc else h_hi, sc_lo if sc else h_lo)

            def by_class(u, slot, x_hi, x_lo, first=False, evacuated_before=None):
                pe.wait_ge(split_done, u + 1)
                for r in ((1, 2, 3, 0) if first else range(NT)):
                    if first and r == 0:
                        pe.wait_ge(evacuated, evacuated_before)
                    mm = one_class(r, slot, x_hi, x_lo, first, False)
                mm.then_inc(units_done, 1)

            def one_class(r, slot, x_hi, x_lo, first, last):
                q = slice(r * P, (r + 1) * P)
                for hv in range(2):
                    out, w = ps[:, 2 * r + hv], slice(hv * S, (hv + 1) * S)
                    nc.tensor.matmul(out, x_hi[:, q], w_hi[:, slot, w], start=first, stop=False)
                    nc.tensor.matmul(out, x_hi[:, q], w_lo[:, slot, w], start=False, stop=False)
                    mm = nc.tensor.matmul(out, x_lo[:, q], w_hi[:, slot, w], start=False, stop=last)
                return mm

            def last_by_class(u, slots, operands, n):
                pe.wait_ge(split_done, u + 1)
                for m, r in ((0, 0), (0, 1), (0, 2), (1, 0), (1, 1), (0, 3), (1, 2), (1, 3)):
                    if (m, r) == (1, 0):
                        pe.wait_ge(split_done, u + 2)
                    mm = one_class(r, slots[m], *operands[m], False, m == 1)
                    if r == NT - 1:
                        mm.then_inc(units_done, 1)
                    elif m == 1:
                        mm.then_inc(n["product"], 1)

            def norm(n, turned):
                pe.wait_ge(n["scaled"], NT)
                for r in range(NT):
                    if r:
                        pe.wait_ge(n["rows"], r)
                    else:
                        pe.wait_ge(n["rows_act"], 1)
                    for b in range(DB):
                        mm = nc.tensor.transpose(turned(b, r), br[:, r, b * P:(b + 1) * P], ident)
                        if r == NT - 1:
                            mm.then_inc(n["turned"], 1)

            for k in range(DB - 2):
                pe.wait_ge(mix_steps, 1 + 4 * (k + 1))
                if k == 0:
                    pe.wait_ge(gg_ready, 2)
                by_class(U_WO + k, (U_WO + k) % 2, mix_hi[:, k], mix_lo[:, k], k == 0, E_UP)
            pe.wait_ge(mix_steps, 1 + 4 * DB)
            last_by_class(U_WO + DB - 2, ((U_WO + DB) % 2, (U_WO + DB + 1) % 2),
                          [(mix_hi[:, k], mix_lo[:, k]) for k in (DB - 2, DB - 1)], n1)
            norm(n1, lambda b, r: natural(ps[:, b])[:, :, r])
            opening((U_UP, U_UP + 1), (R_UP, R_UP + 1), h_hi, h_lo, n1["lo"], 1, 1,
                    (n1["full_act"], 1), (n1["full_dve"], 1))
            for j in (2, 3):
                unit(U_UP + j, (U_UP + j) % 2, (R_UP + j) % 2, (evacuated, E_UP + j - 1))
            with pe.Fori(1, FF_PAIRS // 2) as i:
                for j in range(4):
                    unit(U_UP + 4 * i + j, (U_UP + j) % 2, (R_UP + j) % 2, (evacuated, E_UP + 4 * i + j - 1))
            pe.wait_ge(n1["lo"], DB)

            def down(k, j, first=False):
                pe.wait_ge(staged_hi, k + 1)
                pe.wait_ge(staged_lo, k + 1)
                by_class(U_DOWN + k, (U_DOWN + j) % 2, at_hi[:, j], at_lo[:, j], first, E_ATT)

            down(0, 0, first=True)
            down(1, 1)
            with pe.Fori(1, FF_PAIRS // 2 - 1) as i:
                for j in range(2):
                    down(2 * i + j, j)
            pe.wait_ge(staged_hi, FF_PAIRS)
            pe.wait_ge(staged_lo, FF_PAIRS)
            last_by_class(U_DOWN + FF_PAIRS - 2, (U_DOWN % 2, (U_DOWN + 1) % 2),
                          [(at_hi[:, j], at_lo[:, j]) for j in range(2)], n2)
            norm(n2, lambda b, r: ps[:, b, r * P:(r + 1) * P])

            def head_transforms():
                pe.wait_ge(wf_in, 16 * 2)
                for b in range(4):
                    for m in range(2):
                        out = ps[:, 2 + b // 2, (b % 2) * 256 + m * P:(b % 2) * 256 + (m + 1) * P]
                        mm = nc.tensor.matmul(out, dhd[:, m], wfb[:, b], start=True, stop=True)
                mm.then_inc(wf_sums, 1)

            def half(p, x):
                j = x // 2
                u = U_ATT + N_ATT * p + j
                if x % 2 == 0:
                    tiles(u, (U_ATT + j) % 2, (R_ATT + j) % 2, h_hi, h_lo, range(0, 4), range(0, 4),
                          ready=True, free=(evacuated, E_ATT + N_ATT * p + j - 1), start=True)
                    return
                tiles(u, (U_ATT + j) % 2, (R_ATT + j) % 2, h_hi, h_lo, range(4, 8), range(4, 8), signal=units_done)
                follow(p, j)

            def follow(p, j):
                if 1 <= j <= 6:
                    m = j - 1
                    pe.wait_ge(qsq_split, 6 * p + m + 1)
                    if m == 0:
                        pe.wait_ge(head_ready, 1)
                    if m:
                        pe.wait_ge(qk_root, 6 * p + m)
                    elif not is_first(p):
                        pe.wait_ge(yf_steps, 2 * p - 1)
                    nc.tensor.matmul(ps[:, 7], head_r[:], qsq_hi[:], start=True, stop=False)
                    nc.tensor.matmul(ps[:, 7], head_r[:], qsq_lo[:], start=False, stop=True).then_inc(qk_total, 1)
                if 7 <= j <= 9:
                    c = j - 7
                    pe.wait_ge(evacuated, E_ATT + N_ATT * p + 6 + c + 1)
                    if c:
                        pe.wait_ge(v_ready, 3 * p + c)
                    else:
                        pe.wait_ge(qk_root, 6 * p + 6)
                    for t in range(NT):
                        mm = nc.tensor.transpose(ps[:, 7, t * P:(t + 1) * P], vT[:, t * P:(t + 1) * P], ident)
                    mm.then_inc(v_turned, 1)
                if j >= 10:
                    m = j - 10
                    if m:
                        pe.wait_ge(fv_ready, 2 * p + 1)
                    else:
                        pe.wait_ge(v_ready, 3 * p + 3)
                        pe.wait_ge(wf_ready, 2)
                        pe.wait_ge(evacuated, E_ATT + N_ATT * p + 10)
                    for t in range(2 * m, 2 * m + 2):
                        mm = nc.tensor.matmul(ps[:, 7, (t % 2) * 256:(t % 2) * 256 + 256], ufT[:, t * P:(t + 1) * P],
                                              blocks(wf, p), start=True, stop=True)
                    mm.then_inc(fv_done, 1)

            def token_transform(a):
                pe.wait_ge(fv_ready, 2 * a + 2)
                for t in range(NT):
                    nc.tensor.matmul(ps[:, 7], fv[:, t, 0:P], dft[:, 0, t], start=(t == 0), stop=False)
                    mm = nc.tensor.matmul(ps[:, 7], fv[:, t, P:2 * P], dft[:, 1, t], start=False,
                                          stop=(t == NT - 1))
                mm.then_inc(ft_done, 1)

            def scores(a, n):
                rows, r = slice(64 * (n // 4), 64 * (n // 4) + 64), n % 4
                q = slice(r * P, (r + 1) * P)
                if n == 0:
                    pe.wait_ge(qk_moved, a + 1)
                pe.wait_ge(biased, 1 + 8 * a + n)
                nc.tensor.matmul(ps[:, 2], qk[rows, 0, q], qk[rows, CFG], start=True, stop=True)
                nc.tensor.matmul(ps[:, 3, 0:P], qk[rows, 1, q], qk[rows, CFG + 1, q], start=True, stop=True)
                nc.tensor.matmul(ps[:, 3, P:2 * P], qk[rows, 2, q], qk[rows, CFG + 2, q], start=True,
                                 stop=True).then_inc(scored, 1)

            def turn_p(a, n):
                pe.wait_ge(normed, 16 * a + 2 * n + 2)
                pe.wait_ge(pt_ready, 1 + 8 * a + n)
                for m in range(6):
                    mm = nc.tensor.transpose(ps[:, 4 + m // 4, (m % 4) * P:(m % 4 + 1) * P],
                                             pr[:, m * P:(m + 1) * P], ident)
                mm.then_inc(p_turned, 1)

            def attend(a, n):
                rows, r = slice(64 * (n // 4), 64 * (n // 4) + 64), n % 4
                pe.wait_ge(pt_ready, 1 + 8 * a + n + 1)
                if n == 0:
                    pe.wait_ge(v_moved, a + 1)
                    pe.wait_ge(ya_steps, 1 + 2 * a)
                for m in range(6):
                    cfg, tile = (0, m) if m < 4 else (m - 3, r)
                    mm = nc.tensor.matmul(ps[rows, 6, r * P:(r + 1) * P], vN[:, cfg, tile, rows],
                                          pt[:, m * P:(m + 1) * P], start=(r == 0 and m == 0),
                                          stop=(m == 5), skip_group_check=True)
                mm.then_inc(attended, 1)

            opening((U_ATT, U_ATT + 1), (R_ATT, R_ATT + 1), h_hi, h_lo, n2["lo"], 1, 1,
                    (n2["full_act"], 1), (n2["full_dve"], 1))
            follow(0, 1)
            for x in range(4, 2 * N_ATT):
                half(0, x)
                if x == 7:
                    head_transforms()
            pe.wait_ge(att_in, 16 * 2)
            with pe.Fori(0, 3) as a:
                for n in range(8):
                    scores(a, n)
                    half(a + 1, 3 * n)
                    half(a + 1, 3 * n + 1)
                    if n == 0:
                        token_transform(a)
                    turn_p(a, n)
                    half(a + 1, 3 * n + 2)
                    attend(a, n)

            def out_turn(n):
                pe.wait_ge(evacuated, E_OUT + n + 1)
                if n:
                    pe.wait_ge(out_added, n)
                else:
                    pe.wait_ge(yf_steps, 2 * 3 + 1)
                src = (ufT, sgf)[n % 2]
                for r in range(NT):
                    mm = nc.tensor.transpose(ps[:, 7, r * P:(r + 1) * P], src[:, r * P:(r + 1) * P], ident)
                mm.then_inc(out_turned, 1)

            for n in range(8):
                u, bank = U_OUT + n, (R_ATT + n) % 2
                scores(3, n)
                if n == 0:
                    token_transform(3)
                tiles(u, u % 2, bank, yo_hi, yo_lo, range(0, 4), OUT_TILES[0:4], ready=True,
                      free=(evacuated, E_OUT + n - 1), start=True)
                if n:
                    out_turn(n - 1)
                turn_p(3, n)
                if n == 0:
                    attend(3, n)
                    pe.wait_ge(ya_steps, 1 + 2 * 3)
                    pe.wait_ge(yf_steps, 2 * 4)
                tiles(u, u % 2, bank, yo_hi, yo_lo, range(4, 7), OUT_TILES[4:7], signal=units_done)
                if n:
                    attend(3, n)
            out_turn(7)
            pe.wait_ge(ya_steps, 1 + 2 * 4)
            pe.wait_ge(split_done, U_LAST + 1)
            pe.wait_ge(evacuated, E_OUT + 8)
            slot = U_LAST % 2
            for hv in range(2):
                w = slice(hv * S, (hv + 1) * S)
                for t in range(NT):
                    bank = 4 * hv + t
                    out, q = ps[:, bank], slice(t * P, (t + 1) * P)
                    if bank == 7:
                        pe.wait_ge(out_added, DB)
                    nc.tensor.matmul(out, yo_hi[:, 7, q], w_hi[:, slot, w], start=True, stop=False)
                    nc.tensor.matmul(out, yo_hi[:, 7, q], w_lo[:, slot, w], start=False, stop=False)
                    nc.tensor.matmul(out, yo_lo[:, 7, q], w_hi[:, slot, w], start=False,
                                     stop=True).then_inc(out_sums, 1)

        @block.scalar
        def _(act):
            A = nc.scalar.activation

            act.wait_ge(tab_in, 16)
            A(small[:, 0:8], col("c", 0, DB), ACT.Silu).then_inc(cact_ready, 1)
            act.wait_ge(x_in, 16)
            for t in range(NT):
                if t:
                    act.wait_ge(row_stats, t)
                A(junk[:], x_tok[:, t], ACT.Square, accum_out=small[:, 8 + t:9 + t]).then_inc(row_stats, 1)
            act.wait_ge(row_stats, 4)
            act.wait_ge(setup, 3)
            A(small[:, 12:16], small[:, 8:12], ACT.Sqrt, bias=eps[:, 0:1], scale=1.0 / D).then_inc(row_stats, 1)
            for b in range(DB):
                act.wait_ge(x_turned, b + 1)
                A(xn[:, b], ps[:, 4 + b % 4], ACT.Copy).then_inc(xn_ready, 1)
            act.wait_ge(mod0_ready, 2)
            act.wait_ge(xn_ready, DB)
            for b in range(DB):
                A(h_hi[:, b], xn[:, b], ACT.Identity, bias=mod[:, b:b + 1],
                  scale=coef[:, 0, b:b + 1]).then_inc(h_hi_ready, 1)
            A(dtw[:, 7, 0:SSD_HEADS], col("a_log", 0, SSD_HEADS), ACT.Exp).then_inc(dt_act, 1)

            act.wait_ge(units_done, 1 + 1)
            A(dtr[:, 0], ps[0:SSD_HEADS, 0], ACT.Identity,
              bias=tab[0:SSD_HEADS, COL["dt_bias"]:COL["dt_bias"] + 1]).then_inc(evacuated, 1)
            act.wait_ge(dt_turned, 1)
            A(dtw[:, 1], ps[:, 5, 0:P], ACT.Abs).then_inc(dt_act, 1)
            act.wait_ge(dt_act, 2)
            A(dtw[:, 1], dtw[:, 1], ACT.Exp, scale=-1.0).then_inc(dt_act, 1)
            act.wait_ge(dt_turned, 2)
            A(dtr[:, 1], ps[0:SSD_HEADS, 3], ACT.Copy).then_inc(dt_act, 1)
            act.wait_ge(dt_act, 4)
            act.dma_start(acs_dram, dtr[:, 1]).then_inc(acs_stored, 16)

            with act.Fori(0, GROUPS) as g:
                def load_abc(c):
                    act.wait_ge(decays, 1 + 4 * g + max(c - 1, 0))
                    src = acs_dram[bass.ds(HEADS_G * g, HEADS_G), c * P:(c + 1) * P]
                    act.dma_start(abc[:, c % 2], src.unsqueeze(0).broadcast_to([P, HEADS_G, P])
                                  ).then_inc(abc_in[c % 2], 16)

                def out_of(j, unit_no):
                    act.wait_ge(units_done, 1 + U_GRP + N_GRP * g + unit_no + 1)

                def conv_in(j):
                    out_of(j, j)
                    if j < 4:
                        act.wait_ge(sc_steps, 1 + 10 * g)
                    else:
                        act.wait_ge(conv_taps, 18 * g + 3 * (j - 4) + 3)
                    bank = ps[:, (R_GRP + j) % 2]
                    A(ev[:, j % 4, 3:3 + S], bank, ACT.Copy)
                    if j >= 2:
                        act.wait_ge(conv_out, 6 * g + j - 1)
                    A(cv[:, j % 2], bank, ACT.Identity, bias=col("conv", (6 * g + j) * 5 + 4),
                      scale=col("conv", (6 * g + j) * 5 + 3)).then_inc(evacuated, 1)

                def conv_silu(j):
                    act.wait_ge(conv_taps, 18 * g + 3 * j + 3)
                    dst = (BT[:], CT[:])[j] if j < 2 else xcT[:, j - 2]
                    A(dst, cv[:, j % 2], ACT.Silu).then_inc(conv_out, 1)
                    if j >= 2:
                        act.wait_ge(conv_out, 6 * g + j + 1)
                        A(yg[:, j - 2], xcT[:, j - 2], ACT.Identity,
                          scale=col("d_skip", 4 * g + j - 2)).then_inc(skip_ready, 1)

                def z(b):
                    out_of(6 + b, 6 + b)
                    A(zs[:, b], ps[:, (R_GRP + 6 + b) % 2], ACT.Silu).then_inc(evacuated, 1)

                def chunk(c):
                    if c < 3:
                        load_abc(c + 1)
                    act.wait_ge(abc_in[c % 2], 32 * g + 16 * (c // 2) + 16)
                    act.wait_ge(dt_tokens, 1)
                    act.wait_ge(y_done, 1 + 4 * g + max(c - 1, 0))
                    for h in range(HEADS_G):
                        ins = A(dec[:, c % 2, h], abc[:, c % 2, h], ACT.Relu,
                                bias=acsN[:, c, bass.ds(HEADS_G * g + h, 1)], scale=-1.0)
                    ins.then_inc(dec_args, 1)
                    act.wait_ge(dec_args, 4 * g + c + 1)
                    A(dec[:, c % 2], dec[:, c % 2], ACT.Exp, scale=-1.0)
                    A(eld[:, c], abc[:, c % 2, :, P - 1], ACT.Exp)
                    A(ect[:, c % 2], abc[:, c % 2], ACT.Exp).then_inc(decays, 1)

                def sc_in(e):
                    out_of(10 + e, 10 + e)
                    if e < 4:
                        act.wait_ge(conv_taps, 18 * g + 18)
                    else:
                        act.wait_ge(sc_steps, 1 + 10 * g + 1)
                    A(ev[:, (6 + e) % 4, 3:3 + S], ps[:, (R_GRP + 10 + e) % 2], ACT.Copy).then_inc(evacuated, 1)

                act.wait_ge(gate_steps, 1 + 15 * g)
                conv_in(0)
                conv_in(1)
                act.wait_ge(acs_stored, 16)
                load_abc(0)
                for j in range(2, 6):
                    conv_silu(j - 2)
                    conv_in(j)
                    if j == 3:
                        chunk(0)
                conv_silu(4)
                conv_silu(5)
                z(0)
                chunk(1)
                z(1)
                z(2)
                chunk(2)
                z(3)
                chunk(3)
                sc_in(0)
                sc_in(1)
                sc_in(2)
                act.wait_ge(gate_steps, 1 + 15 * g + 5)
                A(xcT[:], yg[:], ACT.Square).then_inc(y_squared, 1)
                sc_in(3)
                act.wait_ge(group_sum, g + 1)
                A(sct[:], ps[:, 4], ACT.Sqrt, bias=eps[:, 0:1], scale=1.0 / S).then_inc(group_root, 1)
                sc_in(4)
                for b in range(4):
                    act.wait_ge(gate_steps, 1 + 15 * g + 8 + b)
                    A(y_hi[:, b], yg[:, b], ACT.Copy).then_inc(y_hi_ready, 1)
                sc_in(5)

            act.wait_ge(sc_steps, 1 + 10 * GROUPS)
            for q in range(2):
                A(sc_hi[:, 4 * q:4 * q + 4], ysc[:, 4 * q:4 * q + 4], ACT.Copy).then_inc(sc_hi_ready, 1)
            act.wait_ge(units_done, 1 + U_MIX)
            with act.Fori(0, 2) as i:
                def hi(j):
                    act.wait_ge(mix_steps, 1 + 16 * i + 4 * j + 3)
                    A(permuted(blocks(mix_hi, 4 * i + j)), natural(mixf[:, j % 2]), ACT.Copy).then_inc(mix_hi_ready, 1)
                for j in range(4):
                    for m in range(3):
                        act.wait_ge(units_done, 1 + U_MIX + 12 * i + 3 * j + m + 1)
                        if m == 0 and j < 2:
                            act.wait_ge(mix_steps, 1 + 16 * i)
                        elif m == 0:
                            act.wait_ge(mix_steps, 1 + 16 * i + 4 * (j - 2) + 3)
                        A(gts[:, j % 2, m], ps[:, (R_MIX + 3 * j + m) % 2],
                          ACT.Sigmoid if m < 2 else ACT.Copy).then_inc(evacuated, 1)
                        if m == 0 and j:
                            hi(j - 1)
                        if m == 1 and j == 2:
                            act.wait_ge(gg_spread, i + 1)
                            A(halves(blocks(gg, i)), ps[:, 2:4], ACT.Copy).then_inc(gg_ready, 1)
                hi(3)

            act.wait_ge(mix_steps, 1 + 32)
            act.dma_start(xr[:], arrays["x_classes"]).then_inc(x2_in, 16)
            act.wait_ge(coef_ready, 3)
            A(small[:, 24:25], eps[:, 0:1], ACT.Sqrt)

            def norm(n, unit_no, then, scale, shift):
                def root(m, first, r):
                    act.wait_ge(n["squared"], m + 1)
                    A(small[:, first + 4 + r:first + 5 + r], small[:, first + r:first + 1 + r],
                      ACT.Sqrt, bias=eps[:, 0:1], scale=1.0 / D).then_inc(n["root"], 1)

                def product(r):
                    if r < NT - 1:
                        act.wait_ge(n["product"], r + 1)
                    else:
                        act.wait_ge(units_done, 1 + unit_no + 1)
                    A(halves(br[:, r]), banks_of(r), ACT.Square, accum_out=small[:, 8 + r:9 + r]).then_inc(n["squared"], 1)
                    root(NORM_A[r], 8, r)

                def residual(r):
                    act.wait_ge(n["added"], r + 1)
                    A(br[:, r], xr[:, r], ACT.Square, accum_out=small[:, 20 + r:21 + r]).then_inc(n["squared"], 1)
                    root(NORM_B[r], 20, r)

                def rows(r):
                    act.wait_ge(n["inverse"], NORM_B[r] + 1)
                    A(br[:, r], xr[:, r], ACT.Copy, scale=small[:, 28 + r:29 + r]).then_inc(n["rows_act"], 1)

                product(0)
                product(1)
                product(2)
                residual(0)
                product(3)
                residual(1)
                rows(0)
                residual(2)
                residual(3)
                then()

                def full(b):
                    act.wait_ge(n["turned"], b + 1)
                    if b >= 4:
                        act.wait_ge(n["lo"], b - 3)
                    A(hn[:, b % 4], ps[:, b], ACT.Identity, scale=scale(b), **shift(b)).then_inc(n["full_act"], 1)

                def hi(b):
                    act.wait_ge(n["full_dve" if b % 2 else "full_act"], b // 2 + 1)
                    A(h_hi[:, b], hn[:, b % 4], ACT.Copy).then_inc(n["hi"], 1)

                full(0)
                hi(0)
                for b in range(2, DB, 2):
                    full(b)
                    hi(b - 1)
                    hi(b)
                hi(DB - 1)

            norm(n1, U_WO + DB - 1, lambda: None, lambda b: coef[:, 2, b:b + 1],
                 lambda b: {"bias": mod[:, 24 + b:25 + b]})

            def up_round(i):
                def tap_in(j):
                    act.wait_ge(units_done, 1 + U_UP + 4 * i + j + 1)
                    act.wait_ge(ffn_taps, 8 * i + 2 * j + 2)
                    act.wait_ge(ffn_steps, 4 * i + 2 * (j // 2) + 1)
                    A(fe[:, j, 2:2 + S], ps[:, (R_UP + j) % 2], ACT.Copy)
                    A(fcv[:, j], ps[:, (R_UP + j) % 2], ACT.Identity, bias=col("ffn_w", 16 * i + 4 * j + 3),
                      scale=col("ffn_w", 16 * i + 4 * j + 2)).then_inc(evacuated, 1)

                def silu(p):
                    act.wait_ge(ffn_taps, 8 + 8 * i + 4 * p + 2)
                    A(fcv[:, 2 * p], fcv[:, 2 * p], ACT.Silu).then_inc(ffn_silu, 1)

                def hi(p):
                    act.wait_ge(ffn_steps, 4 + 4 * i + 2 * p + 1)
                    A(blocks(act_hi, 2 * i + p), af[:, p], ACT.Copy).then_inc(act_hi_ready, 1)

                tap_in(0)
                tap_in(1)
                silu(0)
                tap_in(2)
                hi(0)
                tap_in(3)
                silu(1)
                hi(1)

            def stage_hi(k, j):
                act.wait_ge(act_hi_ready, k + 1)
                A(permuted(at_hi[:, j]), natural(blocks(act_hi, k)), ACT.Copy).then_inc(staged_hi, 1)

            up_round(0)
            stage_hi(0, 0)
            stage_hi(1, 1)
            with act.Fori(1, FF_PAIRS // 2) as i:
                up_round(i)

            A(small[:, 31:32], eps[:, 0:1], ACT.Sqrt)
            with act.Fori(1, FF_PAIRS // 2) as i:
                for j in range(2):
                    act.wait_ge(units_done, 1 + U_DOWN + 2 * i + j - 1)
                    stage_hi(2 * i + j, j)

            def loads():
                act.dma_start(wfb[:], arrays["w_fourier"]).then_inc(wf_in, 16)
                act.dma_start(dhd[:], arrays["dft_head"]).then_inc(wf_in, 16)
                act.dma_start(x2_dram, xr[:]).then_inc(x2_stored, 16)
                act.dma_start(dft[:], arrays["dft"]).then_inc(att_in, 16)
                act.dma_start(bias[:], arrays["dist"]).then_inc(att_in, 16)

            norm(n2, U_DOWN + FF_PAIRS - 1, loads, lambda b: col("nw2", b), lambda b: {})

            def take_head_transforms():
                act.wait_ge(wf_sums, 1)
                for m in range(2):
                    A(wf[:, 2 * m:2 * m + 2], ps[:, 2 + m].rearrange("p (b w) -> p b w", b=2),
                      ACT.Copy).then_inc(wf_ready, 1)

            def take(p, j):
                act.wait_ge(units_done, 1 + U_ATT + N_ATT * p + j + 1)
                bank = ps[:, (R_ATT + j) % 2]
                first = is_first(p)
                if j < 6:
                    if not (first and j == 0):
                        act.wait_ge(qk_total, 6 * p + j)
                    if j == 0 and not first:
                        act.wait_ge(qk_moved, p)
                    A(qk_next[:, j], bank, ACT.Copy)
                    A(qsq[:], bank, ACT.Square)
                    A(qsq_hi[:], bank, ACT.Square).then_inc(evacuated, 1)
                elif j < 9:
                    if not (first and j == 6):
                        act.wait_ge(v_turned, 3 * p + j - 6)
                    A(vT[:], bank, ACT.Copy).then_inc(evacuated, 1)
                elif j == 9:
                    if not first:
                        act.wait_ge(fv_done, 2 * p)
                    A(ufT[:], bank, ACT.Copy).then_inc(evacuated, 1)
                elif j == 10:
                    if not first:
                        act.wait_ge(yf_steps, 2 * p - 1)
                    A(sgf[:], bank, ACT.Silu).then_inc(evacuated, 1)
                else:
                    if not first:
                        act.wait_ge(gate_moved, p)
                    A(sga_next[:], bank, ACT.Silu).then_inc(evacuated, 1)
                if 1 <= j <= 6:
                    m = j - 1
                    act.wait_ge(qk_total, 6 * p + m + 1)
                    if not (first and m < 3):
                        act.wait_ge(qk_steps, 12 * p + 2 * (m - 3) + 2)
                    A(qrt[:, m % 3], ps[:, 7], ACT.Sqrt, bias=eps[:, 1:2] if m < 3 else eps[:, 0:1],
                      scale=1.0 if m < 3 else 1.0 / HP).then_inc(qk_root, 1)
                if 7 <= j <= 9:
                    c = j - 7
                    act.wait_ge(v_turned, 3 * p + c + 1)
                    if c == 0 and not first:
                        act.wait_ge(v_moved, p)
                    A(vN_next[:, c], ps[:, 7].rearrange("p (t w) -> p t w", t=NT), ACT.Copy).then_inc(v_ready, 1)
                if j >= 10:
                    m = j - 10
                    act.wait_ge(fv_done, 2 * p + m + 1)
                    if m == 0 and not first:
                        act.wait_ge(ft_done, p)
                    A(fv[:, 2 * m:2 * m + 2], ps[:, 7].rearrange("p (t w) -> p t w", t=2),
                      ACT.Copy).then_inc(fv_ready, 1)

            def move_v(p):
                act.wait_ge(v_ready, 3 * p + 3)
                if not is_first(p):
                    act.wait_ge(attended, 1 + 8 * p)
                A(vN[:], vN_next[:], ACT.Copy).then_inc(v_moved, 1)

            def exp(a, n):
                act.wait_ge(biased, 1 + 8 * a + n + 1)
                A(pr[:], pr[:], ACT.Exp, bias=stat[:, 0:1], scale=-1.0,
                  accum_out=stat[:, 1:2]).then_inc(exped, 1)

            def pt_out(a, n):
                act.wait_ge(p_turned, 1 + 8 * a + n + 1)
                act.wait_ge(attended, 1 + 8 * a + n)
                A(pt[:], ps[:, 4:6].rearrange("p b w -> p (b w)")[:, 0:6 * P], ACT.Copy).then_inc(pt_ready, 1)
                A(bias[:, n % 4], bias[:, n % 4], ACT.Copy, scale=0.5).then_inc(bias_scaled, 1)

            def hi_fourier(a):
                act.wait_ge(yf_steps, 2 * a + 1)
                A(blocks(yo_hi, a), yf[:], ACT.Copy).then_inc(yf_hi_ready, 1)

            def hi_attention(a):
                act.wait_ge(ya_steps, 1 + 2 * a + 1)
                A(blocks(yo_hi, 4 + a), ya[:], ACT.Copy).then_inc(ya_hi_ready, 1)

            act.wait_ge(n2["lo"], DB)
            A(head_r[:], head_ones, ACT.Copy).then_inc(head_ready, 1)
            for j in range(N_ATT):
                take(0, j)
                if j == 4:
                    take_head_transforms()
            act.wait_ge(x2_stored, 16)
            move_v(0)
            act.wait_ge(att_in, 16 * 2)
            with act.Fori(0, 3) as a:
                for n in range(8):
                    exp(a, n)
                    take(a + 1, 3 * n // 2)
                    pt_out(a, n)
                    if n == 0:
                        hi_fourier(a)
                    if n % 2:
                        take(a + 1, (3 * n + 1) // 2)
                hi_attention(a)
                move_v(a + 1)

            act.wait_ge(units_done, 1 + U_OUT)
            for hv in range(2):
                cols = slice(hv * S, (hv + 1) * S)
                act.dma_start(x_res[:, :, cols], x2_dram[:, :, cols]).then_inc(x_res_in[hv], 16)
            for n in range(8):
                exp(3, n)
                pt_out(3, n)
                if n == 0:
                    hi_fourier(3)
                act.wait_ge(units_done, 1 + U_OUT + n + 1)
                if n >= 2:
                    act.wait_ge(out_turned, n - 1)
                A((ufT, sgf)[n % 2][:], ps[:, (R_ATT + n) % 2], ACT.Copy).then_inc(evacuated, 1)
            hi_attention(3)
            out = arrays["out"].rearrange("(i r) d -> i r d", r=NT)
            for hv in range(2):
                for t in range(NT):
                    cols = slice(hv * S, (hv + 1) * S)
                    act.wait_ge(out_steps, 4 * hv + t + 1)
                    act.dma_start(out[:, t, cols], x_res[:, t, cols]).then_inc(out_stored, 16)
            act.wait_ge(out_stored, 16 * 8)

        @block.vector
        def _(dve):
            V = nc.vector
            TT, STT, TS = V.tensor_tensor, V.scalar_tensor_tensor, V.tensor_scalar

            V.memset(ones[:], 1.0).then_inc(setup, 1)
            V.memset(eps[:, 0:1], EPS).then_inc(setup, 1)
            V.memset(eps[:, 1:2], HP * EPS).then_inc(setup, 1)
            V.memset(ev[:, :, 0:3], 0.0).then_inc(setup, 1)
            V.memset(scp[:, 0:2], 0.0).then_inc(setup, 1)

            def ada_start(m):
                for k in range(8):
                    n = 8 * m + k
                    dve.wait_ge(ada0_in[k], 16 * (m + 1))
                    if k == 0:
                        TS(acc0[:, m], ada0[:, k], small[:, k:k + 1], None, ALU.mult).then_inc(ada0_steps, 1)
                    else:
                        dve.wait_ge(ada0_steps, n)
                        STT(acc0[:, m], ada0[:, k], small[:, k:k + 1], acc0[:, m], ALU.mult,
                            ALU.add).then_inc(ada0_steps, 1)

            dve.wait_ge(cact_ready, 1)
            ada_start(0)
            dve.wait_ge(row_stats, 5)
            V.reciprocal(small[:, 16:20], small[:, 12:16]).then_inc(setup, 1)
            dve.wait_ge(setup, 6)
            for t in range(NT):
                TS(x_tok[:, t], x_tok[:, t], small[:, 16 + t:17 + t], None, ALU.mult).then_inc(row_scaled, 1)
            ada_start(1)
            dve.wait_ge(mod0_sums, 2)
            TT(mod[:, 0:16], ps[:, 2, 0:16], col("ada_b", 0, 16), ALU.add).then_inc(mod0_ready, 1)
            dve.wait_ge(mod0_ready, 1)
            STT(coef[:, 0], mod[:, 8:16], 1.0, col("g_pre", 0, DB), ALU.add, ALU.mult).then_inc(mod0_ready, 1)
            dve.wait_ge(mod0_ready, 2)
            dve.wait_ge(xn_ready, DB)
            for b in range(DB + 1):
                if b < DB:
                    if b >= 2:
                        dve.wait_ge(h_lo_ready, b - 1)
                    TS(hf[:, b % 2], xn[:, b], coef[:, 0, b:b + 1], mod[:, b:b + 1], ALU.mult,
                       ALU.add).then_inc(hf_ready, 1)
                if b:
                    dve.wait_ge(hf_ready, b)
                    dve.wait_ge(h_hi_ready, b)
                    TT(h_lo[:, b - 1], hf[:, (b - 1) % 2], h_hi[:, b - 1].bitcast(F32),
                       ALU.subtract).then_inc(h_lo_ready, 1)

            n_dt = [0]

            def dt_step(ins):
                ins.then_inc(dt_steps, 1)
                n_dt[0] += 1
                dve.wait_ge(dt_steps, n_dt[0])

            e, z, dt = dtw[:, 1], dtw[:, 4], dtN[:].rearrange("p c h -> p (c h)")
            dve.wait_ge(dt_act, 2)
            dt_step(TS(dtw[:, 2], ps[:, 5, 0:P], 0.0, None, ALU.max))
            dve.wait_ge(dt_act, 3)
            dt_step(TS(dtw[:, 3], e, 2.0, None, ALU.add))
            dt_step(V.reciprocal(dtw[:, 4], dtw[:, 3]))
            dt_step(TT(dtw[:, 3], e, dtw[:, 4], ALU.mult))
            dt_step(TT(z, dtw[:, 3], dtw[:, 3], ALU.mult))
            dt_step(TS(dtw[:, 5], z, 1.0 / 15, None, ALU.mult))
            for k in (13, 11, 9, 7, 5, 3):
                dt_step(STT(dtw[:, 5], dtw[:, 5], 1.0 / k, z, ALU.add, ALU.mult))
            dt_step(STT(dtw[:, 6], dtw[:, 5], 1.0, dtw[:, 3], ALU.add, ALU.mult))
            dt_step(STT(dt, dtw[:, 6], 2.0, dtw[:, 2], ALU.mult, ALU.add))
            dt_step(STT(dtw[:, 0].rearrange("p (c h) -> p c h", c=NT), dtN[:], -1.0,
                        dtw[:, 7, 0:SSD_HEADS].unsqueeze(1).broadcast_to([P, NT, SSD_HEADS]), ALU.mult, ALU.mult))
            dve.wait_ge(dt_turned, 2)
            V.tensor_copy(acsN[:].rearrange("p c h -> p (c h)"), ps[:, 5, P:2 * P]).then_inc(dt_tokens, 1)
            dve.wait_ge(dt_tokens, 1)
            dve.wait_ge(acc_cleared, 1)

            with dve.Fori(0, GROUPS) as g:
                def ada_piece(n):
                    k, hv = n // 2, n % 2
                    dve.wait_ge(ada_in[hv], 128 * g + 16 * k + 16)
                    part, w = ada_acc[:, hv * S:(hv + 1) * S], small[:, k:k + 1]
                    if k == 0:
                        dve.wait_ge(mod_sums, 1 + g)
                        TS(part, ada_raw[:, hv], w, None, ALU.mult).then_inc(ada_steps, 1)
                    else:
                        dve.wait_ge(ada_steps, 1 + 16 * g + n - 1)
                        STT(part, ada_raw[:, hv], w, part, ALU.mult, ALU.add).then_inc(ada_steps, 1)

                def conv(j):
                    dve.wait_ge(evacuated, E_GRP + 16 * g + j + 1)
                    for k in range(3):
                        if k:
                            dve.wait_ge(conv_taps, 18 * g + 3 * j + k)
                        STT(cv[:, j % 2], ev[:, j % 4, k:k + S], col("conv", (6 * g + j) * 5 + k),
                            cv[:, j % 2], ALU.mult, ALU.add).then_inc(conv_taps, 1)
                        if k < 2 and j < 5:
                            ada_piece(2 * j + k)

                def chunk(c):
                    base = 24 * g + 6 * c
                    dve.wait_ge(chunk_inputs, 4 * g + c + 1)
                    dve.wait_ge(y_done, 1 + 4 * g + max(c - 1, 0))
                    TT(scm[:, c % 2], ps[:, 5, 0:P], causal, ALU.mult).then_inc(chunk_steps, 1)
                    V.tensor_copy(bn[:, c % 2], ps[:, 5, P:2 * P]).then_inc(chunk_steps, 1)
                    TT(by_head(xdt[:, c % 2]), by_head(ps[:, 4]), per_token(dtN, c, g),
                       ALU.mult).then_inc(chunk_steps, 1)
                    dve.wait_ge(decays, 1 + 4 * g + c + 1)
                    dve.wait_ge(chunk_steps, 1 + base + 3)
                    TT(by_head(xst[:, c % 2]), by_head(xdt[:, c % 2]),
                       dec[:, c % 2, :, P - 1:P].broadcast_to([P, HEADS_G, HP]), ALU.mult).then_inc(chunk_steps, 1)
                    dve.wait_ge(chunk_steps, 1 + base + 4)
                    TT(dec[:, c % 2], dec[:, c % 2], scm[:, c % 2].unsqueeze(1).broadcast_to([P, HEADS_G, P]),
                       ALU.mult).then_inc(chunk_steps, 1)
                    TT(ect[:, c % 2], ect[:, c % 2],
                       CT[:, c * P:(c + 1) * P].unsqueeze(1).broadcast_to([P, HEADS_G, P]),
                       ALU.mult).then_inc(chunk_steps, 1)

                def state(c):
                    dve.wait_ge(s_done, 3 * g + c + 1)
                    if c == 0:
                        V.tensor_copy(hst[:, 1], ps[:, 7]).then_inc(state_steps, 1)
                        return
                    new, old = (c + 1) % 2, c % 2
                    if c == 2:
                        dve.wait_ge(y_done, 1 + 4 * g + 2)
                    dve.wait_ge(state_steps, 1 + 5 * g + (1, 3)[c - 1])
                    TT(by_head(hst[:, new]), by_head(hst[:, old]),
                       eld[:, c].unsqueeze(2).broadcast_to([P, HEADS_G, HP]), ALU.mult).then_inc(state_steps, 1)
                    dve.wait_ge(state_steps, 1 + 5 * g + (2, 4)[c - 1])
                    TT(hst[:, new], hst[:, new], ps[:, 7], ALU.add).then_inc(state_steps, 1)

                def add_y(c):
                    dve.wait_ge(y_done, 1 + 4 * g + c + 1)
                    dve.wait_ge(skip_ready, 4 * g + 4)
                    y = yg[:, :, c * P:(c + 1) * P]
                    TT(y, y, ps[:, 6 - 4 * (c % 2)].rearrange("p (b l) -> p b l", b=4), ALU.add).then_inc(gate_steps, 1)

                def short_conv(q):
                    e = 3 * q
                    dve.wait_ge(evacuated, E_GRP + 16 * g + 10 + e + 2)
                    TT(scp[:, 2:2 + S], ev[:, (6 + e) % 4, 3:3 + S], ev[:, (7 + e) % 4, 3:3 + S],
                       ALU.mult).then_inc(sc_steps, 1)
                    y = zs[:, q]
                    for k in (2, 1, 0):
                        dve.wait_ge(sc_steps, 1 + 10 * g + 5 * q + 3 - k)
                        w, u = col("sc_w", (2 * g + q) * 3 + k), scp[:, k:k + S]
                        if k == 2:
                            TS(y, u, w, None, ALU.mult).then_inc(sc_steps, 1)
                        else:
                            STT(y, u, w, y, ALU.mult, ALU.add).then_inc(sc_steps, 1)
                    dve.wait_ge(sc_steps, 1 + 10 * g + 5 * q + 4)
                    dve.wait_ge(evacuated, E_GRP + 16 * g + 10 + e + 3)
                    TT(blocks(ysc, 2 * g + q), y, ev[:, (8 + e) % 4, 3:3 + S], ALU.mult).then_inc(sc_steps, 1)

                for j in range(6):
                    conv(j)
                chunk(0)
                ada_piece(10)
                chunk(1)
                ada_piece(11)
                state(0)
                chunk(2)
                add_y(0)
                state(1)
                ada_piece(12)
                ada_piece(13)
                chunk(3)
                ada_piece(14)
                ada_piece(15)
                add_y(1)
                state(2)
                add_y(2)
                add_y(3)
                dve.wait_ge(gate_steps, 1 + 15 * g + 4)
                TT(yg[:], yg[:], zs[:], ALU.mult).then_inc(gate_steps, 1)
                dve.wait_ge(gate_steps, 1 + 15 * g + 5)
                short_conv(0)
                dve.wait_ge(y_squared, g + 1)
                V.tensor_reduce(sct[:], xcT[:].rearrange("p b t -> p t b"), AX.X, ALU.add).then_inc(gate_steps, 1)
                dve.wait_ge(mod_sums, 1 + g + 1)
                TT(mod[:, bass.ds(16 + 8 * g, 8)], ps[:, 7, 0:8], col("ada_b", 16 + 8 * g, 8),
                   ALU.add).then_inc(mod_ready, 1)
                dve.wait_ge(group_root, 1 + g + 1)
                V.reciprocal(sct[:], sct[:]).then_inc(gate_steps, 1)
                dve.wait_ge(gate_steps, 1 + 15 * g + 7)
                for b in range(4):
                    STT(yg[:, b], yg[:, b], col("ssd_g", 4 * g + b), sct[:], ALU.mult,
                        ALU.mult).then_inc(gate_steps, 1)
                for b in range(4):
                    dve.wait_ge(y_hi_ready, 4 * g + b + 1)
                    TT(y_lo[:, b], yg[:, b], y_hi[:, b].bitcast(F32), ALU.subtract).then_inc(gate_steps, 1)
                short_conv(1)
                for n in range(DB):
                    if n % 2 == 0:
                        dve.wait_ge(half_done, 4 * g + n // 2 + 1)
                    else:
                        dve.wait_ge(units_done, 1 + U_GRP + N_GRP * g + 16 + n // 2 + 1)
                    TT(ssd_acc[:, n], ssd_acc[:, n], ps[:, (R_GRP + 16 + n) % 2], ALU.add).then_inc(acc_steps[n % 2], 1)

            dve.wait_ge(mod_ready, 1 + 4)
            TT(coef[:, 1], mod[:, 16:24], col("g_post", 0, DB), ALU.mult).then_inc(coef_ready, 1)
            STT(coef[:, 2], mod[:, 32:40], 1.0, col("f_pre", 0, DB), ALU.add, ALU.mult).then_inc(coef_ready, 1)
            TT(coef[:, 3], mod[:, 40:48], col("f_post", 0, DB), ALU.mult).then_inc(coef_ready, 1)
            dve.wait_ge(coef_ready, 3)
            for parity in acc_steps:
                dve.wait_ge(parity, 1 + 4 * GROUPS)
            for m in range(2):
                TT(dgc[:, m].rearrange("p (b c) -> p b c", b=DB), ident.unsqueeze(1).broadcast_to([P, DB, P]),
                   coef[:, 2 * m + 1].unsqueeze(2).broadcast_to([P, DB, P]), ALU.mult).then_inc(gg_diag, 1)
            for q in range(2):
                dve.wait_ge(sc_hi_ready, q + 1)
                TT(sc_lo[:, 4 * q:4 * q + 4], ysc[:, 4 * q:4 * q + 4], sc_hi[:, 4 * q:4 * q + 4].bitcast(F32),
                   ALU.subtract).then_inc(sc_lo_ready, 1)
            with dve.Fori(0, 2) as i:
                for j in range(4):
                    at_ = 16 * i + 4 * j
                    dve.wait_ge(evacuated, E_MIX + 12 * i + 3 * j + 3)
                    TT(gts[:, j % 2, 2], gts[:, j % 2, 2], gts[:, j % 2, 1], ALU.mult).then_inc(mix_steps, 1)
                    TT(gts[:, j % 2, 0], gts[:, j % 2, 0], blocks(ssd_acc, 4 * i + j), ALU.mult).then_inc(mix_steps, 1)
                    dve.wait_ge(mix_steps, 1 + at_ + 2)
                    TT(mixf[:, j % 2], gts[:, j % 2, 0], gts[:, j % 2, 2], ALU.add).then_inc(mix_steps, 1)
                    dve.wait_ge(mix_hi_ready, 4 * i + j + 1)
                    TT(permuted(blocks(mix_lo, 4 * i + j)), natural(mixf[:, j % 2]),
                       permuted(blocks(mix_hi, 4 * i + j)).bitcast(F32), ALU.subtract).then_inc(mix_steps, 1)

            def norm(n, m, scale, shift):
                def inverse(k, first, r):
                    dve.wait_ge(n["root"], k + 1)
                    V.reciprocal(small[:, first + r:first + 1 + r],
                                 small[:, first - 4 + r:first - 3 + r]).then_inc(n["inverse"], 1)

                def rows(r):
                    dve.wait_ge(n["inverse"], NORM_B[r] + 1)
                    TS(br[:, r], xr[:, r], small[:, 28 + r:29 + r], None, ALU.mult).then_inc(n["rows"], 1)

                for r in range(NT):
                    inverse(NORM_A[r], 16, r)
                    dve.wait_ge(n["inverse"], NORM_A[r] + 1)
                    STT(halves(br[:, r]), banks_of(r), small[:, 16 + r:17 + r], halves(gg[:, m]), ALU.mult,
                        ALU.mult).then_inc(n["scaled"], 1)
                    if r >= 2:
                        inverse(NORM_B[r - 2], 28, r - 2)
                    dve.wait_ge(n["scaled"], r + 1)
                    TT(xr[:, r], xr[:, r], br[:, r], ALU.add).then_inc(n["added"], 1)
                inverse(NORM_B[2], 28, 2)
                rows(1)
                rows(2)
                inverse(NORM_B[3], 28, 3)
                rows(3)

                def full(b):
                    dve.wait_ge(n["turned"], b + 1)
                    if b >= 4:
                        dve.wait_ge(n["lo"], b - 3)
                    TS(hn[:, b % 4], ps[:, b], scale(b), shift(b), ALU.mult,
                       *((ALU.add,) if shift(b) is not None else ())).then_inc(n["full_dve"], 1)

                def lo(b):
                    dve.wait_ge(n["hi"], b + 1)
                    TT(h_lo[:, b], hn[:, b % 4], h_hi[:, b].bitcast(F32), ALU.subtract).then_inc(n["lo"], 1)

                full(1)
                lo(0)
                for b in range(3, DB, 2):
                    full(b)
                    lo(b - 2)
                    lo(b - 1)
                lo(DB - 1)

            dve.wait_ge(x2_in, 16)
            dve.wait_ge(gg_ready, 2)
            norm(n1, 0, lambda b: coef[:, 2, b:b + 1], lambda b: mod[:, 24 + b:25 + b])

            for j in range(4):
                V.memset(fe[:, j, 0:2], 0.0).then_inc(ffn_taps, 2)
            V.memset(af[:, 0, 0:1], 0.0).then_inc(ffn_steps, 4)
            def up_round(i):
                for p in range(2):
                    for j in (2 * p, 2 * p + 1):
                        dve.wait_ge(evacuated, E_UP + 4 * i + j + 1)
                        for k in range(2):
                            if k:
                                dve.wait_ge(ffn_taps, 8 + 8 * i + 2 * j + 1)
                            STT(fcv[:, j], fe[:, j, k:k + S], col("ffn_w", 16 * i + 4 * j + k), fcv[:, j],
                                ALU.mult, ALU.add).then_inc(ffn_taps, 1)
                    dve.wait_ge(ffn_taps, 8 + 8 * i + 4 * p + 4)
                    dve.wait_ge(ffn_silu, 2 * i + p + 1)
                    TT(af[:, p], fcv[:, 2 * p], fcv[:, 2 * p + 1], ALU.mult).then_inc(ffn_steps, 1)
                    dve.wait_ge(act_hi_ready, 2 * i + p + 1)
                    TT(blocks(act_lo, 2 * i + p), af[:, p], blocks(act_hi, 2 * i + p).bitcast(F32),
                       ALU.subtract).then_inc(ffn_steps, 1)

            def stage_lo(k, j):
                dve.wait_ge(ffn_steps, 4 + 2 * k + 2)
                V.tensor_copy(permuted(at_lo[:, j]), natural(blocks(act_lo, k))).then_inc(staged_lo, 1)

            up_round(0)
            stage_lo(0, 0)
            stage_lo(1, 1)
            with dve.Fori(1, FF_PAIRS // 2) as i:
                up_round(i)

            with dve.Fori(1, FF_PAIRS // 2) as i:
                for j in range(2):
                    dve.wait_ge(units_done, 1 + U_DOWN + 2 * i + j - 1)
                    stage_lo(2 * i + j, j)
            norm(n2, 1, lambda b: col("nw2", b), lambda b: None)

            def scale_qk(p, j):
                dve.wait_ge(qk_root, 6 * p + j + 1)
                V.reciprocal(qrt[:, j % 3], qrt[:, j % 3]).then_inc(qk_steps, 1)
                dve.wait_ge(qk_steps, 12 * p + 2 * j + 1)
                STT(qk_next[:, j], qk_next[:, j], col("qk_w", 6 * p + j), qrt[:, j % 3], ALU.mult,
                    ALU.mult).then_inc(qk_steps, 1)

            def split_squares(p, j):
                dve.wait_ge(evacuated, E_ATT + N_ATT * p + j + 1)
                if not (is_first(p) and j == 0):
                    dve.wait_ge(qk_total, 6 * p + j)
                TT(qsq_lo[:], qsq[:], qsq_hi[:].bitcast(F32), ALU.subtract).then_inc(qsq_split, 1)

            def move_qk(p):
                dve.wait_ge(qk_steps, 12 * p + 12)
                if not is_first(p):
                    dve.wait_ge(scored, 8 * p)
                V.tensor_copy(qk[:], qk_next[:]).then_inc(qk_moved, 1)

            def move_gate(p):
                dve.wait_ge(evacuated, E_ATT + N_ATT * p + 12)
                V.tensor_copy(sga[:], sga_next[:]).then_inc(gate_moved, 1)

            def split_y(source, gate, y, steps, hi_ready, pair, at_block):
                TT(y[:], source, gate, ALU.mult).then_inc(steps, 1)
                dve.wait_ge(hi_ready, pair + 1)
                TT(blocks(yo_lo, at_block), y[:], blocks(yo_hi, at_block).bitcast(F32),
                   ALU.subtract).then_inc(steps, 1)

            def fourier(a):
                dve.wait_ge(ft_done, a + 1)
                dve.wait_ge(evacuated, E_ATT + N_ATT * a + 11)
                split_y(ps[:, 7], sgf[:], yf, yf_steps, yf_hi_ready, a, a)

            def attention(a):
                dve.wait_ge(attended, 1 + 8 * a + 8)
                dve.wait_ge(gate_moved, a + 1)
                split_y(ps[:, 6], sga[:], ya, ya_steps, ya_hi_ready, a, 4 + a)

            def add_bias(a, n):
                dve.wait_ge(scored, 8 * a + n + 1)
                dve.wait_ge(bias_scaled, 8 * a + n + 1)
                dve.wait_ge(p_turned, 1 + 8 * a + n)
                V.memset(stat[:, 3:4], 0.0)
                V.tensor_tensor_reduce(
                    pr[:], ps[:, 2:4].rearrange("p b w -> p (b w)")[:, 0:6 * P], bias[:, n % 4],
                    -1.0, 3e38, ALU.add, ALU.min, stat[:, 0:1]).then_inc(biased, 1)

            def normalise(a, n):
                dve.wait_ge(exped, 8 * a + n + 1)
                V.reciprocal(stat[:, 2:3], stat[:, 1:2]).then_inc(normed, 1)
                dve.wait_ge(normed, 16 * a + 2 * n + 1)
                TS(pr[:], pr[:], stat[:, 2:3], None, ALU.mult).then_inc(normed, 1)

            for j in range(6):
                split_squares(0, j)
                if j:
                    scale_qk(0, j - 1)
            scale_qk(0, 5)
            move_qk(0)
            move_gate(0)
            dve.wait_ge(att_in, 16 * 2)
            with dve.Fori(0, 3) as a:
                for n in range(8):
                    add_bias(a, n)
                    normalise(a, n)
                    if n == 0:
                        fourier(a)
                        split_squares(a + 1, 0)
                    elif n < 7:
                        if n in (1, 3):
                            split_squares(a + 1, (3 * n - 1) // 2)
                        scale_qk(a + 1, n - 1)
                        if n <= 3:
                            split_squares(a + 1, (3 * n + 1) // 2)
                move_qk(a + 1)
                attention(a)
                move_gate(a + 1)

            def add_block(n):
                dve.wait_ge(out_turned, n + 1)
                dve.wait_ge(x_res_in[n // 4], 16)
                x = x_res[:, :, n * P:(n + 1) * P]
                TT(x, x, ps[:, 7].rearrange("p (r c) -> p r c", r=NT), ALU.add).then_inc(out_added, 1)

            for n in range(8):
                add_bias(3, n)
                normalise(3, n)
                if n == 0:
                    fourier(3)
                else:
                    add_block(n - 1)
            attention(3)
            add_block(7)
            dve.wait_ge(out_added, DB)
            for m in range(8):
                hv, t = m // 4, m % 4
                dve.wait_ge(out_sums, m + 1)
                x = x_res[:, t, hv * S:(hv + 1) * S]
                TT(x, x, ps[:, m], ALU.add).then_inc(out_steps, 1)


def lay_out(i):
    f = {k: np.ascontiguousarray(np.asarray(v, np.float32)) for k, v in i.items()}

    def blocks_of(w):
        k, n = w.shape
        return w.reshape(k // P, P, n // P, P).transpose(2, 1, 0, 3)

    def column(v):
        return v.reshape(-1, P).T

    zero = np.zeros
    w_in = f["w_in"][0]
    cut = np.cumsum([2048, 3072, SSD_HEADS, D, D, D])
    z, xbc, dt, scb, scc, sch, gates = (w_in[:, x:y] for x, y in zip([0, *cut], [*cut, w_in.shape[1]]))
    z, xbc, scb, scc, sch, gates = map(blocks_of, (z, xbc, scb, scc, sch, gates))
    units = []
    units.append(blocks_of(np.concatenate([dt, zero((D, P - SSD_HEADS), np.float32)], 1))[0])
    w_ssd = blocks_of(f["w_ssd_out"][0])
    for g in range(GROUPS):
        units += [xbc[16 + g], xbc[20 + g]] + [xbc[4 * g + b] for b in range(4)] + [z[4 * g + b] for b in range(4)]
        for q in range(2):
            units += [scc[2 * g + q], sch[2 * g + q], scb[2 * g + q]]
        for n in range(0, DB, 2):
            units.append(np.concatenate([w_ssd[n][:, 4 * g:4 * g + 4], w_ssd[n + 1][:, 4 * g:4 * g + 4]], 1))
    w_sc = blocks_of(f["w_sc_out"][0])
    for j in range(DB):
        units += [gates[j], gates[DB + j], w_sc[j]]
    units += list(f["w_o"][0].reshape(DB, P, D))
    up = blocks_of(f["w_up"][0])
    for p in range(FF_PAIRS):
        units += [up[p], up[FF_PAIRS + p]]
    units += list(f["w_down"][0].reshape(FF_PAIRS, P, D))
    w2 = f["w_in_2"]
    qkv = CFG * S
    uf, gf = blocks_of(w2[:, :S]), blocks_of(w2[:, S:2 * S])
    q, k, v = (blocks_of(w2[:, 2 * S + n * qkv:2 * S + (n + 1) * qkv]) for n in range(3))
    ga = blocks_of(w2[:, 2 * S + 3 * qkv:])
    for i2 in range(4):
        for m in (q, k, v):
            units += [m[4 * c + i2] for c in range(CFG)]
        units += [uf[i2], gf[i2], ga[i2]]
    out2 = blocks_of(f["w_out_2"])
    for n in range(DB):
        units.append(np.concatenate([out2[n][:, OUT_TILES], zero((P, 1, P), np.float32)], 1))
    units.append(out2[:, :, 7].transpose(1, 0, 2))
    stream = np.stack([u.reshape(P, UW) for u in units])
    assert len(units) == UNITS

    t = {}
    t["ident"] = np.eye(P, dtype=np.float32)
    t["causal"] = np.triu(np.ones((P, P), np.float32))
    t["head_ones"] = np.kron(np.eye(2, dtype=np.float32), np.ones((HP, HP), np.float32))
    t["c"] = column(f["c"][0])
    t["ada_b"] = column(f["ada_b"][0])
    t["g_pre"], t["g_post"] = column(f["mix_pre_g"][0]), column(f["mix_post_g"][0])
    t["f_pre"], t["f_post"] = column(f["ffn_pre_g"][0]), column(f["ffn_post_g"][0])
    t["nw2"] = column(f["norm_w_2"])
    cw = np.concatenate([f["ssd_conv_w"][0], f["ssd_conv_b"]], 0).reshape(5, 24, P)
    order = [b for g in range(GROUPS) for b in (16 + g, 20 + g, 4 * g, 4 * g + 1, 4 * g + 2, 4 * g + 3)]
    t["conv"] = cw[:, order].transpose(2, 1, 0).reshape(P, 120)
    t["d_skip"] = column(np.repeat(f["ssd_d"][0], HP))
    t["ssd_g"] = column(f["ssd_norm_g"][0])
    t["sc_w"] = f["sc_conv_w"][0].reshape(3, DB, P).transpose(2, 1, 0).reshape(P, 3 * DB)
    fw = np.concatenate([f["ffn_conv_w"][0], f["ffn_conv_b"]], 0).reshape(4, 2, FF_PAIRS, P)
    t["ffn_w"] = fw.transpose(3, 2, 1, 0).reshape(P, 8 * FF_PAIRS)
    qk = [f[n].reshape(CFG, 4, P) for n in ("q_norm_w_2", "k_norm_w_2")]
    t["qk_w"] = np.stack(qk).transpose(3, 2, 0, 1).reshape(P, 24)
    t["dt_bias"] = np.concatenate([f["ssd_dt_bias"][0], zero(P - SSD_HEADS, np.float32)])[:, None]
    t["a_log"] = np.repeat(f["ssd_a_log"], P, 0)
    table = np.concatenate([t[n] for n, _ in _widths], 1)
    assert table.shape == (P, NCOL)

    tok = np.arange(S).reshape(P, NT).T.reshape(-1)
    angle = 2 * np.pi * (np.outer(tok, tok) % S) / S
    dft = np.stack([np.cos(angle), np.sin(angle)]).reshape(2, NT, P, S).transpose(2, 0, 1, 3)
    ch = 2 * np.pi * (np.outer(np.arange(HP), np.arange(HP)) % HP) / HP
    scale = 1 / np.sqrt(S * HP)
    dft_head = np.stack([np.kron(np.eye(2), m) for m in (np.cos(ch) * scale, -np.sin(ch) * scale)], 1)
    i1 = np.arange(P)
    dist = np.full((P, NT, 6 * P), MASKED)
    near = np.abs(i1[:, None] - i1[None])
    for r in range(NT):
        far = np.abs((4 * i1 + r)[:, None] - tok[None])
        dist[:, r, :S] = np.where(far <= 64, -far, MASKED)
        dist[:, r, S:S + P] = np.where(near <= 64, -4.0 * near, MASKED)
        dist[:, r, S + P:] = np.where(near % 4 == 0, -4.0 * near, MASKED)
    wfo = zero((P, 4, P), np.float32)
    wfo[:HP, :, :HP] = f["w_fourier_2"][0::2].transpose(1, 0, 2)
    wfo[HP:, :, HP:] = f["w_fourier_2"][1::2].transpose(1, 0, 2)
    dist *= 0.5
    return {
        "stream": stream,
        "ada": f["ada_w"][0].reshape(8, P, 6, D).transpose(2, 0, 1, 3).reshape(48, P, D),
        "table": table,
        "x": f["x"][0].reshape(NT, P, D).transpose(1, 0, 2),
        "x_classes": f["x"][0].reshape(P, NT, D),
        "dft": dft.astype(np.float32),
        "dft_head": dft_head.astype(np.float32),
        "dist": dist.reshape(P, -1).astype(np.float32),
        "w_fourier": wfo,
    }


def kernel(**inputs):
    import concourse.bacc as bacc
    from concourse.bass_utils import run_bass_kernel_spmd

    arrays = {k: np.ascontiguousarray(v) for k, v in lay_out(inputs).items()}
    nc = bacc.Bacc("TRN2", target_bir_lowering=False, num_devices=1)
    a = {k: nc.dram_tensor(k, v.shape, F32, kind="ExternalInput").ap() for k, v in arrays.items()}
    a["out"] = nc.dram_tensor("out", (S, D), F32, kind="ExternalOutput").ap()
    build(nc, a)
    r = run_bass_kernel_spmd(nc, [arrays], core_ids=[0])
    return r.results[0]["out"].reshape(1, S, D)
```
